# Optimizing a Trainium2 kernel written in Bass

```python
import math
import jax, jax.numpy as jnp
from jax import lax
import numpy as np

D_MODEL = 1024
BATCH = 1
SEQ = 512
DEPTH = 2

N_MIXERS = 4
DN_ALPHA = (2.0 * DEPTH) ** 0.25
DN_BETA = (8.0 * DEPTH) ** -0.25
LN_EPS = 1e-5

GDN_HEADS = 8
GDN_DK = D_MODEL // GDN_HEADS
GDN_DV = D_MODEL // GDN_HEADS
GDN_CONV = 4
GDN_CHUNK = 64
RET_HEADS = 4
RET_DK = D_MODEL // RET_HEADS
RET_DV = 2 * D_MODEL // RET_HEADS
RET_CHUNK = 128
RET_ROPE_BASE = 10000.0
GMLP_CHUNK = 128
GMLP_WIDTH = 2 * D_MODEL
GMLP_GROUPS = 8
SB_HEADS = 16
SB_DH = D_MODEL // SB_HEADS
SB_BLOCK = 128
FFN_HIDDEN = ((8 * D_MODEL // 3 + 255) // 256) * 256
FFN_CONV = 3


F32 = jnp.float32

def _standardize(x, eps):
    xf = x.astype(F32)
    mu = jnp.mean(xf, axis=-1, keepdims=True)
    xc = xf - mu
    var = jnp.mean(xc * xc, axis=-1, keepdims=True)
    return xc * lax.rsqrt(var + eps)

def layer_norm(x, g, b):
    return (_standardize(x, LN_EPS) * g.astype(F32) + b.astype(F32)).astype(x.dtype)

def _l2norm(x, eps=1e-6):
    return x * lax.rsqrt(jnp.sum(x * x, axis=-1, keepdims=True) + eps)

def causal_dwconv(x, w):
    k_w = w.shape[0]
    s = x.shape[1]
    xp = jnp.pad(x, ((0, 0), (k_w - 1, 0), (0, 0)))
    y = xp[:, k_w - 1:k_w - 1 + s] * w[k_w - 1]
    for j in range(k_w - 1):
        y = y + xp[:, j:j + s] * w[j]
    return y

def _chunk_heads(t, n_heads, chunk):
    b, s, hd = t.shape
    return t.astype(F32).reshape(b, s // chunk, chunk, n_heads, hd // n_heads).transpose(0, 3, 1, 2, 4)

def _unchunk_heads(t):
    b, h, n, c, d = t.shape
    return t.transpose(0, 2, 3, 1, 4).reshape(b, n * c, h, d)

def gated_deltanet(h, w_in, conv_w, a_log, dt_bias, norm_w, w_out):
    H, dk, dv, C = GDN_HEADS, GDN_DK, GDN_DV, GDN_CHUNK
    b_, s, _ = h.shape
    n_qkv = 2 * H * dk + H * dv
    proj = h @ w_in
    qkv, z, a, bt = jnp.split(proj, [n_qkv, n_qkv + H * dv, n_qkv + H * dv + H], axis=-1)
    qkv = jax.nn.silu(causal_dwconv(qkv, conv_w))
    q, k, v = jnp.split(qkv, [H * dk, 2 * H * dk], axis=-1)
    q = _l2norm(_chunk_heads(q, H, C)) * (dk ** -0.5)
    k = _l2norm(_chunk_heads(k, H, C))
    v = _chunk_heads(v, H, C)
    beta = jax.nn.sigmoid(_chunk_heads(bt, H, C)[..., 0])
    g = -jnp.exp(a_log.astype(F32))[:, None, None] * jax.nn.softplus(
        _chunk_heads(a, H, C)[..., 0] + dt_bias.astype(F32)[:, None, None])
    gc = jnp.cumsum(g, axis=-1)
    idx = jnp.arange(C)
    causal = idx[:, None] >= idx[None, :]
    strict = idx[:, None] > idx[None, :]
    diff = gc[..., :, None] - gc[..., None, :]
    decay = jnp.where(causal, jnp.exp(jnp.where(causal, diff, 0.0)), 0.0)
    kb = k * beta[..., None]
    kk = jnp.where(strict, jnp.einsum('bhncd,bhnmd->bhncm', kb, k) * decay, 0.0)
    eye = jnp.eye(C, dtype=F32)
    rhs = jnp.concatenate([v * beta[..., None], kb * jnp.exp(gc)[..., None]], axis=-1)
    sol = lax.linalg.triangular_solve(kk + eye, rhs, left_side=True, lower=True, unit_diagonal=True)
    u, w = sol[..., :dv], sol[..., dv:]
    qk = jnp.where(causal, jnp.einsum('bhncd,bhnmd->bhncm', q, k) * decay, 0.0)

    def step(state, inp):
        q_n, k_n, u_n, w_n, qk_n, g_n = inp
        v_new = u_n - jnp.einsum('bhck,bhkv->bhcv', w_n, state)
        o = (jnp.einsum('bhck,bhkv->bhcv', q_n * jnp.exp(g_n)[..., None], state)
             + jnp.einsum('bhcm,bhmv->bhcv', qk_n, v_new))
        g_last = g_n[..., -1:]
        state = (state * jnp.exp(g_last)[..., None]
                 + jnp.einsum('bhck,bhcv->bhkv', k_n * jnp.exp(g_last - g_n)[..., None], v_new))
        return state, o

    xs = tuple(jnp.moveaxis(t, 2, 0) for t in (q, k, u, w, qk, gc))
    state0 = jnp.zeros((b_, H, dk, dv), F32)
    _, o = lax.scan(step, state0, xs)
    o = _unchunk_heads(jnp.moveaxis(o, 0, 2))
    o = o * lax.rsqrt(jnp.mean(o * o, axis=-1, keepdims=True) + 1e-6) * norm_w.astype(F32)
    o = o * jax.nn.silu(z.astype(F32).reshape(b_, s, H, dv))
    return o.reshape(b_, s, H * dv).astype(h.dtype) @ w_out

def retention(h, w_in, w_out):
    H, dk, dv, C = RET_HEADS, RET_DK, RET_DV, RET_CHUNK
    b_, s, _ = h.shape
    q, k, v, gate = jnp.split(h @ w_in, [H * dk, 2 * H * dk, 2 * H * dk + H * dv], axis=-1)
    pos = jnp.arange(s, dtype=F32)
    inv_freq = RET_ROPE_BASE ** (-jnp.linspace(0.0, 1.0, dk // 2, dtype=F32))
    ang = pos[:, None] * inv_freq[None, :]
    cos_a, sin_a = jnp.cos(ang)[:, None, :], jnp.sin(ang)[:, None, :]

    def rot(t):
        t = t.astype(F32).reshape(b_, s, H, dk)
        t1, t2 = t[..., :dk // 2], t[..., dk // 2:]
        return jnp.concatenate([t1 * cos_a - t2 * sin_a, t1 * sin_a + t2 * cos_a], axis=-1).reshape(b_, s, H * dk)

    q = _chunk_heads(rot(q), H, C)
    k = _chunk_heads(rot(k), H, C) * (dk ** -0.5)
    v = _chunk_heads(v, H, C)
    log_gamma = jnp.log(1.0 - jnp.power(2.0, -5.0 - jnp.arange(H, dtype=F32)))
    idx = jnp.arange(C, dtype=F32)
    rel = idx[:, None] - idx[None, :]
    dmask = jnp.where(rel >= 0, jnp.exp(jnp.maximum(rel, 0.0) * log_gamma[:, None, None]), 0.0)
    scores = jnp.einsum('bhncd,bhnmd->bhncm', q, k) * dmask[None, :, None]
    intra = jnp.einsum('bhncm,bhnmv->bhncv', scores, v)
    zeta = jnp.exp((C - 1.0 - idx)[None, :] * log_gamma[:, None])
    xi = jnp.exp((idx + 1.0)[None, :] * log_gamma[:, None])
    gamma_c = jnp.exp(C * log_gamma)

    def step(state, inp):
        q_n, k_n, v_n = inp
        o = jnp.einsum('bhck,bhkv->bhcv', q_n, state) * xi[None, :, :, None]
        state = (state * gamma_c[None, :, None, None]
                 + jnp.einsum('bhck,bhcv->bhkv', k_n * zeta[None, :, :, None], v_n))
        return state, o

    xs = tuple(jnp.moveaxis(t, 2, 0) for t in (q, k, v))
    _, inter = lax.scan(step, jnp.zeros((b_, H, dk, dv), F32), xs)
    o = _unchunk_heads(intra + jnp.moveaxis(inter, 0, 2))
    o = _standardize(o, 1e-6).reshape(b_, s, H * dv)
    o = o * jax.nn.silu(gate.astype(F32))
    return o.astype(h.dtype) @ w_out

def chunked_gmlp(h, w_in, ln_g, ln_b, w_s, b_s, w_out):
    C, G, W = GMLP_CHUNK, GMLP_GROUPS, GMLP_WIDTH
    b_, s, _ = h.shape
    u, v = jnp.split(jax.nn.gelu(h @ w_in, approximate=False), 2, axis=-1)
    v = layer_norm(v, ln_g, ln_b).reshape(b_, s // C, C, G, W // G)
    causal = jnp.tril(jnp.ones((C, C), dtype=bool))
    ws = jnp.where(causal, w_s, 0.0).astype(v.dtype)
    vs = jnp.einsum('gts,bnsgd->bntgd', ws, v) + b_s.T.astype(v.dtype)[None, None, :, :, None]
    return (u * vs.reshape(b_, s, W)) @ w_out

def stick_breaking(h, w_in, w_out):
    H, dh, T = SB_HEADS, SB_DH, SB_BLOCK
    b_, s, _ = h.shape
    nb = s // T
    q, k, v = jnp.split(h @ w_in, 3, axis=-1)
    q, k, v = (t.reshape(b_, s, H, dh).transpose(0, 2, 1, 3) for t in (q, k, v))
    qb = q.reshape(b_, H, nb, T, dh).transpose(2, 0, 1, 3, 4)
    key_pos = jnp.arange(s)
    scale = dh ** -0.5

    def block(args):
        q_blk, blk = args
        z = jnp.einsum('bhtd,bhsd->bhts', q_blk, k).astype(F32) * scale
        q_pos = blk * T + jnp.arange(T)
        strict = key_pos[None, :] < q_pos[:, None]
        log_1mb = jnp.where(strict, jax.nn.log_sigmoid(-z), 0.0)
        after = lax.cumsum(log_1mb, axis=3, reverse=True) - log_1mb
        a = jnp.where(strict, jnp.exp(jax.nn.log_sigmoid(z) + after), 0.0)
        return jnp.einsum('bhts,bhsd->bhtd', a.astype(v.dtype), v)

    o = lax.map(block, (qb, jnp.arange(nb)))
    o = o.transpose(1, 0, 3, 2, 4).reshape(b_, s, H * dh)
    return o @ w_out

def conv_ffn(h, w_up, conv_w, conv_b, w_down):
    gate, up = jnp.split(h @ w_up, 2, axis=-1)
    gate = causal_dwconv(gate, conv_w) + conv_b
    return (jax.nn.silu(gate) * up) @ w_down

def first_inputs(seed: int = 0) -> dict:
    key = jax.random.key(seed)
    ks = jax.random.split(key, 32)
    D, F = D_MODEL, FFN_HIDDEN

    def nrm(i, shape, scale):
        return jax.random.normal(ks[i], shape, F32) * scale

    gdn_qkv = 2 * GDN_HEADS * GDN_DK + GDN_HEADS * GDN_DV
    gdn_in = gdn_qkv + GDN_HEADS * GDN_DV + 2 * GDN_HEADS
    ret_in = 2 * RET_HEADS * RET_DK + 2 * RET_HEADS * RET_DV
    a_vals = jax.random.uniform(ks[14], (GDN_HEADS,), F32, 1.0, 16.0)
    dt = jnp.exp(jax.random.uniform(ks[15], (GDN_HEADS,), F32, math.log(1e-3), math.log(1e-1)))
    return {
        'x': nrm(0, (BATCH, SEQ, D), 1.0),
        'c': nrm(1, (BATCH, D), 1.0),
        'cond_w': nrm(2, (D, D), D ** -0.5),
        'cond_b': nrm(3, (D,), 0.01),
        'ada_w': nrm(4, (DEPTH, D, 6 * D), 0.1 * D ** -0.5),
        'ada_b': nrm(5, (DEPTH, 6 * D), 0.01),
        'ln_g': 1.0 + nrm(6, (DEPTH, 2, D), 0.02),
        'ln_b': nrm(7, (DEPTH, 2, D), 0.02),
        'ffn_up': nrm(8, (DEPTH, D, 2 * F), D ** -0.5),
        'ffn_conv_w': nrm(9, (DEPTH, FFN_CONV, F), FFN_CONV ** -0.5),
        'ffn_conv_b': nrm(10, (DEPTH, F), 0.01),
        'ffn_down': nrm(11, (DEPTH, F, D), DN_BETA * F ** -0.5),
        'gdn_w_in': nrm(12, (D, gdn_in), D ** -0.5),
        'gdn_conv_w': nrm(13, (GDN_CONV, gdn_qkv), GDN_CONV ** -0.5),
        'gdn_a_log': jnp.log(a_vals),
        'gdn_dt_bias': dt + jnp.log(-jnp.expm1(-dt)),
        'gdn_norm_w': 1.0 + nrm(16, (GDN_DV,), 0.02),
        'gdn_w_out': nrm(17, (GDN_HEADS * GDN_DV, D), DN_BETA * (GDN_HEADS * GDN_DV) ** -0.5),
        'ret_w_in': nrm(18, (D, ret_in), D ** -0.5),
        'ret_w_out': nrm(19, (RET_HEADS * RET_DV, D), DN_BETA * (RET_HEADS * RET_DV) ** -0.5),
        'gmlp_w_in': nrm(20, (D, 2 * GMLP_WIDTH), D ** -0.5),
        'gmlp_ln_g': 1.0 + nrm(21, (GMLP_WIDTH,), 0.02),
        'gmlp_ln_b': nrm(22, (GMLP_WIDTH,), 0.02),
        'gmlp_w_s': nrm(23, (GMLP_GROUPS, GMLP_CHUNK, GMLP_CHUNK), GMLP_CHUNK ** -0.5),
        'gmlp_b_s': 1.0 + nrm(24, (GMLP_GROUPS, GMLP_CHUNK), 0.01),
        'gmlp_w_out': nrm(25, (GMLP_WIDTH, D), DN_BETA * GMLP_WIDTH ** -0.5),
        'sb_w_in': nrm(26, (D, 3 * D), D ** -0.5),
        'sb_w_out': nrm(27, (D, D), DN_BETA * D ** -0.5),
    }

def first_block(x, c, cond_w, cond_b, ada_w, ada_b, ln_g, ln_b, ffn_up, ffn_conv_w, ffn_conv_b, ffn_down,
              gdn_w_in, gdn_conv_w, gdn_a_log, gdn_dt_bias, gdn_norm_w, gdn_w_out,
              ret_w_in, ret_w_out,
              gmlp_w_in, gmlp_ln_g, gmlp_ln_b, gmlp_w_s, gmlp_b_s, gmlp_w_out,
              sb_w_in, sb_w_out):
    mixers = (
        lambda t: gated_deltanet(t, gdn_w_in, gdn_conv_w, gdn_a_log, gdn_dt_bias, gdn_norm_w, gdn_w_out),
        lambda t: retention(t, ret_w_in, ret_w_out),
        lambda t: chunked_gmlp(t, gmlp_w_in, gmlp_ln_g, gmlp_ln_b, gmlp_w_s, gmlp_b_s, gmlp_w_out),
        lambda t: stick_breaking(t, sb_w_in, sb_w_out),
    )
    e = jax.nn.silu(c @ cond_w + cond_b)
    for i in range(DEPTH):
        mod = (e @ ada_w[i] + ada_b[i])[:, None, :]
        sh1, sc1, g1, sh2, sc2, g2 = jnp.split(mod, 6, axis=-1)
        y = mixers[i % N_MIXERS](x * (1.0 + sc1) + sh1)
        x = layer_norm(DN_ALPHA * x + (1.0 + g1) * y, ln_g[i, 0], ln_b[i, 0])
        y = conv_ffn(x * (1.0 + sc2) + sh2, ffn_up[i], ffn_conv_w[i], ffn_conv_b[i], ffn_down[i])
        x = layer_norm(DN_ALPHA * x + (1.0 + g2) * y, ln_g[i, 1], ln_b[i, 1])
    return x


DEPTH_2 = 1

HG_HEADS = 4
HG_HD = 128
HG_WIDTH = HG_HEADS * HG_HD
HG_CHUNK = 64
NSA_HEADS = 8
NSA_KV_HEADS = 2
NSA_HD = 64
NSA_GROUP = NSA_HEADS // NSA_KV_HEADS
NSA_WIDTH = NSA_HEADS * NSA_HD
NSA_KV_WIDTH = NSA_KV_HEADS * NSA_HD
N_BRANCH = 3
CMP_BLOCK = 32
CMP_STRIDE = 16
CMP_HIDDEN = 256
SLC_BLOCK = 64
SLC_TOPK = 16
SLC_Q_CHUNK = 64
WIN = 512
WIN_Q_BLOCK = 128
MIX_WIDTH = HG_WIDTH + NSA_WIDTH
ROPE_DIM = NSA_HD // 4
ROPE_THETA = 500000.0
D_FF = 2816
CONV_W = 3
EPS = 1e-6
NEG = -1e30
IN_SIZES = [HG_WIDTH] * 4 + [NSA_WIDTH] + [NSA_KV_WIDTH] * 6 + [N_BRANCH * NSA_HEADS]
IN_COLS = sum(IN_SIZES)


def rmsnorm(x, g):
    xf = x.astype(jnp.float32)
    y = xf * lax.rsqrt(jnp.mean(xf * xf, axis=-1, keepdims=True) + EPS)
    return (y * g.astype(jnp.float32)).astype(x.dtype)

def rope_partial(x, pos):
    half = ROPE_DIM // 2
    inv = ROPE_THETA ** (-jnp.arange(half, dtype=jnp.float32) * 2.0 / ROPE_DIM)
    ang = pos.astype(jnp.float32)[:, None, :, None] * inv
    cos, sin = jnp.cos(ang), jnp.sin(ang)
    xf = x.astype(jnp.float32)
    x1, x2, rest = xf[..., :half], xf[..., half:ROPE_DIM], xf[..., ROPE_DIM:]
    out = jnp.concatenate([x1 * cos - x2 * sin, x2 * cos + x1 * sin, rest], axis=-1)
    return out.astype(x.dtype)

def to_heads(z, n, hd):
    B, T, _ = z.shape
    return z.reshape(B, T, n, hd).transpose(0, 2, 1, 3)

def hgrn2(q_pre, f_pre, i_pre, g_pre, lb, norm_g):
    B, T, _ = q_pre.shape
    f32 = jnp.float32
    nc = T // HG_CHUNK
    zf = f_pre.astype(f32)
    lbf = lb.astype(f32)
    logf = jnp.logaddexp(jnp.log(lbf), jnp.log1p(-lbf) + jax.nn.log_sigmoid(zf))
    k = (1.0 - lbf) * jax.nn.sigmoid(-zf)
    q = jax.nn.silu(q_pre.astype(f32))
    v = i_pre.astype(f32)

    def chunked(z):
        return z.reshape(B, nc, HG_CHUNK, HG_HEADS, HG_HD).transpose(1, 0, 3, 2, 4)

    qc, kc, vc = chunked(q), chunked(k), chunked(v)
    bc = jnp.cumsum(chunked(logf), axis=-2)
    causal = jnp.tril(jnp.ones((HG_CHUNK, HG_CHUNK), dtype=bool))

    def step(S, inp):
        qi, ki, vi, bi = inp
        o_inter = jnp.einsum('bhtk,bhkv->bhtv', qi * jnp.exp(bi), S)
        diff = bi[:, :, :, None, :] - bi[:, :, None, :, :]
        dec = jnp.where(causal[:, :, None], jnp.exp(jnp.minimum(diff, 0.0)), 0.0)
        A = jnp.einsum('bhtsk,bhsk->bhts', dec * qi[:, :, :, None, :], ki)
        o = o_inter + jnp.einsum('bhts,bhsv->bhtv', A, vi)
        bl = bi[:, :, -1:, :]
        S = jnp.exp(bl[:, :, 0, :])[..., None] * S + jnp.einsum('bhsk,bhsv->bhkv', ki * jnp.exp(bl - bi), vi)
        return S, o

    S0 = jnp.zeros((B, HG_HEADS, HG_HD, HG_HD), f32)
    _, o = lax.scan(step, S0, (qc, kc, vc, bc))
    o = o.transpose(1, 0, 3, 2, 4).reshape(B, T, HG_HEADS, HG_HD)
    g = jax.nn.silu(g_pre.astype(f32)).reshape(B, T, HG_HEADS, HG_HD)
    o = rmsnorm(o, norm_g) * g
    return o.reshape(B, T, HG_WIDTH).astype(q_pre.dtype)

def compress(blocks, pe, w1, w2):
    B, G, n, L, hd = blocks.shape
    flat = (blocks + pe).reshape(B, G, n, L * hd)
    return jax.nn.silu(flat @ w1) @ w2

def nsa(q_pre, kc_pre, vc_pre, ks_pre, vs_pre, kw_pre, vw_pre, g_pre, pos, q_g, k_g, pe, w1, w2):
    B, T, _ = q_pre.shape
    f32 = jnp.float32
    G, R, hd = NSA_KV_HEADS, NSA_GROUP, NSA_HD
    scale = NSA_HD ** -0.5
    tpos = jnp.arange(T)

    q = rope_partial(rmsnorm(to_heads(q_pre, NSA_HEADS, hd), q_g), pos).reshape(B, G, R, T, hd)
    k_c = rope_partial(rmsnorm(to_heads(kc_pre, G, hd), k_g[0]), pos)
    k_s = rope_partial(rmsnorm(to_heads(ks_pre, G, hd), k_g[1]), pos)
    k_w = rope_partial(rmsnorm(to_heads(kw_pre, G, hd), k_g[2]), pos)
    v_c, v_s, v_w = to_heads(vc_pre, G, hd), to_heads(vs_pre, G, hd), to_heads(vw_pre, G, hd)

    n_cmp = (T - CMP_BLOCK) // CMP_STRIDE + 1
    cidx = np.arange(n_cmp)[:, None] * CMP_STRIDE + np.arange(CMP_BLOCK)[None]
    k_cmp = compress(k_c[:, :, cidx], pe[0], w1[0], w2[0])
    v_cmp = compress(v_c[:, :, cidx], pe[1], w1[1], w2[1])
    s = jnp.einsum('bgrtd,bgnd->bgrtn', q, k_cmp).astype(f32) * scale
    cvalid = jnp.asarray(cidx[:, -1])[None, :] <= tpos[:, None]
    any_valid = jnp.any(cvalid, axis=-1, keepdims=True)
    p_cmp = jax.nn.softmax(jnp.where(cvalid, s, NEG), axis=-1) * any_valid
    o_cmp = jnp.einsum('bgrtn,bgnd->bgrtd', p_cmp.astype(v_cmp.dtype), v_cmp)

    nb = T // SLC_BLOCK
    n_sel = min(SLC_TOPK, nb)
    cst = np.arange(n_cmp) * CMP_STRIDE
    sst = np.arange(nb) * SLC_BLOCK
    ovl = np.clip(np.minimum(cst[:, None] + CMP_BLOCK, sst[None] + SLC_BLOCK)
                  - np.maximum(cst[:, None], sst[None]), 0, None) / CMP_BLOCK
    M = jnp.asarray(ovl, dtype=f32)
    imp = jnp.einsum('bgtn,nj->bgtj', p_cmp.sum(axis=2), M)
    cur = tpos // SLC_BLOCK
    j = jnp.arange(nb)
    forced = (j[None] == 0) | (j[None] == cur[:, None]) | (j[None] == cur[:, None] - 1)
    blk_causal = j[None] <= cur[:, None]
    imp = jnp.where(blk_causal, jnp.where(forced, jnp.inf, imp), -1.0)
    _, sel = lax.top_k(imp, n_sel)

    kb = k_s.reshape(B, G, nb, SLC_BLOCK, hd)
    vb = v_s.reshape(B, G, nb, SLC_BLOCK, hd)
    nq = T // SLC_Q_CHUNK
    q_ch = q.reshape(B, G, R, nq, SLC_Q_CHUNK, hd).transpose(3, 0, 1, 2, 4, 5)
    sel_ch = sel.reshape(B, G, nq, SLC_Q_CHUNK, n_sel).transpose(2, 0, 1, 3, 4)
    t_ch = tpos.reshape(nq, SLC_Q_CHUNK)
    gather = jax.vmap(jax.vmap(lambda blocks, ix: blocks[ix]))
    offs = jnp.arange(SLC_BLOCK)

    def sel_chunk(args):
        qc, ic, tc = args
        kg = gather(kb, ic)
        vg = gather(vb, ic)
        sc = jnp.einsum('bgrqd,bgqnld->bgrqnl', qc, kg).astype(f32) * scale
        kpos = ic[..., None] * SLC_BLOCK + offs
        m = kpos <= tc[None, None, :, None, None]
        sc = jnp.where(m[:, :, None], sc, NEG)
        shp = sc.shape
        p = jax.nn.softmax(sc.reshape(shp[:-2] + (shp[-2] * shp[-1],)), axis=-1).reshape(shp)
        return jnp.einsum('bgrqnl,bgqnld->bgrqd', p.astype(vg.dtype), vg)

    o_slc = lax.map(sel_chunk, (q_ch, sel_ch, t_ch))
    o_slc = o_slc.transpose(1, 2, 3, 0, 4, 5).reshape(B, G, R, T, hd)

    nwb = T // WIN_Q_BLOCK
    span = WIN + WIN_Q_BLOCK
    widx = np.arange(nwb)[:, None] * WIN_Q_BLOCK + np.arange(span)[None]
    padw = ((0, 0), (0, 0), (WIN, 0), (0, 0))
    kwin = jnp.pad(k_w, padw)[:, :, widx]
    vwin = jnp.pad(v_w, padw)[:, :, widx]
    qw = q.reshape(B, G, R, nwb, WIN_Q_BLOCK, hd)
    sw = jnp.einsum('bgrnqd,bgnkd->bgrnqk', qw, kwin).astype(f32) * scale
    kpos = jnp.asarray(widx - WIN)[:, None, :]
    qpos = (jnp.arange(nwb)[:, None] * WIN_Q_BLOCK + jnp.arange(WIN_Q_BLOCK)[None])[:, :, None]
    mw = (kpos <= qpos) & (qpos - kpos < WIN) & (kpos >= 0)
    pw = jax.nn.softmax(jnp.where(mw, sw, NEG), axis=-1)
    o_win = jnp.einsum('bgrnqk,bgnkd->bgrnqd', pw.astype(vwin.dtype), vwin).reshape(B, G, R, T, hd)

    gates = jax.nn.sigmoid(g_pre.astype(f32)).reshape(B, T, NSA_HEADS, N_BRANCH)
    gates = gates.transpose(0, 2, 1, 3).reshape(B, G, R, T, N_BRANCH)
    o = (gates[..., 0:1] * o_cmp.astype(f32) + gates[..., 1:2] * o_slc.astype(f32)
         + gates[..., 2:3] * o_win.astype(f32))
    o = o.reshape(B, NSA_HEADS, T, hd).transpose(0, 2, 1, 3).reshape(B, T, NSA_WIDTH)
    return o.astype(q_pre.dtype)

def causal_dwconv_2(u, w, b):
    T = u.shape[1]
    up = jnp.pad(u, ((0, 0), (CONV_W - 1, 0), (0, 0)))
    y = b
    for j in range(CONV_W):
        y = y + up[:, j:j + T] * w[j]
    return y

def second_inputs(seed: int = 0) -> dict:
    key = jax.random.key(seed)
    ks = jax.random.split(key, 24)
    f32 = jnp.float32

    def nrm(k, shape, s):
        return jax.random.normal(k, shape, f32) * s

    return {
        "x": nrm(ks[0], (BATCH, SEQ, D_MODEL), 1.0),
        "c": nrm(ks[1], (BATCH, D_MODEL), 1.0),
        "positions": (jnp.arange(SEQ, dtype=jnp.int32)[None]
                      + jax.random.randint(ks[2], (BATCH, 1), 0, 4096, dtype=jnp.int32)),
        "w_ada": nrm(ks[3], (DEPTH_2, D_MODEL, 6 * D_MODEL), D_MODEL ** -0.5),
        "b_ada": nrm(ks[4], (DEPTH_2, 6 * D_MODEL), 0.02),
        "norm1_g": 1.0 + nrm(ks[5], (DEPTH_2, D_MODEL), 0.02),
        "w_in": nrm(ks[6], (DEPTH_2, D_MODEL, IN_COLS), D_MODEL ** -0.5),
        "lb_logits": nrm(ks[7], (DEPTH_2 + 1, HG_WIDTH), 1.0),
        "hg_norm_g": 1.0 + nrm(ks[8], (DEPTH_2, HG_HD), 0.02),
        "q_norm_g": 1.0 + nrm(ks[9], (DEPTH_2, NSA_HD), 0.02),
        "k_norm_g": 1.0 + nrm(ks[10], (DEPTH_2, N_BRANCH, NSA_HD), 0.02),
        "pe_cmp": nrm(ks[11], (DEPTH_2, 2, CMP_BLOCK, NSA_HD), 0.02),
        "w_cmp1": nrm(ks[12], (DEPTH_2, 2, CMP_BLOCK * NSA_HD, CMP_HIDDEN), (CMP_BLOCK * NSA_HD) ** -0.5),
        "w_cmp2": nrm(ks[13], (DEPTH_2, 2, CMP_HIDDEN, NSA_HD), CMP_HIDDEN ** -0.5),
        "w_out": nrm(ks[14], (DEPTH_2, MIX_WIDTH, D_MODEL), MIX_WIDTH ** -0.5),
        "norm2_g": 1.0 + nrm(ks[15], (DEPTH_2, D_MODEL), 0.02),
        "w_up": nrm(ks[16], (DEPTH_2, D_MODEL, 2 * D_FF), D_MODEL ** -0.5),
        "conv_w": nrm(ks[17], (DEPTH_2, CONV_W, 2 * D_FF), CONV_W ** -0.5),
        "conv_b": nrm(ks[18], (DEPTH_2, 2 * D_FF), 0.02),
        "w_down": nrm(ks[19], (DEPTH_2, D_FF, D_MODEL), D_FF ** -0.5),
    }

def second_block(x, c, positions, w_ada, b_ada, norm1_g, w_in, lb_logits, hg_norm_g, q_norm_g,
              k_norm_g, pe_cmp, w_cmp1, w_cmp2, w_out, norm2_g, w_up, conv_w, conv_b, w_down):
    offsets = np.cumsum(IN_SIZES)[:-1].tolist()
    lbs = jnp.cumsum(jax.nn.softmax(lb_logits.astype(jnp.float32), axis=0), axis=0)
    cs = jax.nn.silu(c)
    for l in range(DEPTH_2):
        mod = cs @ w_ada[l] + b_ada[l]
        sh1, sc1, gt1, sh2, sc2, gt2 = [m[:, None, :] for m in jnp.split(mod, 6, axis=-1)]

        h = rmsnorm(x, norm1_g[l]) * (1.0 + sc1) + sh1
        z = h @ w_in[l]
        (hq, hf, hi, hgt, nq_, kc_, vc_, ks_, vs_, kw_, vw_, ng_) = jnp.split(z, offsets, axis=-1)
        o_hg = hgrn2(hq, hf, hi, hgt, lbs[l], hg_norm_g[l])
        o_nsa = nsa(nq_, kc_, vc_, ks_, vs_, kw_, vw_, ng_, positions, q_norm_g[l], k_norm_g[l],
                    pe_cmp[l], w_cmp1[l], w_cmp2[l])
        mix = jnp.concatenate([o_hg, o_nsa], axis=-1) @ w_out[l]
        x = x + gt1 * mix

        h2 = rmsnorm(x, norm2_g[l]) * (1.0 + sc2) + sh2
        u = causal_dwconv_2(h2 @ w_up[l], conv_w[l], conv_b[l])
        a, v = jnp.split(u, 2, axis=-1)
        x = x + gt2 * ((jax.nn.silu(a) * v) @ w_down[l])
    return x


def setup_inputs(seed=0):
    out = dict(first_inputs(seed))
    for name, value in second_inputs(seed + 1).items():
        if name != "x":
            out[name + "_2"] = value
    return out


def reference(
    x, c, cond_w, cond_b, ada_w, ada_b, ln_g, ln_b, ffn_up, ffn_conv_w, ffn_conv_b, ffn_down,
    gdn_w_in, gdn_conv_w, gdn_a_log, gdn_dt_bias, gdn_norm_w, gdn_w_out, ret_w_in, ret_w_out,
    gmlp_w_in, gmlp_ln_g, gmlp_ln_b, gmlp_w_s, gmlp_b_s, gmlp_w_out, sb_w_in, sb_w_out, c_2,
    positions_2, w_ada_2, b_ada_2, norm1_g_2, w_in_2, lb_logits_2, hg_norm_g_2, q_norm_g_2,
    k_norm_g_2, pe_cmp_2, w_cmp1_2, w_cmp2_2, w_out_2, norm2_g_2, w_up_2, conv_w_2, conv_b_2,
    w_down_2,
):
    x = first_block(
        x, c, cond_w, cond_b, ada_w, ada_b, ln_g, ln_b, ffn_up, ffn_conv_w, ffn_conv_b,
        ffn_down, gdn_w_in, gdn_conv_w, gdn_a_log, gdn_dt_bias, gdn_norm_w, gdn_w_out, ret_w_in,
        ret_w_out, gmlp_w_in, gmlp_ln_g, gmlp_ln_b, gmlp_w_s, gmlp_b_s, gmlp_w_out, sb_w_in,
        sb_w_out,
    )
    return second_block(
        x, c_2, positions_2, w_ada_2, b_ada_2, norm1_g_2, w_in_2, lb_logits_2, hg_norm_g_2,
        q_norm_g_2, k_norm_g_2, pe_cmp_2, w_cmp1_2, w_cmp2_2, w_out_2, norm2_g_2, w_up_2,
        conv_w_2, conv_b_2, w_down_2,
    )


_drawn_inputs = setup_inputs


def setup_inputs(seed=0):
    import zlib

    import numpy as np

    out = dict(_drawn_inputs(seed))
    spreads = {}
    factors = {'cond_b': 8.0,
     'ada_b': 4.429,
     'ffn_conv_b': 8.0,
     'gdn_norm_w': 8.0,
     'norm1_g_2': 6.833,
     'hg_norm_g_2': 22.073,
     'q_norm_g_2': 93.804,
     'k_norm_g_2': 30.593,
     'pe_cmp_2': 200.0,
     'norm2_g_2': 20.198,
     'conv_b_2': 20.775}
    for name, (base, spread) in spreads.items():
        noise = np.random.default_rng([zlib.crc32(name.encode()), seed]).standard_normal(out[name].shape)
        drawn = base * np.exp(spread * noise) if base else spread * noise
        out[name] = __import__('jax').numpy.asarray(drawn.astype(out[name].dtype))
    for name, factor in factors.items():
        out[name] = (out[name] * factor).astype(out[name].dtype)
    return out
```

```python
from contextlib import ExitStack

import numpy as np
import concourse.bass as bass
from concourse import mybir

ACT = mybir.ActivationFunctionType
ALU = mybir.AluOpType
F32 = mybir.dt.float32
I32 = mybir.dt.int32
AX = mybir.AxisListType.X

P = 128
D = 1024
T = 512
KC = D // P
NT = T // P
ALPHA = 4.0 ** 0.25
LN_EPS = 1e-5
EPS = 1e-6
FF = 2816
FC = FF // P
GH = 8
RH, RDK, RDV = 4, 256, 512
HH = 4
NH, NG, ND = 8, 2, 64
CB, CS = 32, 16
NCMP = (T - CB) // CS + 1
NEG = -1e30
MAGIC = 1.5 * 2.0 ** 23
SLOTS = 3
SLOT = 4096
LEVELS = [1, 2, 4, 8, 16, 32, 64]


class Steps:

    def __init__(self, plan, engine):
        self.n, self.plan, self.engine = 0, plan, engine

    def tick(self, *name):
        self.n += 1
        if name:
            self.plan[(self.engine, *name)] = self.n
        return 1

    def mark(self, *name):
        self.plan[(self.engine, *name)] = self.n


def load_order():
    out = [("cond", 0), ("cond", 1)] + [("ada", 0, l) for l in range(4)]
    out.append(("gdn", 0))
    for h in range(GH):
        if h + 1 < GH:
            out.append(("gdn", h + 1))
        out.append(("ada", 0, 4 + h))
    out += [("gdn_out", l) for l in range(2)]
    for i in range(3):
        for l in range(FC // 2):
            out.append(("up", i, l))
            if i < 2:
                out.append(("ada", i + 1, l))
        if i < 2:
            out.append(("ada", i + 1, 11))
        out += [("down", i, n) for n in range(KC)]
        if i == 0:
            out.append(("ret_qk", 0))
            for h in range(RH):
                out += [("ret_v", h), ("ret_g", h)]
                if h + 1 < RH:
                    out.append(("ret_qk", h + 1))
            out += [("ret_out", l) for l in range(4)]
        if i == 1:
            out += [("mix", h) for h in range(HH)] + [("mix_hi", 0), ("mix_c", 0), ("mix_v", 0)]
            out += [("cmp", 0, 0), ("cmp", 0, 1), ("cmp", 1, 0), ("cmp", 1, 1)]
            out += [("mix_out", l) for l in range(2)]
    return out


def program(nc, dr, out, plan):
    loads = load_order()
    load_at = {key: n for n, key in enumerate(loads)}

    with ExitStack() as ctx:
        def sb(name, shape, dt=F32):
            return ctx.enter_context(nc.sbuf_tensor(name, shape, dt))

        def sem(name):
            return ctx.enter_context(nc.semaphore(name))

        B = [ctx.enter_context(nc.psum_tensor(f"bank{i}", [P, 512], F32)) for i in range(8)]
        B4 = [b[:, :].rearrange("p (i c) -> p i c", c=P) for b in B]

        pe_done, act_done, dve_done, pool_done = (sem(n) for n in ("pe_done", "act_done", "dve_done", "pool_done"))
        ring_full = [sem(f"ring_full{s}") for s in range(SLOTS)]
        consts_in = sem("consts_in")
        ret_tables_in = sem("ret_tables_in")
        nsa_tables_in = sem("nsa_tables_in")
        stored = sem("stored")
        PE, AC, DV, PO = (Steps(plan, e) for e in ("pe", "act", "dve", "pool"))
        DONE = {"pe": pe_done, "act": act_done, "dve": dve_done, "pool": pool_done}

        def at(*name):
            return plan.get(name, 1)

        ring = sb("ring", [P, SLOTS, SLOT])
        XT = sb("XT", [P, KC, T])
        HT = sb("HT", [P, KC, T])
        arena = sb("arena", [P, 21504])
        ident = sb("ident", [P, P])
        maskL = sb("maskL", [P, 7, P])
        maskU = sb("maskU", [P, 7, P])
        causal = sb("causal", [P, 4, P])
        ones = sb("ones", [P, 4, P])
        sel = sb("sel", [GH, GH, P])
        mod = sb("mod", [P, 3, 48])
        mod1 = sb("mod1", [P, 3, 48])
        ada_b = sb("ada_b", [P, 3, 48])
        lnp = sb("lnp", [P, 6, KC, 2])
        ffc = sb("ffc", [P, 3, FC, 2, 4])
        gconv = sb("gconv", [P, 3 * GH, 4])
        gvec = sb("gvec", [P, 16])
        cvec = sb("cvec", [P, 3, KC])
        evec = sb("evec", [P, 2, KC])
        wab = sb("wab", [P, KC, 64])
        small = sb("small", [P, 64])

        def region(offset, *shape):
            size = int(np.prod(shape))
            v = arena[:, offset:offset + size]
            if len(shape) == 2:
                v = v.rearrange("p (a b) -> p a b", b=shape[1])
            if len(shape) == 3:
                v = v.rearrange("p (a b c) -> p a b c", b=shape[1], c=shape[2])
            return v

        block = ctx.enter_context(nc.Block())
        stages = []

        def begin(eng, me, stage):
            n = stages.index(stage) if stage in stages else (stages.append(stage) or len(stages) - 1)
            if n:
                for other, steps in (("pe", PE), ("act", AC), ("dve", DV), ("pool", PO)):
                    v = plan.get((other, "end", stages[n - 1]), 0)
                    if v:
                        eng.wait_ge(DONE[other], v)

        def slot_of(pe, key):
            n = load_at[key]
            pe.wait_ge(ring_full[n % SLOTS], 16 * (n // SLOTS + 1))
            return ring[:, n % SLOTS, :]

        def units(pe, key, kc=KC, width=P):
            v = slot_of(pe, key)
            n = min(SLOT // (kc * width), 4)
            return v[:, 0:n * kc * width].rearrange("p (u k n) -> p u k n", u=n, k=kc)

        def used(key):
            PE.mark("used", load_at[key])

        def pe_ada(pe, i, l, e):
            w = units(pe, ("ada", i, l))
            for u in range(4):
                c = 64 + 48 * i + 4 * l + u
                for k in range(KC):
                    last = nc.tensor.matmul(B[7][:, c:c + 1], w[:, u, k, :], evec[:, e, k:k + 1],
                                            start=(k == 0), stop=(k == KC - 1))
            last.then_inc(pe_done, PE.tick("ada", i, l))
            used(("ada", i, l))

        def pe_residual(pe, tag, key_of, kc, src, per_load, has_mean):
            begin(pe, "pe", tag)
            for n in range(KC):
                w = units(pe, key_of(n // per_load), kc)
                bank = B[n % 2]
                if n >= 2:
                    pe.wait_ge(dve_done, at("dve", tag, "res", n - 2))
                for k in range(kc):
                    last = nc.tensor.matmul(bank[:, :], w[:, n % per_load, k, :], src(k), start=(k == 0), stop=(k == kc - 1))
                last.then_inc(pe_done, PE.tick(tag, "proj", n))
                if n % per_load == per_load - 1:
                    used(key_of(n // per_load))
                if has_mean and n:
                    pe.wait_ge(dve_done, at("dve", tag, "res", n - 1))
                    nc.tensor.matmul(B[2][:, :], ones[:, 1, :], XT[:, n - 1, :], start=(n == 1), stop=False)
            if has_mean:
                pe.wait_ge(dve_done, at("dve", tag, "res", KC - 1))
                nc.tensor.matmul(B[2][:, :], ones[:, 1, :], XT[:, KC - 1, :], start=False, stop=True)\
                    .then_inc(pe_done, PE.tick(tag, "mean"))
            PE.mark("end", tag)

        def pe_squares(pe, tag):
            begin(pe, "pe", tag)
            for n in range(KC):
                pe.wait_ge(act_done, at("act", tag, "square", n))
                nc.tensor.matmul(B[3][:, :], ones[:, 1, :], arena[:, (n % 4) * T:(n % 4 + 1) * T],
                                 start=(n == 0), stop=(n == KC - 1)).then_inc(pe_done, PE.tick(tag, "square_used", n))
            PE.mark("end", tag)

        def pe_up(pe, i):
            tag = f"up{i}"
            begin(pe, "pe", tag)
            for j in range(FC):
                w = units(pe, ("up", i, j // 2))
                if j >= 2:
                    pe.wait_ge(dve_done, at("dve", tag, "hidden", j - 2))
                for half in range(2):
                    for k in range(KC):
                        last = nc.tensor.matmul(B[2 * (j % 2) + half][:, :], w[:, 2 * (j % 2) + half, k, :], HT[:, k, :],
                                                start=(k == 0), stop=(k == KC - 1))
                last.then_inc(pe_done, PE.tick(tag, "proj", j))
                if j % 2:
                    used(("up", i, j // 2))
                    if i < 2:
                        pe_ada(pe, i + 1, j // 2, i)
            if i < 2:
                pe_ada(pe, i + 1, 11, i)
            PE.mark("end", tag)

        hidden = region(0, FC, T)
        ffn_y = region(FC * T, 2, T)
        ffn_u = region(FC * T + 2 * T, 2, T)
        sq4 = region(0, 4, T)
        rstd = region(4 * T, T)

        def dve_residual(dve, tag, gate, i, scaled):
            begin(dve, "dve", tag)
            if scaled:
                dve.wait_ge(pool_done, at("pool", tag, "alpha"))
            g = mod1 if scaled else mod
            for n in range(KC):
                dve.wait_ge(pe_done, at("pe", tag, "proj", n))
                nc.vector.scalar_tensor_tensor(out=XT[:, n, :], in0=B[n % 2][:, :], scalar=g[:, i, gate + n:gate + n + 1],
                                               in1=XT[:, n, :], op0=ALU.mult, op1=ALU.add)\
                    .then_inc(dve_done, DV.tick(tag, "res", n))
            DV.mark("end", tag)

        def pool_residual(pool, tag):
            begin(pool, "pool", tag)
            for n in range(KC):
                last = nc.gpsimd.tensor_scalar(XT[:, n, :], XT[:, n, :], ALPHA, 0.0, ALU.mult, ALU.add)
            last.then_inc(pool_done, PO.tick(tag, "alpha"))
            PO.mark("end", tag)

        def dve_layer_norm(dve, tag, before, which, i, sc, sh, modulate):
            begin(dve, "dve", tag)
            for n in range(KC):
                nc.vector.tensor_tensor(XT[:, n, :], XT[:, n, :], B[2][:, :], ALU.subtract)\
                    .then_inc(dve_done, DV.tick(tag, "centred", n))
            dve.wait_ge(act_done, at("act", tag, "std"))
            nc.vector.reciprocal(rstd, rstd).then_inc(dve_done, DV.tick())
            dve.wait_ge(dve_done, DV.n)
            for n in range(KC):
                nc.vector.tensor_tensor(XT[:, n, :], XT[:, n, :], rstd, ALU.mult).then_inc(dve_done, DV.tick(tag, "normed", n))
            if modulate:
                for n in range(KC):
                    dve.wait_ge(act_done, at("act", tag, "affine", n))
                    nc.vector.tensor_scalar(HT[:, n, :], XT[:, n, :], mod1[:, i, sc + n:sc + n + 1], mod[:, i, sh + n:sh + n + 1],
                                            ALU.mult, ALU.add).then_inc(dve_done, DV.tick(tag, "modulated", n))
            DV.mark("end", tag)

        def act_squares(act, tag, centred):
            for n in range(KC):
                if centred:
                    act.wait_ge(dve_done, at("dve", tag, "centred", n))
                if n >= 4:
                    act.wait_ge(pe_done, at("pe", tag, "square_used", n - 4))
                nc.scalar.activation(sq4[:, n % 4, :], XT[:, n, :], ACT.Square).then_inc(act_done, AC.tick(tag, "square", n))
            act.wait_ge(pe_done, at("pe", tag, "square_used", KC - 1))
            eps = gvec[:, 4:5] if centred else gvec[:, 5:6]
            nc.scalar.activation(rstd, B[3][:, :], ACT.Sqrt, bias=eps).then_inc(act_done, AC.tick(tag, "std"))

        def act_layer_norm(act, tag, which):
            begin(act, "act", tag)
            act_squares(act, tag, True)
            for n in range(KC):
                act.wait_ge(dve_done, at("dve", tag, "normed", n))
                nc.scalar.activation(XT[:, n, :], XT[:, n, :], ACT.Identity, bias=lnp[:, which, n, 1:2], scale=lnp[:, which, n, 0:1])\
                    .then_inc(act_done, AC.tick(tag, "affine", n))
            AC.mark("end", tag)

        def act_rms(act, tag):
            begin(act, "act", tag)
            act_squares(act, tag, False)
            AC.mark("end", tag)

        def dve_rms(dve, tag, which, sc, sh):
            begin(dve, "dve", tag)
            dve.wait_ge(act_done, at("act", tag, "std"))
            nc.vector.reciprocal(rstd, rstd).then_inc(dve_done, DV.tick())
            dve.wait_ge(dve_done, DV.n)
            for n in range(KC):
                nc.vector.scalar_tensor_tensor(out=HT[:, n, :], in0=XT[:, n, :], scalar=lnp[:, which, n, 0:1], in1=rstd,
                                               op0=ALU.mult, op1=ALU.mult).then_inc(dve_done, DV.tick())
            dve.wait_ge(dve_done, DV.n)
            for n in range(KC):
                nc.vector.tensor_scalar(HT[:, n, :], HT[:, n, :], mod1[:, 2, sc + n:sc + n + 1], mod[:, 2, sh + n:sh + n + 1],
                                        ALU.mult, ALU.add).then_inc(dve_done, DV.tick(tag, "modulated", n))
            DV.mark("end", tag)

        def conv(dve, out_, src, taps, width):
            nc.vector.tensor_scalar(out_, src[:, :], taps(width - 1), None, ALU.mult).then_inc(dve_done, DV.tick())
            for j in range(1, width):
                dve.wait_ge(dve_done, DV.n)
                last = nc.vector.scalar_tensor_tensor(out=out_[:, j:], in0=src[:, 0:T - j], scalar=taps(width - 1 - j), in1=out_[:, j:],
                                                      op0=ALU.mult, op1=ALU.add)
                if j < width - 1:
                    last.then_inc(dve_done, DV.tick())
            return last

        def dve_up(dve, i):
            tag = f"up{i}"
            begin(dve, "dve", tag)
            for j in range(FC):
                s = j % 2
                dve.wait_ge(pe_done, at("pe", tag, "proj", j))
                conv(dve, ffn_y[:, s, :], B[2 * s], lambda m: ffc[:, i, j, 0, m:m + 1], 3).then_inc(dve_done, DV.tick(tag, "conv", j))
                if i == 2:
                    conv(dve, ffn_u[:, s, :], B[2 * s + 1], lambda m: ffc[:, i, j, 1, m:m + 1], 3).then_inc(dve_done, DV.tick())
                    dve.wait_ge(dve_done, DV.n)
                    dve.wait_ge(act_done, at("act", tag, "gate", j))
                    nc.vector.scalar_tensor_tensor(out=hidden[:, j, :], in0=ffn_u[:, s, :], scalar=ffc[:, i, j, 1, 3:4],
                                                   in1=ffn_y[:, s, :], op0=ALU.add, op1=ALU.mult)\
                        .then_inc(dve_done, DV.tick(tag, "hidden", j))
                else:
                    dve.wait_ge(act_done, at("act", tag, "gate", j))
                    nc.vector.tensor_tensor(hidden[:, j, :], ffn_y[:, s, :], B[2 * s + 1][:, :], ALU.mult)\
                        .then_inc(dve_done, DV.tick(tag, "hidden", j))
            if i < 2:
                dve_mod(dve, i + 1, 0, 48, 11)
            DV.mark("end", tag)

        def act_up(act, i):
            tag = f"up{i}"
            begin(act, "act", tag)
            for j in range(FC):
                act.wait_ge(dve_done, at("dve", tag, "conv", j))
                nc.scalar.activation(ffn_y[:, j % 2, :], ffn_y[:, j % 2, :], ACT.Silu, bias=ffc[:, i, j, 0, 3:4])\
                    .then_inc(act_done, AC.tick(tag, "gate", j))
            AC.mark("end", tag)

        def dve_mod(dve, i, c0, c1, l):
            dve.wait_ge(pe_done, at("pe", "ada", i, l))
            nc.vector.tensor_tensor(mod[:, i, c0:c1], B[7][:, 64 + 48 * i + c0:64 + 48 * i + c1], ada_b[:, i, c0:c1], ALU.add)\
                .then_inc(dve_done, DV.tick())
            dve.wait_ge(dve_done, DV.n)
            nc.vector.tensor_scalar(mod1[:, i, c0:c1], mod[:, i, c0:c1], 1.0, None, ALU.add).then_inc(dve_done, DV.tick("mod", i, c1))

        o = 0
        OT_g = region(0, GH, T)
        o = GH * T
        G = {}
        for name in ("cq", "ck", "cv", "qs", "ks", "vs", "zs", "s1", "s2", "r1", "r2", "dp", "dn", "L", "LT", "D", "E", "Tm",
                     "QK", "vb", "kb", "kd", "U", "W", "qe", "eg"):
            G[name] = region(o, T)
            G[name + "4"] = region(o, NT, P)
            o += T
        ROWS = region(o, T); o += T
        COLS = region(o, NT, P); o += T
        gdn_S = region(o, 2, P); o += 2 * P
        gdn_vn = region(o, 2, P); o += 2 * P
        EGL = small[:, 0:4]
        EGLB = small[:, 8:40].rearrange("p (h i) -> p h i", i=4)
        rowt = [G["s1"], G["s2"], G["r1"], G["r2"], G["dp"]]
        reset = G["dn"]
        assert o <= 21504

        def pe_dense4(pe, key, n0, n1):
            h = key[1]
            w = units(pe, key)
            for n in range(n0, n1):
                u, k = n // KC, n % KC
                if k == 0:
                    if u >= 2:
                        pe.wait_ge(dve_done, at("dve", "gdn", "conv", h, u - 2))
                    elif h and u == 0:
                        pe.wait_ge(dve_done, at("dve", "gdn", "conv", h - 1, 2))
                    elif h and u == 1:
                        pe.wait_ge(act_done, at("act", "gdn", "z", h - 1))
                last = nc.tensor.matmul(B[u % 2][:, :], w[:, u, k, :], HT[:, k, :], start=(k == 0), stop=(k == KC - 1))
                if k == KC - 1:
                    last.then_inc(pe_done, PE.tick("gdn", "proj", h, u))
            if n1 == 4 * KC:
                used(key)

        def pe_gdn(pe):
            begin(pe, "pe", "gdn")
            pe.wait_ge(dve_done, at("dve", "gdn", "input"))
            for k in range(KC):
                last = nc.tensor.matmul(B[3][0:64, :], wab[:, k, :], HT[:, k, :], start=(k == 0), stop=(k == KC - 1))
            last.then_inc(pe_done, PE.tick("gdn", "ab"))
            pe_dense4(pe, ("gdn", 0), 0, 16)
            pe.wait_ge(act_done, at("act", "gdn", "rows"))
            pe.wait_ge(dve_done, at("dve", "gdn", "rows"))
            for i in range(NT):
                last = nc.tensor.transpose(B4[3][:, i, :], ROWS[:, i * P:(i + 1) * P], ident[:, :])
            last.then_inc(pe_done, PE.tick("gdn", "cols"))
            for h in range(GH):
                last = nc.tensor.matmul(B[4][:, 4 * h:4 * h + 4], sel[:, h, :], EGL[0:GH, :], start=True, stop=True)
            last.then_inc(pe_done, PE.tick("gdn", "eglb"))
            pe_dense4(pe, ("gdn", 0), 16, 32)

            for h in range(GH):
                def fill(part):
                    if h + 1 < GH:
                        pe_dense4(pe, ("gdn", h + 1), 2 * part, 2 * part + 2)

                pe.wait_ge(act_done, at("act", "gdn", "sq", h, 0))
                nc.tensor.matmul(B[2][:, :], ones[:, 0, :], G["s1"], start=True, stop=True).then_inc(pe_done, PE.tick("gdn", "ssq", h, 0))
                pe.wait_ge(act_done, at("act", "gdn", "sq", h, 1))
                if h:
                    pe.wait_ge(dve_done, at("dve", "gdn", "out", h - 1))
                nc.tensor.matmul(B[3][:, :], ones[:, 0, :], G["s2"], start=True, stop=True).then_inc(pe_done, PE.tick("gdn", "ssq", h, 1))
                if h == 0:
                    pe.wait_ge(dve_done, at("dve", "gdn", "eglb"))
                nc.tensor.matmul(B[4][:, :], sel[:, h, :], ROWS[0:GH, :], start=True, stop=True).then_inc(pe_done, PE.tick("gdn", "gcb", h))
                pe.wait_ge(act_done, at("act", "gdn", "std", h))
                for i in range(NT):
                    last = nc.tensor.transpose(B4[2][:, i, :], G["vs4"][:, i, :], ident[:, :])
                last.then_inc(pe_done, PE.tick("gdn", "vtok", h))
                pe.wait_ge(dve_done, at("dve", "gdn", "khat", h))
                for i in range(NT):
                    last = nc.tensor.transpose(B4[3][:, i, :], G["ks4"][:, i, :], ident[:, :])
                last.then_inc(pe_done, PE.tick("gdn", "ktok", h))
                for i in range(NT):
                    last = nc.tensor.matmul(B4[5][:, i, :], G["ks4"][:, i, :], G["ks4"][:, i, :], start=True, stop=True)
                last.then_inc(pe_done, PE.tick("gdn", "kk", h))
                for i in range(NT):
                    last = nc.tensor.matmul(B4[6][:, i, :], G["ks4"][:, i, :], G["qs4"][:, i, :], start=True, stop=True)
                last.then_inc(pe_done, PE.tick("gdn", "qk", h))
                fill(0)
                pe.wait_ge(dve_done, at("dve", "gdn", "L", h))
                for i in range(NT):
                    last = nc.tensor.transpose(B4[5][:, i, :], G["L4"][:, i, :], ident[:, :])
                last.then_inc(pe_done, PE.tick("gdn", "LT", h))
                fill(1)
                for l in range(1, 7):
                    pe.wait_ge(dve_done, at("dve", "gdn", "inv", h, l - 1))
                    for i in range(NT):
                        last = nc.tensor.matmul(B4[5][:, i, :], G["LT4"][:, i, :], G["D4"][:, i, :], start=True, stop=True)
                    last.then_inc(pe_done, PE.tick("gdn", "LD", h, l))
                    fill(2 * l)
                    pe.wait_ge(dve_done, at("dve", "gdn", "Tm", h, l))
                    if l < 6:
                        for i in range(NT):
                            last = nc.tensor.matmul(B4[6][:, i, :], G["E4"][:, i, :], G["Tm4"][:, i, :], start=True, stop=True)
                        last.then_inc(pe_done, PE.tick("gdn", "DT", h, l))
                    for i in range(NT):
                        last = nc.tensor.matmul(B4[4][:, i, :], G["Tm4"][:, i, :], G["E4"][:, i, :], start=True, stop=True)
                    last.then_inc(pe_done, PE.tick("gdn", "TE", h, l))
                    fill(2 * l + 1)
                pe.wait_ge(dve_done, at("dve", "gdn", "inv", h, 6))
                for i in range(NT):
                    last = nc.tensor.matmul(B4[2][:, i, :], G["E4"][:, i, :], G["vb4"][:, i, :], start=True, stop=True)
                last.then_inc(pe_done, PE.tick("gdn", "U", h))
                for i in range(NT):
                    last = nc.tensor.matmul(B4[3][:, i, :], G["kb4"][:, i, :], G["E4"][:, i, :], start=True, stop=True)
                last.then_inc(pe_done, PE.tick("gdn", "W", h))
                fill(14)
                pe.wait_ge(act_done, at("act", "gdn", "UW", h))
                pe.wait_ge(pool_done, at("pool", "gdn", "qe", h))
                for i in range(NT):
                    if i:
                        pe.wait_ge(dve_done, at("dve", "gdn", "S", h, i - 1))
                        nc.tensor.matmul(B[2][:, 0:P], G["W4"][:, i, :], gdn_S[:, (i - 1) % 2, :], start=True, stop=True)\
                            .then_inc(pe_done, PE.tick("gdn", "wS", h, i))
                        nc.tensor.matmul(B4[3][:, i, :], gdn_S[:, (i - 1) % 2, :], G["qe4"][:, i, :], start=True, stop=False)
                    pe.wait_ge(dve_done, at("dve", "gdn", "vn", h, i))
                    if i < NT - 1:
                        nc.tensor.matmul(B[5][:, 0:P], G["kd4"][:, i, :], gdn_vn[:, i % 2, :], start=True, stop=True)\
                            .then_inc(pe_done, PE.tick("gdn", "kv", h, i))
                    last = nc.tensor.matmul(B4[3][:, i, :], gdn_vn[:, i % 2, :], G["QK4"][:, i, :], start=(i == 0), stop=True)
                    if i == 1:
                        fill(15)
                last.then_inc(pe_done, PE.tick("gdn", "o", h))
                pe_ada(pe, 0, 4 + h, 0)
                pe.wait_ge(act_done, at("act", "gdn", "osq", h))
                nc.tensor.matmul(B[2][:, :], ones[:, 3, :], G["s1"], start=True, stop=True).then_inc(pe_done, PE.tick("gdn", "oss", h))
            PE.mark("end", "gdn")

        def act_gdn(act):
            begin(act, "act", "gdn")
            S1, S2 = G["s1"], G["s2"]
            act.wait_ge(dve_done, at("dve", "gdn", "zeros"))
            act.wait_ge(pe_done, at("pe", "gdn", "ab"))
            nc.scalar.activation(ROWS[32:32 + GH, :], B[3][32:32 + GH, :], ACT.Sigmoid).then_inc(act_done, AC.tick())
            nc.scalar.activation(S1[0:GH, :], B[3][0:GH, :], ACT.Abs, bias=gvec[0:GH, 2:3]).then_inc(act_done, AC.tick())
            nc.scalar.activation(S2[0:GH, :], B[3][0:GH, :], ACT.Relu, bias=gvec[0:GH, 2:3]).then_inc(act_done, AC.tick())
            act.wait_ge(act_done, AC.n)
            nc.scalar.activation(S1[0:GH, :], S1[0:GH, :], ACT.Exp, scale=-1.0).then_inc(act_done, AC.tick())
            nc.scalar.activation(small[0:GH, 40:41], gvec[0:GH, 1:2], ACT.Exp).then_inc(act_done, AC.tick())
            act.wait_ge(act_done, AC.n)
            nc.scalar.activation(S1[0:GH, :], S1[0:GH, :], ACT.Ln, bias=1.0).then_inc(act_done, AC.tick("gdn", "softplus"))
            act.wait_ge(dve_done, at("dve", "gdn", "gc"))
            nc.scalar.activation(ROWS[64:64 + GH, :], ROWS[0:GH, :], ACT.Exp).then_inc(act_done, AC.tick())
            nc.scalar.activation(ROWS[96:96 + GH, :], G["r1"][0:GH, :], ACT.Exp).then_inc(act_done, AC.tick())
            nc.scalar.activation(EGL[0:GH, :], ROWS[0:GH, P - 1::P], ACT.Exp).then_inc(act_done, AC.tick("gdn", "rows"))

            for h in range(GH):
                for u, (src, dst) in enumerate((("cq", "qs"), ("ck", "ks"), ("cv", "vs"))):
                    act.wait_ge(dve_done, at("dve", "gdn", "conv", h, u))
                    if h and u == 0:
                        act.wait_ge(dve_done, at("dve", "gdn", "out", h - 1))
                        act.wait_ge(pe_done, at("pe", "gdn", "oss", h - 1))
                    nc.scalar.activation(G[dst], G[src], ACT.Silu).then_inc(act_done, AC.tick("gdn", "silu", h, u))
                act.wait_ge(act_done, AC.n)
                nc.scalar.activation(S1, G["qs"], ACT.Square).then_inc(act_done, AC.tick("gdn", "sq", h, 0))
                nc.scalar.activation(S2, G["ks"], ACT.Square).then_inc(act_done, AC.tick("gdn", "sq", h, 1))
                act.wait_ge(pe_done, at("pe", "gdn", "proj", h, 3))
                nc.scalar.activation(G["zs"], B[1][:, :], ACT.Silu).then_inc(act_done, AC.tick("gdn", "z", h))
                act.wait_ge(pe_done, at("pe", "gdn", "ssq", h, 0))
                nc.scalar.activation(G["r1"], B[2][:, :], ACT.Sqrt, bias=gvec[:, 5:6]).then_inc(act_done, AC.tick("gdn", "stdq", h))
                act.wait_ge(pe_done, at("pe", "gdn", "ssq", h, 1))
                nc.scalar.activation(G["r2"], B[3][:, :], ACT.Sqrt, bias=gvec[:, 5:6]).then_inc(act_done, AC.tick("gdn", "std", h))
                act.wait_ge(pe_done, at("pe", "gdn", "gcb", h))
                nc.scalar.activation(G["eg"], B[4][:, :], ACT.Exp).then_inc(act_done, AC.tick("gdn", "eg", h))
                act.wait_ge(dve_done, at("dve", "gdn", "diff", h))
                nc.scalar.activation(G["dp"], G["dp"], ACT.Exp, scale=-1.0).then_inc(act_done, AC.tick())
                nc.scalar.activation(G["dn"], G["dn"], ACT.Exp).then_inc(act_done, AC.tick("gdn", "decay", h))
                act.wait_ge(pe_done, at("pe", "gdn", "LT", h))
                nc.scalar.activation(G["LT"], B[5][:, :], ACT.Copy).then_inc(act_done, AC.tick("gdn", "LT", h))
                act.wait_ge(pe_done, at("pe", "gdn", "W", h))
                nc.scalar.activation(G["U"], B[2][:, :], ACT.Copy).then_inc(act_done, AC.tick())
                nc.scalar.activation(G["W"], B[3][:, :], ACT.Copy).then_inc(act_done, AC.tick("gdn", "UW", h))
                act.wait_ge(pe_done, at("pe", "gdn", "o", h))
                nc.scalar.activation(S1, B[3][:, :], ACT.Square).then_inc(act_done, AC.tick("gdn", "osq", h))
                act.wait_ge(pe_done, at("pe", "gdn", "oss", h))
                nc.scalar.activation(G["r1"], B[2][:, :], ACT.Sqrt, bias=gvec[:, 5:6]).then_inc(act_done, AC.tick("gdn", "ostd", h))
            AC.mark("end", "gdn")

        def dve_conv4(dve, h, u):
            dve.wait_ge(pe_done, at("pe", "gdn", "proj", h, u))
            if h:
                dve.wait_ge(act_done, at("act", "gdn", "silu", h - 1, u))
            conv(dve, G[("cq", "ck", "cv")[u]], B[u % 2], lambda m: gconv[:, u * GH + h, m:m + 1], 4)\
                .then_inc(dve_done, DV.tick("gdn", "conv", h, u))

        def dve_gdn(dve):
            begin(dve, "dve", "gdn")
            dve_mod(dve, 0, 0, 16, 3)
            dve.wait_ge(dve_done, DV.n)
            for n in range(KC):
                last = nc.vector.tensor_scalar(HT[:, n, :], XT[:, n, :], mod1[:, 0, 8 + n:9 + n], mod[:, 0, n:n + 1], ALU.mult, ALU.add)
            last.then_inc(dve_done, DV.tick("gdn", "input"))
            nc.vector.memset(reset[0:GH, :], 1.0).then_inc(dve_done, DV.tick())
            nc.vector.memset(ROWS, 0.0).then_inc(dve_done, DV.tick("gdn", "zeros"))
            dve.wait_ge(dve_done, DV.n)
            nc.vector.memset(reset[0:GH, 0::P], 0.0).then_inc(dve_done, DV.tick())
            dve.wait_ge(act_done, at("act", "gdn", "softplus"))
            nc.vector.tensor_scalar(small[0:GH, 41:42], small[0:GH, 40:41], -1.0, None, ALU.mult).then_inc(dve_done, DV.tick())
            nc.vector.tensor_tensor(G["s1"][0:GH, :], G["s1"][0:GH, :], G["s2"][0:GH, :], ALU.add).then_inc(dve_done, DV.tick())
            dve.wait_ge(dve_done, DV.n)
            nc.vector.tensor_scalar(G["s1"][0:GH, :], G["s1"][0:GH, :], small[0:GH, 41:42], None, ALU.mult).then_inc(dve_done, DV.tick())
            dve.wait_ge(dve_done, DV.n)
            nc.vector.tensor_tensor_scan(ROWS[0:GH, :], reset[0:GH, :], G["s1"][0:GH, :], 0.0, ALU.mult, ALU.add)\
                .then_inc(dve_done, DV.tick())
            dve.wait_ge(dve_done, DV.n)
            rows4 = ROWS[0:GH, :].rearrange("p (i c) -> p i c", c=P)
            nc.vector.tensor_tensor(G["r14"][0:GH, :, :], rows4[:, :, P - 1:P].to_broadcast([GH, NT, P]), rows4, ALU.subtract)\
                .then_inc(dve_done, DV.tick("gdn", "gc"))
            DV.mark("gdn", "rows")
            dve_conv4(dve, 0, 0)
            dve_conv4(dve, 0, 1)
            dve.wait_ge(pe_done, at("pe", "gdn", "cols"))
            nc.vector.tensor_copy(COLS[:, :, :], B4[3]).then_inc(dve_done, DV.tick())
            dve.wait_ge(pe_done, at("pe", "gdn", "eglb"))
            nc.vector.tensor_copy(small[:, 8:40], B[4][:, 0:32]).then_inc(dve_done, DV.tick("gdn", "eglb"))
            dve.wait_ge(dve_done, DV.n)
            nc.vector.tensor_tensor(COLS[:, :, 40:48], COLS[:, :, 32:40], COLS[:, :, 64:72], ALU.mult).then_inc(dve_done, DV.tick())
            dve_conv4(dve, 0, 2)

            for h in range(GH):
                gcc = COLS[:, :, h:h + 1]
                beta, bg, el = COLS[:, :, 32 + h:33 + h], COLS[:, :, 40 + h:41 + h], COLS[:, :, 96 + h:97 + h]
                dve.wait_ge(pe_done, at("pe", "gdn", "gcb", h))
                dve.wait_ge(act_done, at("act", "gdn", "eg", h))
                for i in range(NT):
                    nc.vector.tensor_scalar(G["dp4"][:, i, :], B4[4][:, i, :], gcc[:, i, :], 0.0, ALU.subtract, ALU.max)
                    last = nc.vector.tensor_scalar(G["dn4"][:, i, :], B4[4][:, i, :], gcc[:, i, :], 0.0, ALU.subtract, ALU.min)
                last.then_inc(dve_done, DV.tick("gdn", "diff", h))
                nc.vector.reciprocal(G["r2"], G["r2"]).then_inc(dve_done, DV.tick())
                dve.wait_ge(dve_done, DV.n)
                nc.vector.tensor_tensor(G["ks"], G["ks"], G["r2"], ALU.mult).then_inc(dve_done, DV.tick())
                nc.vector.reciprocal(G["r1"], G["r1"]).then_inc(dve_done, DV.tick())
                dve.wait_ge(dve_done, DV.n)
                nc.vector.scalar_tensor_tensor(out=G["qs"], in0=G["qs"], scalar=float(P) ** -0.5, in1=G["r1"], op0=ALU.mult, op1=ALU.mult)\
                    .then_inc(dve_done, DV.tick("gdn", "khat", h))
                dve.wait_ge(pe_done, at("pe", "gdn", "vtok", h))
                for i in range(NT):
                    last = nc.vector.tensor_scalar(G["vb4"][:, i, :], B4[2][:, i, :], beta[:, i, :], None, ALU.mult)
                dve.wait_ge(pe_done, at("pe", "gdn", "ktok", h))
                for i in range(NT):
                    nc.vector.tensor_scalar(G["kb4"][:, i, :], B4[3][:, i, :], bg[:, i, :], None, ALU.mult)
                    last = nc.vector.tensor_scalar(G["kd4"][:, i, :], B4[3][:, i, :], el[:, i, :], None, ALU.mult)
                last.then_inc(dve_done, DV.tick())
                dve.wait_ge(pool_done, at("pool", "gdn", "decay", h))
                dve.wait_ge(pe_done, at("pe", "gdn", "kk", h))
                for i in range(NT):
                    last = nc.vector.scalar_tensor_tensor(out=G["L4"][:, i, :], in0=B4[5][:, i, :], scalar=beta[:, i, :],
                                                          in1=G["dp4"][:, i, :], op0=ALU.mult, op1=ALU.mult)
                last.then_inc(dve_done, DV.tick("gdn", "L", h))
                dve.wait_ge(pe_done, at("pe", "gdn", "qk", h))
                nc.vector.tensor_tensor(G["QK"], B[6][:, :], G["dn"], ALU.mult).then_inc(dve_done, DV.tick())

                def level(mask, l):
                    return mask[:, l:l + 1, :].to_broadcast([P, NT, P])

                idb = ident[:, :].rearrange("p (a c) -> p a c", a=1).to_broadcast([P, NT, P])
                dve.wait_ge(dve_done, DV.n)
                nc.vector.tensor_tensor(G["D4"], G["L4"], level(maskL, 0), ALU.mult).then_inc(dve_done, DV.tick())
                dve.wait_ge(dve_done, DV.n)
                nc.vector.tensor_tensor(G["D4"], idb, G["D4"], ALU.subtract).then_inc(dve_done, DV.tick())
                dve.wait_ge(act_done, at("act", "gdn", "LT", h))
                nc.vector.tensor_tensor(G["E4"], G["LT4"], level(maskU, 0), ALU.mult).then_inc(dve_done, DV.tick())
                dve.wait_ge(dve_done, DV.n)
                nc.vector.tensor_tensor(G["E4"], idb, G["E4"], ALU.subtract).then_inc(dve_done, DV.tick("gdn", "inv", h, 0))
                for l in range(1, 7):
                    dve.wait_ge(pe_done, at("pe", "gdn", "LD", h, l))
                    nc.vector.tensor_tensor(G["Tm4"], B4[5], level(maskL, l), ALU.mult).then_inc(dve_done, DV.tick("gdn", "Tm", h, l))
                    if l < 6:
                        dve.wait_ge(pe_done, at("pe", "gdn", "DT", h, l))
                        nc.vector.tensor_tensor(G["D"], G["D"], B[6][:, :], ALU.subtract).then_inc(dve_done, DV.tick())
                    dve.wait_ge(pe_done, at("pe", "gdn", "TE", h, l))
                    nc.vector.tensor_tensor(G["E"], G["E"], B[4][:, :], ALU.subtract).then_inc(dve_done, DV.tick("gdn", "inv", h, l))
                    if l % 2 == 1 and h + 1 < GH:
                        if l == 1:
                            dve_conv4(dve, h + 1, 0)
                        if l == 3:
                            dve_conv4(dve, h + 1, 1)
                        if l == 5:
                            dve_conv4(dve, h + 1, 2)
                dve.wait_ge(act_done, at("act", "gdn", "UW", h))
                for i in range(NT):
                    if i == 0:
                        nc.vector.tensor_copy(gdn_vn[:, 0, :], G["U4"][:, 0, :]).then_inc(dve_done, DV.tick("gdn", "vn", h, 0))
                    else:
                        dve.wait_ge(pe_done, at("pe", "gdn", "wS", h, i))
                        nc.vector.tensor_tensor(gdn_vn[:, i % 2, :], G["U4"][:, i, :], B[2][:, 0:P], ALU.subtract)\
                            .then_inc(dve_done, DV.tick("gdn", "vn", h, i))
                    if i < NT - 1:
                        dve.wait_ge(pe_done, at("pe", "gdn", "kv", h, i))
                        if i == 0:
                            nc.vector.tensor_copy(gdn_S[:, 0, :], B[5][:, 0:P]).then_inc(dve_done, DV.tick("gdn", "S", h, 0))
                        else:
                            dve.wait_ge(dve_done, at("dve", "gdn", "S", h, i - 1))
                            nc.vector.scalar_tensor_tensor(out=gdn_S[:, i % 2, :], in0=gdn_S[:, (i - 1) % 2, :], scalar=EGLB[:, h, i:i + 1],
                                                           in1=B[5][:, 0:P], op0=ALU.mult, op1=ALU.add)\
                                .then_inc(dve_done, DV.tick("gdn", "S", h, i))
                dve.wait_ge(act_done, at("act", "gdn", "ostd", h))
                nc.vector.reciprocal(G["r1"], G["r1"]).then_inc(dve_done, DV.tick())
                dve.wait_ge(dve_done, DV.n)
                nc.vector.scalar_tensor_tensor(out=OT_g[:, h, :], in0=B[3][:, :], scalar=gvec[:, 0:1], in1=G["r1"], op0=ALU.mult, op1=ALU.mult)\
                    .then_inc(dve_done, DV.tick())
                dve.wait_ge(dve_done, DV.n)
                nc.vector.tensor_tensor(OT_g[:, h, :], OT_g[:, h, :], G["zs"], ALU.mult).then_inc(dve_done, DV.tick("gdn", "out", h))
            dve_mod(dve, 0, 16, 48, 11)
            DV.mark("end", "gdn")

        def pool_gdn(pool):
            begin(pool, "pool", "gdn")
            for h in range(GH):
                pool.wait_ge(act_done, at("act", "gdn", "decay", h))
                nc.gpsimd.tensor_tensor(G["dp4"], G["dp4"], causal[:, 0:1, :].to_broadcast([P, NT, P]), ALU.mult)
                nc.gpsimd.tensor_tensor(G["dn4"], G["dn4"], causal[:, 1:2, :].to_broadcast([P, NT, P]), ALU.mult)\
                    .then_inc(pool_done, PO.tick("gdn", "decay", h))
                pool.wait_ge(dve_done, at("dve", "gdn", "khat", h))
                nc.gpsimd.tensor_tensor(G["qe"], G["qs"], G["eg"], ALU.mult).then_inc(pool_done, PO.tick("gdn", "qe", h))
            PO.mark("end", "gdn")

        OT_r = region(0, 16, T)
        o = 16 * T
        R = {}
        for name in ("q1", "q2", "k1", "k2", "ta", "tb", "tc", "td", "sq0", "sq1", "rs"):
            R[name] = region(o, T); o += T
        ret_V = region(o, NT, RDV); o += NT * RDV
        ret_G = region(o, 4, T); o += 4 * T
        ret_P = region(o, NT, T); o += NT * T
        ret_cos = region(o, T); o += T
        ret_sin = region(o, T); o += T
        ret_D = region(o, 1, T); o += T
        assert o <= 21504

        def pe_ret(pe):
            begin(pe, "pe", "ret")

            def qk(h):
                X = 4 * (h % 2)
                w = units(pe, ("ret_qk", h))
                if h:
                    pe.wait_ge(act_done, at("act", "ret", "gate", h - 1, 3))
                for u in range(4):
                    for k in range(KC):
                        last = nc.tensor.matmul(B[X + u][:, :], w[:, u, k, :], HT[:, k, :], start=(k == 0), stop=(k == KC - 1))
                    last.then_inc(pe_done, PE.tick("ret", "qk", h, u))
                used(("ret_qk", h))

            qk(0)
            for h in range(RH):
                X, Y = 4 * (h % 2), 4 - 4 * (h % 2)
                w = slot_of(pe, ("ret_v", h)).rearrange("p (k n) -> p k n", k=KC)
                if h:
                    pe.wait_ge(act_done, at("act", "ret", "std", h - 1))
                for i in range(NT):
                    for k in range(KC):
                        last = nc.tensor.matmul(B[Y + i][:, :], HT[:, k, i * P:(i + 1) * P], w[:, k, :], start=(k == 0), stop=(k == KC - 1))
                    last.then_inc(pe_done, PE.tick("ret", "v", h, i))
                used(("ret_v", h))
                pe.wait_ge(pool_done, at("pool", "ret", "rope", h))
                for j in range(NT):
                    for c, (kk, qq) in enumerate((("k1", "q1"), ("k2", "q2"))):
                        last = nc.tensor.matmul(B[X + j][:, 0:T - j * P], R[kk][:, j * P:(j + 1) * P], R[qq][:, j * P:T],
                                                start=(c == 0), stop=(c == 1))
                    last.then_inc(pe_done, PE.tick("ret", "score", h, j))
                w = units(pe, ("ret_g", h))
                for u in range(4):
                    pe.wait_ge(act_done, at("act", "ret", "v", h, u))
                    for k in range(KC):
                        last = nc.tensor.matmul(B[Y + u][:, :], w[:, u, k, :], HT[:, k, :], start=(k == 0), stop=(k == KC - 1))
                    last.then_inc(pe_done, PE.tick("ret", "gate", h, u))
                used(("ret_g", h))
                pe.wait_ge(dve_done, at("dve", "ret", "p", h, 3))
                for c in range(4):
                    for j in range(NT):
                        last = nc.tensor.matmul(B[X + c][:, j * P:T], ret_V[:, j, c * P:(c + 1) * P], ret_P[:, j, 0:T - j * P],
                                                start=(j == 0), stop=(j == NT - 1))
                    last.then_inc(pe_done, PE.tick("ret", "o", h, c))
                if h + 1 < RH:
                    qk(h + 1)
                for c in range(4):
                    pe.wait_ge(act_done, at("act", "ret", "o", h, 3))
                    last = nc.tensor.matmul(B[X][:, :], ones[:, 2, :], OT_r[:, 4 * h + c, :], start=(c == 0), stop=(c == 3))
                last.then_inc(pe_done, PE.tick("ret", "mean", h))
                for c in range(4):
                    pe.wait_ge(act_done, at("act", "ret", "sq", h, c))
                    last = nc.tensor.matmul(B[X + 1][:, :], ones[:, 2, :], R[f"sq{c % 2}"], start=(c == 0), stop=(c == 3))
                    last.then_inc(pe_done, PE.tick("ret", "var", h, c))
            PE.mark("end", "ret")

        def dve_ret(dve):
            begin(dve, "dve", "ret")
            dve.wait_ge(ret_tables_in, 32)
            for h in range(RH):
                X = 4 * (h % 2)
                for n, dsts in ((0, ("ta", "tb")), (2, ("tc", "td"))):
                    if h:
                        dve.wait_ge(pool_done, at("pool", "ret", "rope", h - 1))
                    if n:
                        dve.wait_ge(pool_done, at("pool", "ret", "ropeq", h))
                    dve.wait_ge(pe_done, at("pe", "ret", "qk", h, n))
                    nc.vector.tensor_tensor(R["ta"], B[X + n][:, :], ret_cos, ALU.mult)
                    nc.vector.tensor_tensor(R["tb"], B[X + n][:, :], ret_sin, ALU.mult)
                    dve.wait_ge(pe_done, at("pe", "ret", "qk", h, n + 1))
                    nc.vector.tensor_tensor(R["tc"], B[X + n + 1][:, :], ret_sin, ALU.mult)
                    nc.vector.tensor_tensor(R["td"], B[X + n + 1][:, :], ret_cos, ALU.mult)\
                        .then_inc(dve_done, DV.tick("ret", "rope", h, n))
                dve.wait_ge(ret_tables_in, 48 + 16 * h)
                for j in range(NT):
                    dve.wait_ge(pe_done, at("pe", "ret", "score", h, j))
                    if h and j == 0:
                        dve.wait_ge(pe_done, at("pe", "ret", "o", h - 1, 3))
                    nc.vector.tensor_tensor(ret_P[:, j, 0:T - j * P], B[X + j][:, 0:T - j * P], ret_D[:, 0, 0:T - j * P], ALU.mult)\
                        .then_inc(dve_done, DV.tick("ret", "p", h, j))
                dve.wait_ge(pe_done, at("pe", "ret", "mean", h))
                for c in range(4):
                    nc.vector.tensor_tensor(OT_r[:, 4 * h + c, :], OT_r[:, 4 * h + c, :], B[X][:, :], ALU.subtract)\
                        .then_inc(dve_done, DV.tick("ret", "centred", h, c))
                dve.wait_ge(act_done, at("act", "ret", "std", h))
                nc.vector.reciprocal(R["rs"], R["rs"]).then_inc(dve_done, DV.tick())
                dve.wait_ge(dve_done, DV.n)
                for c in range(4):
                    nc.vector.tensor_tensor(OT_r[:, 4 * h + c, :], OT_r[:, 4 * h + c, :], R["rs"], ALU.mult).then_inc(dve_done, DV.tick())
                dve.wait_ge(dve_done, DV.n)
                for c in range(4):
                    last = nc.vector.tensor_tensor(OT_r[:, 4 * h + c, :], OT_r[:, 4 * h + c, :], ret_G[:, c, :], ALU.mult)
                last.then_inc(dve_done, DV.tick("ret", "out", h))
            DV.mark("end", "ret")

        def pool_ret(pool):
            begin(pool, "pool", "ret")
            for h in range(RH):
                for n, a, b in ((0, "q1", "q2"), (2, "k1", "k2")):
                    pool.wait_ge(dve_done, at("dve", "ret", "rope", h, n))
                    if h and n == 0:
                        pool.wait_ge(pe_done, at("pe", "ret", "score", h - 1, 3))
                    nc.gpsimd.tensor_tensor(R[a], R["ta"], R["tc"], ALU.subtract)
                    nc.gpsimd.tensor_tensor(R[b], R["tb"], R["td"], ALU.add)\
                        .then_inc(pool_done, PO.tick("ret", "ropeq" if n == 0 else "rope", h))
            PO.mark("end", "ret")

        def act_ret(act):
            begin(act, "act", "ret")
            act.dma_start(ret_cos, dr["ret_cos"]).then_inc(ret_tables_in, 16)
            act.dma_start(ret_sin, dr["ret_sin"]).then_inc(ret_tables_in, 16)
            for h in range(RH):
                X, Y = 4 * (h % 2), 4 - 4 * (h % 2)
                if h:
                    act.wait_ge(dve_done, at("dve", "ret", "p", h - 1, 3))
                act.wait_ge(ret_tables_in, 32 + 16 * h)
                act.dma_start(ret_D[:, 0, :], dr["ret_D"][h]).then_inc(ret_tables_in, 16)
                for i in range(NT):
                    act.wait_ge(pe_done, at("pe", "ret", "v", h, i))
                    nc.scalar.activation(ret_V[:, i, :], B[Y + i][:, :], ACT.Copy).then_inc(act_done, AC.tick("ret", "v", h, i))
                for u in range(4):
                    act.wait_ge(pe_done, at("pe", "ret", "gate", h, u))
                    if h and u == 0:
                        act.wait_ge(dve_done, at("dve", "ret", "out", h - 1))
                    nc.scalar.activation(ret_G[:, u, :], B[Y + u][:, :], ACT.Silu).then_inc(act_done, AC.tick("ret", "gate", h, u))
                for c in range(4):
                    act.wait_ge(pe_done, at("pe", "ret", "o", h, c))
                    nc.scalar.activation(OT_r[:, 4 * h + c, :], B[X + c][:, :], ACT.Copy).then_inc(act_done, AC.tick("ret", "o", h, c))
                for c in range(4):
                    act.wait_ge(dve_done, at("dve", "ret", "centred", h, c))
                    if c >= 2:
                        act.wait_ge(pe_done, at("pe", "ret", "var", h, c - 2))
                    nc.scalar.activation(R[f"sq{c % 2}"], OT_r[:, 4 * h + c, :], ACT.Square).then_inc(act_done, AC.tick("ret", "sq", h, c))
                act.wait_ge(pe_done, at("pe", "ret", "var", h, 3))
                nc.scalar.activation(R["rs"], B[X + 1][:, :], ACT.Sqrt, bias=gvec[:, 5:6]).then_inc(act_done, AC.tick("ret", "std", h))
            AC.mark("end", "ret")

        o = 0
        QH = region(o, HH, T); o += HH * T
        KH = region(o, HH, T); o += HH * T
        BH = region(o, HH, T); o += HH * T
        GH_ = region(o, HH, T); o += HH * T
        NX = region(o, 8, T); o += 8 * T
        HI = region(o, NT, T); o += NT * T
        VSW = region(o, NT, 280); o += NT * 280
        COSF = region(o, T); o += T
        SINF = region(o, T); o += T
        work = o
        assert work + 5024 <= 21504
        angle = [region(work + n * T, T) for n in range(4)]
        hreset = region(work + 4 * T, T)

        def pe_mix(pe):
            begin(pe, "pe", "mix")
            for h in range(HH):
                w = units(pe, ("mix", h))
                X = 4 * (h % 2)
                for u in range(4):
                    if h >= 2:
                        pe.wait_ge(act_done, at("act", "mix", "taken", h - 2, u))
                    for k in range(KC):
                        last = nc.tensor.matmul(B[X + u][:, :], w[:, u, k, :], HT[:, k, :], start=(k == 0), stop=(k == KC - 1))
                    last.then_inc(pe_done, PE.tick("mix", "proj", h, u))
                used(("mix", h))
            w = slot_of(pe, ("mix_hi", 0)).rearrange("p (k n) -> p k n", k=KC)
            for i in range(NT):
                pe.wait_ge(act_done, at("act", "mix", "taken", 2, i))
                for k in range(KC):
                    last = nc.tensor.matmul(B[i][:, :], HT[:, k, i * P:(i + 1) * P], w[:, k, :], start=(k == 0), stop=(k == KC - 1))
                last.then_inc(pe_done, PE.tick("mix", "hi", i))
            used(("mix_hi", 0))
            w = units(pe, ("mix_c", 0))
            for u in range(4):
                pe.wait_ge(act_done, at("act", "mix", "taken", 3, u))
                for k in range(KC):
                    last = nc.tensor.matmul(B[4 + u][:, :], w[:, u, k, :], HT[:, k, :], start=(k == 0), stop=(k == KC - 1))
                last.then_inc(pe_done, PE.tick("mix", "c", u))
            used(("mix_c", 0))
            w = slot_of(pe, ("mix_v", 0))[:, 0:KC * 280].rearrange("p (k n) -> p k n", k=KC)
            for i in range(NT):
                pe.wait_ge(act_done, at("act", "mix", "hi", i))
                for k in range(KC):
                    last = nc.tensor.matmul(B[i][:, 0:280], HT[:, k, i * P:(i + 1) * P], w[:, k, :], start=(k == 0), stop=(k == KC - 1))
                last.then_inc(pe_done, PE.tick("mix", "v", i))
            used(("mix_v", 0))
            PE.mark("end", "mix")

        def act_mix(act):
            begin(act, "act", "mix")
            act.dma_start(angle[0].bitcast(I32), dr["pos"]).then_inc(nsa_tables_in, 16)
            for h in range(HH):
                X = 4 * (h % 2)
                act.wait_ge(pe_done, at("pe", "mix", "proj", h, 3))
                nc.scalar.activation(QH[:, h, :], B[X][:, :], ACT.Silu).then_inc(act_done, AC.tick("mix", "taken", h, 0))
                nc.scalar.activation(GH_[:, h, :], B[X + 2][:, :], ACT.Silu).then_inc(act_done, AC.tick("mix", "taken", h, 2))
                nc.scalar.activation(NX[:, h, :], B[X + 3][:, :], ACT.Copy).then_inc(act_done, AC.tick("mix", "taken", h, 3))
                nc.scalar.activation(BH[:, h, :], B[X + 1][:, :], ACT.Sigmoid).then_inc(act_done, AC.tick())
                nc.scalar.activation(KH[:, h, :], B[X + 1][:, :], ACT.Sigmoid, scale=-1.0).then_inc(act_done, AC.tick("mix", "taken", h, 1))
            for i in range(NT):
                act.wait_ge(pe_done, at("pe", "mix", "hi", i))
                nc.scalar.activation(HI[:, i, :], B[i][:, :], ACT.Copy).then_inc(act_done, AC.tick("mix", "hi", i))
            for u in range(4):
                act.wait_ge(pe_done, at("pe", "mix", "c", u))
                nc.scalar.activation(NX[:, 4 + u, :], B[4 + u][:, :], ACT.Copy).then_inc(act_done, AC.tick("mix", "c", u))
            for i in range(NT):
                act.wait_ge(pe_done, at("pe", "mix", "v", i))
                nc.scalar.activation(VSW[:, i, :], B[i][:, 0:280], ACT.Copy).then_inc(act_done, AC.tick())
            act.wait_ge(act_done, AC.n)
            nc.scalar.activation(VSW[:, :, 256:280], VSW[:, :, 256:280], ACT.Sigmoid).then_inc(act_done, AC.tick())
            act.wait_ge(dve_done, at("dve", "mix", "f"))
            nc.scalar.activation(BH[:, :, :], BH[:, :, :], ACT.Ln).then_inc(act_done, AC.tick("mix", "logf"))
            act.wait_ge(dve_done, at("dve", "mix", "angles"))
            nc.scalar.activation(SINF, angle[1], ACT.Sin).then_inc(act_done, AC.tick())
            nc.scalar.activation(COSF, angle[2], ACT.Sin).then_inc(act_done, AC.tick())
            AC.mark("end", "mix")

        def dve_mix(dve):
            begin(dve, "dve", "mix")

            def step(ins):
                ins.then_inc(dve_done, DV.tick())
                dve.wait_ge(dve_done, DV.n)

            mx, e0, e1 = small[:, 0:4], small[:, 4:8], small[:, 8:12]
            dve.wait_ge(act_done, at("act", "bounds"))
            step(nc.vector.tensor_tensor(mx, e0, e1, ALU.add))
            step(nc.vector.reciprocal(mx, mx))
            nc.vector.tensor_tensor(e0, e0, mx, ALU.mult)
            step(nc.vector.tensor_tensor(e1, e1, mx, ALU.mult))
            dve.wait_ge(nsa_tables_in, 16)
            step(nc.vector.tensor_copy(angle[1], angle[0].bitcast(I32)))
            step(nc.vector.tensor_scalar(angle[1], angle[1], gvec[:, 6:7], None, ALU.mult))
            step(nc.vector.tensor_scalar(angle[2], angle[1], 1.0 / (2.0 * np.pi), MAGIC, ALU.mult, ALU.add))
            step(nc.vector.tensor_scalar(angle[2], angle[2], MAGIC, None, ALU.subtract))
            for c in TWO_PI:
                step(nc.vector.scalar_tensor_tensor(out=angle[1], in0=angle[2], scalar=-c, in1=angle[1], op0=ALU.mult, op1=ALU.add))
            pi = 3.1415925
            step(nc.vector.tensor_scalar(angle[2], angle[1], np.pi / 2, None, ALU.add))
            step(nc.vector.tensor_scalar(angle[3], angle[2], pi, -2.0 * np.pi, ALU.is_gt, ALU.mult))
            step(nc.vector.tensor_tensor(angle[2], angle[2], angle[3], ALU.add))
            step(nc.vector.tensor_scalar(angle[2], angle[2], pi, -pi, ALU.min, ALU.max))
            step(nc.vector.tensor_scalar(angle[1], angle[1], pi, -pi, ALU.min, ALU.max))
            DV.mark("mix", "angles")
            nc.vector.memset(hreset, 1.0).then_inc(dve_done, DV.tick())
            dve.wait_ge(dve_done, DV.n)
            nc.vector.memset(hreset[:, 0::P], 0.0).then_inc(dve_done, DV.tick())
            for h in range(HH):
                dve.wait_ge(act_done, at("act", "mix", "taken", h, 1))
                nc.vector.tensor_scalar(BH[:, h, :], BH[:, h, :], e1[:, h:h + 1], e0[:, h:h + 1], ALU.mult, ALU.add)
                nc.vector.tensor_scalar(KH[:, h, :], KH[:, h, :], e1[:, h:h + 1], None, ALU.mult).then_inc(dve_done, DV.tick("mix", "f"))
            dve.wait_ge(act_done, at("act", "mix", "logf"))
            dve.wait_ge(dve_done, DV.n)
            for h in range(HH):
                nc.vector.tensor_tensor_scan(NXT_B[:, h, :], hreset, BH[:, h, :], 0.0, ALU.mult, ALU.add).then_inc(dve_done, DV.tick())
            DV.mark("end", "mix")

        NXT_B = BH
        hgb = {n: region(work + m * T, T) for m, n in enumerate(("D0", "D1", "P0", "P1", "AT", "QE", "KD", "QL", "KL"))}
        hgS = region(work + 9 * T, 2, P)
        TASKS = [("diag", i) for i in range(8)] + [("level", l) for l in (3, 4, 5, 6)] + [("qe", 0), ("kd", 0)]
        NTASK = len(TASKS)

        def halves(v, l):
            w = v.rearrange("p (b a s) -> p b a s", a=2, s=LEVELS[l])
            return w[:, :, 0, :], w[:, :, 1, :]

        def tiles(v):
            return v.rearrange("p (i c) -> p i c", c=P)

        def pe_hg(pe):
            begin(pe, "pe", "hg")
            for h in range(HH):
                for t, (kind, x) in enumerate(TASKS):
                    if kind == "diag":
                        pe.wait_ge(pool_done, at("pool", "hg", "k", h, t))
                        if h and t == 0:
                            pe.wait_ge(dve_done, at("dve", "hg", "AT", h - 1))
                        nc.tensor.matmul(B[0][:, :], comb[:, 8 - x:8 - x + P], hgb[f"P{t % 2}"], start=(x == 0), stop=(x == 7))\
                            .then_inc(pe_done, PE.tick("hg", "task", h, t))
                    elif kind == "level":
                        pe.wait_ge(pool_done, at("pool", "hg", "k", h, t))
                        pe.wait_ge(dve_done, at("dve", "hg", "q", h, t))
                        ql, kl = tiles(hgb["QL"]), tiles(hgb["KL"])
                        for i in range(NT):
                            last = nc.tensor.matmul(B4[1 + x % 2][:, i, :], kl[:, i, :], ql[:, i, :], start=True, stop=True)
                        last.then_inc(pe_done, PE.tick("hg", "task", h, t))
                    elif kind == "kd":
                        pe.wait_ge(dve_done, at("dve", "hg", "q", h, t))
                        for i in range(NT):
                            last = nc.tensor.transpose(B4[3][:, i, :], tiles(hgb[f"P{t % 2}"])[:, i, :], ident[:, :])
                        last.then_inc(pe_done, PE.tick("hg", "task", h, t))
                pe.wait_ge(act_done, at("act", "hg", "kd", h))
                for i in range(NT):
                    hv = HI[:, i, h * P:(h + 1) * P]
                    if i < NT - 1:
                        if i:
                            pe.wait_ge(dve_done, at("dve", "hg", "S", h, i - 1))
                        nc.tensor.matmul(B[5][:, 0:P], tiles(hgb["KD"])[:, i, :], hv, start=True, stop=True)\
                            .then_inc(pe_done, PE.tick("hg", "kv", h, i))
                    nc.tensor.matmul(B4[4][:, i, :], hv, tiles(hgb["AT"])[:, i, :], start=True, stop=(i == 0))
                    if i:
                        pe.wait_ge(dve_done, at("dve", "hg", "S", h, i - 1))
                        last = nc.tensor.matmul(B4[4][:, i, :], hgS[:, (i - 1) % 2, :], tiles(hgb["QE"])[:, i, :], start=False, stop=True)
                last.then_inc(pe_done, PE.tick("hg", "o", h))
                pe.wait_ge(act_done, at("act", "hg", "osq", h))
                nc.tensor.matmul(B[6][:, :], ones[:, 3, :], hgb["P0"], start=True, stop=True).then_inc(pe_done, PE.tick("hg", "oss", h))
            PE.mark("end", "hg")

        def dve_hg(dve):
            begin(dve, "dve", "hg")
            nc.vector.memset(hgb["QL"], 0.0).then_inc(dve_done, DV.tick())
            nc.vector.memset(hgb["KL"], 0.0).then_inc(dve_done, DV.tick("hg", "zeros"))
            for h in range(HH):
                b, q, k = BH[:, h, :], QH[:, h, :], KH[:, h, :]

                def diff(t):
                    kind, x = TASKS[t]
                    d = hgb[f"D{t % 2}"]
                    if t >= 2:
                        dve.wait_ge(pool_done, at("pool", "hg", "k", h, min(t - 2, 11)))
                    if kind == "diag":
                        b8 = b.rearrange("p (n e) -> p n e", e=8)
                        ins = nc.vector.tensor_tensor(d.rearrange("p (n e) -> p n e", e=8), b8, b8[:, :, x:x + 1].to_broadcast([P, T // 8, 8]),
                                                      ALU.subtract)
                    elif kind == "level":
                        s = LEVELS[x]
                        lo, up = halves(b, x)
                        dlo, dup = halves(d, x)
                        ref = lo[:, :, s - 1:s].to_broadcast([P, T // (2 * s), s])
                        nc.vector.tensor_tensor(dlo, ref, lo, ALU.subtract)
                        ins = nc.vector.tensor_tensor(dup, up, ref, ALU.subtract)
                    elif kind == "qe":
                        ins = nc.vector.tensor_copy(d, b)
                    else:
                        b4 = tiles(b)
                        ins = nc.vector.tensor_tensor(tiles(d), b4[:, :, P - 1:P].to_broadcast([P, NT, P]), b4, ALU.subtract)
                    ins.then_inc(dve_done, DV.tick("hg", "diff", h, t))

                def accumulate(t):
                    x = TASKS[t][1]
                    dve.wait_ge(pe_done, at("pe", "hg", "task", h, t))
                    nc.vector.tensor_tensor(tiles(hgb["KD"]), B4[1 + x % 2], maskU[:, x:x + 1, :].to_broadcast([P, NT, P]), ALU.mult)\
                        .then_inc(dve_done, DV.tick())
                    dve.wait_ge(dve_done, DV.n)
                    nc.vector.tensor_tensor(hgb["AT"], hgb["AT"], hgb["KD"], ALU.add).then_inc(dve_done, DV.tick("hg", "acc", h, t))

                if h:
                    dve.wait_ge(act_done, at("act", "hg", "ostd", h - 1))
                diff(0)
                for t, (kind, x) in enumerate(TASKS):
                    d = hgb[f"D{t % 2}"]
                    if t + 1 < NTASK:
                        diff(t + 1)
                    dve.wait_ge(act_done, at("act", "hg", "exp", h, t))
                    if kind == "diag":
                        if t >= 2:
                            dve.wait_ge(pe_done, at("pe", "hg", "task", h, t - 2))
                        elif h:
                            dve.wait_ge(pe_done, at("pe", "hg", "oss", h - 1))
                        ins = nc.vector.scalar_tensor_tensor(out=hgb[f"P{t % 2}"], in0=d, scalar=1.0, in1=q, op0=ALU.min, op1=ALU.mult)
                    elif kind == "level":
                        if x > 3:
                            dve.wait_ge(pe_done, at("pe", "hg", "task", h, t - 1))
                        ins = nc.vector.tensor_tensor(halves(hgb["QL"], x)[1], halves(d, x)[1], halves(q, x)[1], ALU.mult)
                    elif kind == "qe":
                        ins = nc.vector.tensor_tensor(hgb["QE"], d, q, ALU.mult)
                    else:
                        ins = nc.vector.tensor_tensor(hgb[f"P{t % 2}"], d, k, ALU.mult)
                    ins.then_inc(dve_done, DV.tick("hg", "q", h, t))
                    if t == 8:
                        dve.wait_ge(pe_done, at("pe", "hg", "task", h, 7))
                        nc.vector.tensor_tensor(tiles(hgb["AT"]), B4[0], causal[:, 3:4, :].to_broadcast([P, NT, P]), ALU.mult)\
                            .then_inc(dve_done, DV.tick("hg", "AT", h))
                        dve.wait_ge(dve_done, DV.n)
                    if t > 8 and t <= 12:
                        accumulate(t - 1)
                        dve.wait_ge(dve_done, DV.n)
                for i in range(NT - 1):
                    dve.wait_ge(pe_done, at("pe", "hg", "kv", h, i))
                    if i == 0:
                        ins = nc.vector.tensor_copy(hgS[:, 0, :], B[5][:, 0:P])
                    else:
                        dve.wait_ge(dve_done, DV.n)
                        ins = nc.vector.scalar_tensor_tensor(out=hgS[:, i % 2, :], in0=hgS[:, (i - 1) % 2, :], scalar=small[:, 16 + i:17 + i],
                                                             in1=B[5][:, 0:P], op0=ALU.mult, op1=ALU.add)
                    ins.then_inc(dve_done, DV.tick("hg", "S", h, i))
                dve.wait_ge(act_done, at("act", "hg", "ostd", h))
                nc.vector.reciprocal(hgb["D0"], hgb["D0"]).then_inc(dve_done, DV.tick())
                dve.wait_ge(dve_done, DV.n)
                nc.vector.scalar_tensor_tensor(out=HT[:, h, :], in0=B[4][:, :], scalar=gvec[:, 7:8], in1=hgb["D0"], op0=ALU.mult, op1=ALU.mult)\
                    .then_inc(dve_done, DV.tick())
                dve.wait_ge(dve_done, DV.n)
                nc.vector.tensor_tensor(HT[:, h, :], HT[:, h, :], GH_[:, h, :], ALU.mult).then_inc(dve_done, DV.tick("hg", "out", h))
            DV.mark("end", "hg")

        def pool_hg(pool):
            begin(pool, "pool", "hg")
            pool.wait_ge(dve_done, at("dve", "hg", "zeros"))
            for h in range(HH):
                k = KH[:, h, :]
                for t, (kind, x) in enumerate(TASKS[:12]):
                    pool.wait_ge(dve_done, at("dve", "hg", "q", h, t))
                    if kind == "diag":
                        p8 = hgb[f"P{t % 2}"].rearrange("p (n e) -> p n e", e=8)
                        k8 = k.rearrange("p (n e) -> p n e", e=8)
                        ins = nc.gpsimd.tensor_tensor(p8, p8, k8[:, :, x:x + 1].to_broadcast([P, T // 8, 8]), ALU.mult)
                    else:
                        ins = nc.gpsimd.tensor_tensor(halves(hgb["KL"], x)[0], halves(hgb[f"D{t % 2}"], x)[0], halves(k, x)[0], ALU.mult)
                    ins.then_inc(pool_done, PO.tick("hg", "k", h, t))
            PO.mark("end", "hg")

        def act_hg(act):
            begin(act, "act", "hg")
            for h in range(HH):
                for t in range(NTASK):
                    d = hgb[f"D{t % 2}"]
                    act.wait_ge(dve_done, at("dve", "hg", "diff", h, t))
                    nc.scalar.activation(d, d, ACT.Exp).then_inc(act_done, AC.tick("hg", "exp", h, t))
                nc.scalar.activation(small[:, 16:20], BH[:, h, P - 1::P], ACT.Exp).then_inc(act_done, AC.tick())
                act.wait_ge(pe_done, at("pe", "hg", "task", h, NTASK - 1))
                act.wait_ge(dve_done, at("dve", "hg", "acc", h, 11))
                nc.scalar.activation(hgb["KD"], B[3][:, :], ACT.Copy).then_inc(act_done, AC.tick("hg", "kd", h))
                act.wait_ge(pe_done, at("pe", "hg", "o", h))
                nc.scalar.activation(hgb["P0"], B[4][:, :], ACT.Square).then_inc(act_done, AC.tick("hg", "osq", h))
                act.wait_ge(pe_done, at("pe", "hg", "oss", h))
                nc.scalar.activation(hgb["D0"], B[6][:, :], ACT.Sqrt, bias=gvec[:, 5:6]).then_inc(act_done, AC.tick("hg", "ostd", h))
                if h + 1 < HH:
                    act.wait_ge(dve_done, at("dve", "hg", "S", h, NT - 2))
            AC.mark("end", "hg")

        sqn = [region(work + m * T, T) for m in range(2)]
        rsn = [region(work + 2 * T, T), region(work + 3 * T, T)]
        tan = region(work + 4 * T, T)
        XP = region(work + 5 * T, 2, 32 * NCMP)
        o = work + 5 * T + 2 * 32 * NCMP
        HID = region(o, 8, 32); o += 256
        KCMP = region(o, 32); o += 32
        VCMP = region(o, 2, ND); o += 128
        assert o <= 21504
        Pn = [region(work + m * T, T) for m in range(2)]
        PTn = [region(work + (2 + m) * T, T) for m in range(2)]
        NORMED = [0, 1, 2, 3, 4, 6, 7]
        GAIN = {0: 0, 1: 0, 2: 0, 3: 0, 4: 1, 6: 2, 7: 3}
        SCALE = ND ** -0.5
        ITEMS = [(r, g, b, i) for r in range(4) for g in range(NG) for b, i in [(0, 0)] + [(b, i) for b in (1, 2) for i in range(NT)]]

        def half(g):
            return slice(ND * g, ND * g + ND)

        def pe_nsa(pe):
            begin(pe, "pe", "nsa")
            for n, c in enumerate(NORMED):
                pe.wait_ge(act_done, at("act", "nsa", "sq", n))
                nc.tensor.matmul(B[n % 2][:, :], headsum[:, :], sqn[n % 2], start=True, stop=True).then_inc(pe_done, PE.tick("nsa", "ss", n))
                pe.wait_ge(dve_done, at("dve", "nsa", "normed", n))
                nc.tensor.matmul(B[2 + n % 2][:, :], rot[:, :], NX[:, c, :], start=True, stop=True).then_inc(pe_done, PE.tick("nsa", "rot", n))
            for kv in range(2):
                pe.wait_ge(dve_done, at("dve", "nsa", "blocks", kv))
                if kv:
                    pe.wait_ge(act_done, at("act", "nsa", "hid", 0))
                else:
                    pe.wait_ge(dve_done, at("dve", "nsa", "rotated", len(NORMED) - 1))
                xp = XP[:, kv, :].rearrange("p (l n) -> p l n", n=NCMP)
                for part in range(2):
                    w = slot_of(pe, ("cmp", kv, part)).rearrange("p (l n) -> p l n", n=256)
                    for g in range(NG):
                        for hc in range(2):
                            for l in range(16):
                                last = nc.tensor.matmul(B[4 * g + hc][:, 0:NCMP], w[half(g), l, hc * P:(hc + 1) * P],
                                                        xp[half(g), 16 * part + l, :], start=(part == 0 and l == 0), stop=(part == 1 and l == 15))
                    last.then_inc(pe_done, PE.tick("nsa", "cmp1", kv, part))
                    used(("cmp", kv, part))
            pe.wait_ge(act_done, at("act", "nsa", "hid", 1))
            for g in range(NG):
                for hc in range(2):
                    nc.tensor.matmul(B[2][half(g), 0:NCMP], w2c[:, 0, hc, :], HID[:, 2 * g + hc, 0:NCMP], start=(hc == 0), stop=(hc == 1))
                for hc in range(2):
                    last = nc.tensor.matmul(B[3][0:NCMP, g * ND:(g + 1) * ND], HID[:, 4 + 2 * g + hc, 0:NCMP], w2c[:, 1, hc, :],
                                            start=(hc == 0), stop=(hc == 1))
            last.then_inc(pe_done, PE.tick("nsa", "cmp2"))
            pe.wait_ge(act_done, at("act", "nsa", "cmp2"))

            def scores(n):
                r, g, b, i = ITEMS[n]
                if n >= 2:
                    pe.wait_ge(act_done, at("act", "nsa", "exp", n - 2))
                if b == 0:
                    for i in range(NT):
                        last = nc.tensor.matmul(B4[n % 2][:, i, 0:NCMP], NX[half(g), r, i * P:(i + 1) * P], KCMP[half(g), 0:NCMP],
                                                start=True, stop=True)
                else:
                    last = nc.tensor.matmul(B[n % 2][:, 0:(i + 1) * P], NX[half(g), r, i * P:(i + 1) * P],
                                            NX[half(g), 5 + b, 0:(i + 1) * P], start=True, stop=True)
                last.then_inc(pe_done, PE.tick("nsa", "score", n))

            scores(0)
            for n, (r, g, b, i) in enumerate(ITEMS):
                if n + 1 < len(ITEMS):
                    scores(n + 1)
                pe.wait_ge(dve_done, at("dve", "nsa", "p", n))
                if n >= 2:
                    pe.wait_ge(act_done, at("act", "nsa", "pt", n - 2))
                p4 = tiles(Pn[n % 2])
                for j in range(NT if b == 0 else i + 1):
                    if b == 0:
                        last = nc.tensor.transpose(B4[2 + n % 2][:, j, :], p4[:, j, :], ident[:, :])
                    else:
                        last = nc.tensor.transpose(B4[2 + n % 2][:, j, :], p4[:, j, :], ident[:, :])
                last.then_inc(pe_done, PE.tick("nsa", "pt", n))
                pe.wait_ge(act_done, at("act", "nsa", "pt", n))
                O = B[4 + r % 2]
                if b == 0:
                    if g == 0 and r >= 2:
                        pe.wait_ge(dve_done, at("dve", "nsa", "o", r - 2))
                    last = nc.tensor.matmul(O[half(g), :], VCMP[0:NCMP, g, :], PTn[n % 2][0:NCMP, :], start=True, stop=True)
                else:
                    for j in range(i + 1):
                        last = nc.tensor.matmul(O[half(g), i * P:(i + 1) * P], VSW[:, j, (b - 1) * P + g * ND:(b - 1) * P + (g + 1) * ND],
                                                tiles(PTn[n % 2])[:, j, :], start=False, stop=True, skip_group_check=True)
                last.then_inc(pe_done, PE.tick("nsa", "pv", n))
            PE.mark("end", "nsa")

        def act_nsa(act):
            begin(act, "act", "nsa")
            for n, c in enumerate(NORMED):
                if n >= 2:
                    act.wait_ge(pe_done, at("pe", "nsa", "ss", n - 2))
                nc.scalar.activation(sqn[n % 2], NX[:, c, :], ACT.Square).then_inc(act_done, AC.tick("nsa", "sq", n))
                act.wait_ge(pe_done, at("pe", "nsa", "ss", n))
                if n >= 2:
                    act.wait_ge(dve_done, at("dve", "nsa", "normed", n - 2))
                nc.scalar.activation(rsn[n % 2], B[n % 2][:, :], ACT.Sqrt, bias=gvec[:, 5:6]).then_inc(act_done, AC.tick("nsa", "std", n))
            for kv in range(2):
                act.wait_ge(pe_done, at("pe", "nsa", "cmp1", kv, 1))
                for g in range(NG):
                    for hc in range(2):
                        last = nc.scalar.activation(HID[:, 4 * kv + 2 * g + hc, 0:NCMP], B[4 * g + hc][:, 0:NCMP], ACT.Silu)
                last.then_inc(act_done, AC.tick("nsa", "hid", kv))
            act.wait_ge(pe_done, at("pe", "nsa", "cmp2"))
            nc.scalar.activation(KCMP[:, 0:NCMP], B[2][:, 0:NCMP], ACT.Copy).then_inc(act_done, AC.tick())
            nc.scalar.activation(VCMP[0:NCMP, :, :], B[3][0:NCMP, 0:2 * ND].rearrange("p (g d) -> p g d", g=2), ACT.Copy)\
                .then_inc(act_done, AC.tick("nsa", "cmp2"))

            def exp(n):
                r, g, b, i = ITEMS[n]
                act.wait_ge(dve_done, at("dve", "nsa", "max", n))
                if n >= 2:
                    act.wait_ge(pe_done, at("pe", "nsa", "pt", n - 2))
                if b == 0:
                    ins = nc.scalar.activation(tiles(Pn[n % 2])[:, :, 0:NCMP], B4[n % 2][:, :, 0:NCMP], ACT.Exp, scale=SCALE)
                    ins.then_inc(act_done, AC.tick("nsa", "exp", n))
                else:
                    ins = nc.scalar.activation(Pn[n % 2][:, 0:(i + 1) * P], B[n % 2][:, 0:(i + 1) * P], ACT.Exp, scale=SCALE,
                                               bias=small[:, 20 + n % 2:21 + n % 2], accum_out=small[:, 22 + n % 2:23 + n % 2])
                    ins.then_inc(act_done, AC.tick("nsa", "exp", n))

            exp(0)
            for n, (r, g, b, i) in enumerate(ITEMS):
                if n + 1 < len(ITEMS):
                    exp(n + 1)
                act.wait_ge(pe_done, at("pe", "nsa", "pt", n))
                if n >= 2:
                    act.wait_ge(pe_done, at("pe", "nsa", "pv", n - 2))
                if b == 0:
                    ins = nc.scalar.activation(PTn[n % 2][0:NCMP, :], B[2 + n % 2][0:NCMP, :], ACT.Copy)
                else:
                    ins = nc.scalar.activation(PTn[n % 2][:, 0:(i + 1) * P], B[2 + n % 2][:, 0:(i + 1) * P], ACT.Copy)
                ins.then_inc(act_done, AC.tick("nsa", "pt", n))
            AC.mark("end", "nsa")

        def dve_nsa(dve):
            begin(dve, "dve", "nsa")

            def step(ins):
                ins.then_inc(dve_done, DV.tick())
                dve.wait_ge(dve_done, DV.n)

            for n, c in enumerate(NORMED):
                dve.wait_ge(act_done, at("act", "nsa", "std", n))
                step(nc.vector.reciprocal(rsn[n % 2], rsn[n % 2]))
                nc.vector.scalar_tensor_tensor(out=NX[:, c, :], in0=NX[:, c, :], scalar=gvec[:, 8 + GAIN[c]:9 + GAIN[c]], in1=rsn[n % 2],
                                               op0=ALU.mult, op1=ALU.mult).then_inc(dve_done, DV.tick("nsa", "normed", n))
                dve.wait_ge(pe_done, at("pe", "nsa", "rot", n))
                nc.vector.tensor_tensor(tan, B[2 + n % 2][:, :], SINF, ALU.mult).then_inc(dve_done, DV.tick())
                step(nc.vector.tensor_tensor(NX[:, c, :], NX[:, c, :], COSF, ALU.mult))
                nc.vector.tensor_tensor(NX[:, c, :], NX[:, c, :], tan, ALU.add).then_inc(dve_done, DV.tick("nsa", "rotated", n))
                dve.wait_ge(dve_done, DV.n)
            for kv in range(2):
                src = NX[:, 4 + kv, :]
                for a in range(2):
                    tok = src[:, a * CS:a * CS + NCMP * CS].rearrange("p (n l) -> p l n", l=CS)
                    dst = XP[:, kv, a * CS * NCMP:(a + 1) * CS * NCMP].rearrange("p (l n) -> p l n", n=NCMP)
                    pos = pecmp[:, kv, a * CS:(a + 1) * CS].rearrange("p (l o) -> p l o", o=1).to_broadcast([P, CS, NCMP])
                    ins = nc.vector.tensor_tensor(dst, tok, pos, ALU.add)
                ins.then_inc(dve_done, DV.tick("nsa", "blocks", kv))
            dve.wait_ge(act_done, at("act", "nsa", "cmp2"))
            for m in range(2):
                nc.vector.memset(Pn[m], 0.0).then_inc(dve_done, DV.tick())
            dve.wait_ge(dve_done, DV.n)
            cm = cmask[:, :, 0:NCMP]

            def front(n):
                r, g, b, i = ITEMS[n]
                dve.wait_ge(pe_done, at("pe", "nsa", "score", n))
                if n >= 2:
                    dve.wait_ge(act_done, at("act", "nsa", "exp", n - 2))
                S = B[n % 2]
                if b == 0:
                    S = B4[n % 2][:, :, 0:NCMP]
                    step(nc.vector.tensor_tensor(S, S, cm, ALU.add))
                    step(nc.vector.reduce_max(small[:, 24:28], S, AX))
                    m4 = small[:, 24:28].rearrange("p (i o) -> p i o", o=1).to_broadcast([P, NT, NCMP])
                    nc.vector.tensor_tensor(S, S, m4, ALU.subtract).then_inc(dve_done, DV.tick("nsa", "max", n))
                else:
                    step(nc.vector.tensor_tensor(S[:, i * P:(i + 1) * P], S[:, i * P:(i + 1) * P], causal[:, 2, :], ALU.add))
                    step(nc.vector.reduce_max(small[:, 28 + n % 2:29 + n % 2], S[:, 0:(i + 1) * P], AX))
                    nc.vector.tensor_scalar(small[:, 20 + n % 2:21 + n % 2], small[:, 28 + n % 2:29 + n % 2], -SCALE, None, ALU.mult)\
                        .then_inc(dve_done, DV.tick("nsa", "max", n))

            front(0)
            for n, (r, g, b, i) in enumerate(ITEMS):
                if n + 1 < len(ITEMS):
                    front(n + 1)
                dve.wait_ge(act_done, at("act", "nsa", "exp", n))
                head = NG * 2 * g + r
                if b == 0:
                    Pc = tiles(Pn[n % 2])[:, :, 0:NCMP]
                    s4 = small[:, 32:36]
                    step(nc.vector.reduce_sum(s4, Pc, AX))
                    step(nc.vector.reciprocal(s4, s4))
                    step(nc.vector.tensor_tensor(s4, s4, cmask[:, :, 31:32].rearrange("p i o -> p (i o)"), ALU.mult))
                    step(nc.vector.tensor_tensor(s4, s4, VSW[:, :, 256 + 3 * head], ALU.mult))
                    w4 = s4.rearrange("p (i o) -> p i o", o=1).to_broadcast([P, NT, NCMP])
                    nc.vector.tensor_tensor(Pc, Pc, w4, ALU.mult).then_inc(dve_done, DV.tick("nsa", "p", n))
                else:
                    s = small[:, 36 + n % 2:37 + n % 2]
                    step(nc.vector.reciprocal(s, small[:, 22 + n % 2:23 + n % 2]))
                    step(nc.vector.tensor_tensor(s, s, VSW[:, i, 256 + 3 * head + b:257 + 3 * head + b], ALU.mult))
                    nc.vector.tensor_scalar(Pn[n % 2][:, 0:(i + 1) * P], Pn[n % 2][:, 0:(i + 1) * P], s, None, ALU.mult)\
                        .then_inc(dve_done, DV.tick("nsa", "p", n))
                if g == 1 and b == 0 and r:
                    dve_o(dve, r - 1)
            dve_o(dve, 3)
            DV.mark("end", "nsa")

        def dve_o(dve, r):
            last_item = max(n for n, item in enumerate(ITEMS) if item[0] == r)
            dve.wait_ge(pe_done, at("pe", "nsa", "pv", last_item))
            nc.vector.tensor_copy(HT[:, 4 + r, :], B[4 + r % 2][:, :]).then_inc(dve_done, DV.tick("nsa", "o", r))

        comb = sb("comb", [P, P + 8])
        headsum = sb("headsum", [P, P])
        rot = sb("rot", [P, P])
        w2c = sb("w2c", [P, 2, 2, ND])
        pecmp = sb("pecmp", [P, 2, CB])
        cmask = sb("cmask", [P, NT, 32])
        lbl = sb("lbl", [P, 2, HH])

        @block.tensor
        def _(pe):
            pe.wait_ge(consts_in, 16 * N_CONSTS)
            for l in range(2):
                w = units(pe, ("cond", l))
                for u in range(4):
                    for k in range(KC):
                        last = nc.tensor.matmul(B[7][:, 4 * l + u:4 * l + u + 1], w[:, u, k, :], cvec[:, 0, k:k + 1],
                                                start=(k == 0), stop=(k == KC - 1))
                last.then_inc(pe_done, PE.tick("cond", l))
                used(("cond", l))
            pe.wait_ge(act_done, at("act", "conditions"))
            for l in range(4):
                pe_ada(pe, 0, l, 0)
            PE.mark("end", "cond")

            pe_gdn(pe)
            pe_residual(pe, "gdn_out", lambda l: ("gdn_out", l), KC, lambda k: OT_g[:, k, :], 4, True)
            pe_squares(pe, "norm0")
            pe_up(pe, 0)
            pe_residual(pe, "down0", lambda l: ("down", 0, l), FC, lambda k: hidden[:, k, :], 1, True)
            pe_squares(pe, "norm1")
            pe_ret(pe)
            pe_residual(pe, "ret_out", lambda l: ("ret_out", l), 16, lambda k: OT_r[:, k, :], 2, True)
            pe_squares(pe, "norm2")
            pe_up(pe, 1)
            pe_residual(pe, "down1", lambda l: ("down", 1, l), FC, lambda k: hidden[:, k, :], 1, True)
            pe_squares(pe, "norm3")
            pe_squares(pe, "norm4")
            pe_mix(pe)
            pe_hg(pe)
            pe_nsa(pe)
            pe_residual(pe, "mix_out", lambda l: ("mix_out", l), KC, lambda k: HT[:, k, :], 4, False)
            pe_squares(pe, "norm5")
            pe_up(pe, 2)
            pe_residual(pe, "down2", lambda l: ("down", 2, l), FC, lambda k: hidden[:, k, :], 1, False)

        @block.sync
        def _(sp):
            for n, key in enumerate(loads):
                if n >= SLOTS:
                    sp.wait_ge(pe_done, at("pe", "used", n - SLOTS))
                src = dr["w"][key[0]]
                for x in key[1:]:
                    src = src[x]
                sp.dma_start(ring[:, n % SLOTS, 0:src.shape[-1]], src).then_inc(ring_full[n % SLOTS], 16)

        @block.scalar
        def _(act):
            for name, dst in (("xT", XT), ("ident", ident), ("maskL", maskL), ("maskU", maskU), ("causal", causal), ("ones", ones),
                              ("sel", sel), ("ada_b", ada_b), ("lnp", lnp), ("ffc", ffc), ("gconv", gconv), ("gvec", gvec),
                              ("cvec", cvec), ("wab", wab), ("comb", comb), ("headsum", headsum), ("rot", rot), ("w2c", w2c),
                              ("pecmp", pecmp), ("cmask", cmask), ("lbl", lbl)):
                act.dma_start(dst[tuple([slice(None)] * len(dst.shape))], dr[name]).then_inc(consts_in, 16)
            act.wait_ge(consts_in, 16 * N_CONSTS)
            act.wait_ge(dve_done, at("dve", "condition"))
            nc.scalar.activation(evec[:, 0, :], evec[:, 0, :], ACT.Silu).then_inc(act_done, AC.tick())
            nc.scalar.activation(evec[:, 1, :], cvec[:, 2, :], ACT.Silu).then_inc(act_done, AC.tick("conditions"))
            AC.mark("end", "cond")
            act_gdn(act)
            AC.mark("end", "gdn_out")
            act_layer_norm(act, "norm0", 0)
            act_up(act, 0)
            AC.mark("end", "down0")
            act_layer_norm(act, "norm1", 1)
            act_ret(act)
            AC.mark("end", "ret_out")
            act_layer_norm(act, "norm2", 2)
            act_up(act, 1)
            AC.mark("end", "down1")
            act_layer_norm(act, "norm3", 3)
            act_rms(act, "norm4")
            nc.scalar.activation(small[:, 4:8], lbl[:, 0, :], ACT.Exp).then_inc(act_done, AC.tick())
            nc.scalar.activation(small[:, 8:12], lbl[:, 1, :], ACT.Exp).then_inc(act_done, AC.tick("bounds"))
            act_mix(act)
            act_hg(act)
            act_nsa(act)
            AC.mark("end", "mix_out")
            act_rms(act, "norm5")
            act_up(act, 2)
            AC.mark("end", "down2")
            act.wait_ge(dve_done, at("dve", "down2", "res", KC - 1))
            act.dma_start(out, XT[:, :, :]).then_inc(stored, 16)
            act.wait_ge(stored, 16)

        @block.vector
        def _(dve):
            dve.wait_ge(consts_in, 16 * N_CONSTS)
            dve.wait_ge(pe_done, at("pe", "cond", 1))
            nc.vector.tensor_tensor(evec[:, 0, :], B[7][:, 0:KC], cvec[:, 1, :], ALU.add).then_inc(dve_done, DV.tick("condition"))
            nc.vector.tensor_tensor(small[:, 48:52], lbl[:, 0, :], lbl[:, 1, :], ALU.max).then_inc(dve_done, DV.tick())
            dve.wait_ge(dve_done, DV.n)
            nc.vector.tensor_tensor(lbl[:, 0, :], lbl[:, 0, :], small[:, 48:52], ALU.subtract).then_inc(dve_done, DV.tick())
            nc.vector.tensor_tensor(lbl[:, 1, :], lbl[:, 1, :], small[:, 48:52], ALU.subtract).then_inc(dve_done, DV.tick())
            DV.mark("end", "cond")
            dve_gdn(dve)
            dve_residual(dve, "gdn_out", 16, 0, True)
            dve_layer_norm(dve, "norm0", None, 0, 0, 32, 24, True)
            dve_up(dve, 0)
            dve_residual(dve, "down0", 40, 0, True)
            dve_layer_norm(dve, "norm1", None, 1, 1, 8, 0, True)
            dve_ret(dve)
            dve_residual(dve, "ret_out", 16, 1, True)
            dve_layer_norm(dve, "norm2", None, 2, 1, 32, 24, True)
            dve_up(dve, 1)
            dve_residual(dve, "down1", 40, 1, True)
            dve_layer_norm(dve, "norm3", None, 3, None, None, None, False)
            dve_rms(dve, "norm4", 4, 8, 0)
            dve_mix(dve)
            dve_hg(dve)
            dve_nsa(dve)
            dve_residual(dve, "mix_out", 16, 2, False)
            dve_rms(dve, "norm5", 5, 32, 24)
            dve_up(dve, 2)
            dve_residual(dve, "down2", 40, 2, False)

        @block.gpsimd
        def _(pool):
            PO.mark("end", "cond")
            pool_gdn(pool)
            pool_residual(pool, "gdn_out")
            PO.mark("end", "norm0")
            PO.mark("end", "up0")
            pool_residual(pool, "down0")
            PO.mark("end", "norm1")
            pool_ret(pool)
            pool_residual(pool, "ret_out")
            PO.mark("end", "norm2")
            PO.mark("end", "up1")
            pool_residual(pool, "down1")
            for s in ("norm3", "norm4", "mix"):
                PO.mark("end", s)
            pool_hg(pool)
            for s in ("nsa", "mix_out", "norm5", "up2", "down2"):
                PO.mark("end", s)


_a = 6.28125
_b = float(np.float32(np.round((2 * np.pi - _a) * 2 ** 21) / 2 ** 21))
TWO_PI = (_a, _b, float(np.float32(2 * np.pi - _a - _b)))
N_CONSTS = 21


def tables():
    f = np.float32
    i = np.arange(P)
    c, m = i[:, None], i[None, :]
    low = np.stack([(c // (2 * s) == m // (2 * s)) & (c % (2 * s) >= s) & (m % (2 * s) < s) for s in LEVELS], 1).astype(f)
    upp = np.stack([(c // (2 * s) == m // (2 * s)) & (m % (2 * s) >= s) & (c % (2 * s) < s) for s in LEVELS], 1).astype(f)
    t = {"ident": np.eye(P, dtype=f), "maskL": low, "maskU": upp}
    t["causal"] = np.stack([(c > m).astype(f), (c <= m).astype(f), np.where(m > c, f(NEG), f(0)), ((c // 8 == m // 8) & (c <= m)).astype(f)], 1)
    t["ones"] = np.stack([np.full((P, P), v, f) for v in (1.0, 1 / D, 1 / 512, 1 / P)], 1)
    t["sel"] = np.repeat(np.eye(GH, dtype=f)[:, :, None], P, 2)
    t["comb"] = np.repeat((np.arange(P + 8) % 8 == 0).astype(f)[None], P, 0)
    t["headsum"] = ((c // ND == m // ND) / ND).astype(f)
    r = np.zeros((P, P), f)
    for g in (0, ND):
        for e in range(8):
            r[g + 8 + e, g + e] = -1
            r[g + e, g + 8 + e] = 1
    t["rot"] = r
    tok = np.arange(T)
    last = np.arange(NCMP) * CS + CB - 1
    cm = np.zeros((P, NT, 32), f)
    cm[:, :, :NCMP] = np.where(last[None] <= tok[:, None], f(0), f(NEG)).reshape(NT, P, NCMP).transpose(1, 0, 2)
    cm[:, :, 31] = (tok >= last[0]).astype(f).reshape(NT, P).T
    t["cmask"] = cm
    inv = f(10000.0) ** (-np.linspace(0.0, 1.0, RDK // 2, dtype=f))
    ang = (tok.astype(f)[None] * inv[:, None]).astype(f)
    t["ret_cos"], t["ret_sin"] = np.cos(ang).astype(f), np.sin(ang).astype(f)
    lg = np.log(1.0 - 2.0 ** (-5.0 - np.arange(RH)))
    rel = tok[None] - i[:, None]
    t["ret_D"] = (np.where(rel >= 0, np.exp(np.maximum(rel, 0) * lg[:, None, None]), 0) * RDK ** -0.5).astype(f)
    th = np.zeros(P, f)
    for g in (0, ND):
        for e in range(8):
            th[g + e] = th[g + 8 + e] = f(500000.0) ** f(-e * 2.0 / 16)
    t["theta"] = th
    return t


def blocks(w, per):
    k, n = w.shape
    return np.ascontiguousarray(w.reshape(k // P, P, n // P // per, per, P).transpose(2, 1, 3, 0, 4)).reshape(n // P // per, P, -1)


def rows(w):
    k, n = w.shape
    return np.ascontiguousarray(w.reshape(k // P, P, n).transpose(1, 0, 2)).reshape(P, -1)


def cols(v):
    return v.reshape(-1, P).T


def layout(x):
    f = np.float32
    t = tables()
    A = {}
    A["xT"] = x["x"][0].reshape(T, KC, P).transpose(2, 1, 0)
    for k in ("ident", "maskL", "maskU", "causal", "ones", "sel", "comb", "headsum", "rot", "cmask", "ret_cos", "ret_sin", "ret_D"):
        A[k] = t[k]
    A["ada_b"] = np.stack([cols(x["ada_b"][0]), cols(x["ada_b"][1]), cols(x["b_ada_2"][0])], 1)
    z = np.zeros(D, f)
    gains = [x["ln_g"][0, 0], x["ln_g"][0, 1], x["ln_g"][1, 0], x["ln_g"][1, 1], x["norm1_g_2"][0], x["norm2_g_2"][0]]
    biases = [x["ln_b"][0, 0], x["ln_b"][0, 1], x["ln_b"][1, 0], x["ln_b"][1, 1], z, z]
    A["lnp"] = np.stack([np.stack([cols(g), cols(b)], 2) for g, b in zip(gains, biases)], 1)
    ffc = np.zeros((P, 3, FC, 2, 4), f)
    for i in range(2):
        for m in range(3):
            ffc[:, i, :, 0, m] = cols(x["ffn_conv_w"][i, m])
        ffc[:, i, :, 0, 3] = cols(x["ffn_conv_b"][i])
    for half in range(2):
        s = slice(half * FF, (half + 1) * FF)
        for m in range(3):
            ffc[:, 2, :, half, m] = cols(x["conv_w_2"][0, m, s])
        ffc[:, 2, :, half, 3] = cols(x["conv_b_2"][0, s])
    A["ffc"] = ffc
    A["gconv"] = np.stack([cols(x["gdn_conv_w"][m]) for m in range(4)], 2)
    gv = np.zeros((P, 16), f)
    gv[:, 0] = x["gdn_norm_w"]
    gv[:GH, 1], gv[:GH, 2] = x["gdn_a_log"], x["gdn_dt_bias"]
    gv[:, 4], gv[:, 5], gv[:, 6] = LN_EPS, EPS, t["theta"]
    gv[:, 7] = x["hg_norm_g_2"][0]
    gv[:, 8] = np.concatenate([x["q_norm_g_2"][0]] * 2)
    for m in range(3):
        gv[:, 9 + m] = np.concatenate([x["k_norm_g_2"][0, m]] * 2)
    A["gvec"] = gv
    A["cvec"] = np.stack([cols(x["c"][0]), cols(x["cond_b"]), cols(x["c_2"][0])], 1)
    w = x["gdn_w_in"]
    ab = np.zeros((D, 64), f)
    ab[:, 0:GH], ab[:, 32:32 + GH] = w[:, 4096:4104], w[:, 4104:4112]
    A["wab"] = rows(ab).reshape(P, KC, 64)
    A["w2c"] = x["w_cmp2_2"][0].reshape(2, 2, P, ND).transpose(2, 0, 1, 3)
    A["pecmp"] = np.concatenate([x["pe_cmp_2"][0].transpose(2, 0, 1)] * 2, 0)
    A["lbl"] = np.stack([cols(x["lb_logits_2"][0]), cols(x["lb_logits_2"][1])], 1)
    A["pos"] = np.repeat(x["positions_2"].reshape(1, T), P, 0)

    W = {}
    W["cond"] = blocks(x["cond_w"], 4)
    W["ada"] = np.stack([blocks(x["ada_w"][0], 4), blocks(x["ada_w"][1], 4), blocks(x["w_ada_2"][0], 4)])
    W["gdn"] = blocks(w[:, :4096].reshape(D, 4, GH, P).transpose(0, 2, 1, 3).reshape(D, -1), 4)
    W["gdn_out"] = blocks(x["gdn_w_out"], 4)
    ups = [x["ffn_up"][0], x["ffn_up"][1], x["w_up_2"][0]]
    W["up"] = np.stack([blocks(u.reshape(D, 2, FC, P).transpose(0, 2, 1, 3).reshape(D, -1), 4) for u in ups])
    W["down"] = np.stack([blocks(d, 1) for d in (x["ffn_down"][0], x["ffn_down"][1], x["w_down_2"][0])])
    w = x["ret_w_in"]
    W["ret_qk"] = blocks(w[:, :2048].reshape(D, 2, RH, RDK).transpose(0, 2, 1, 3).reshape(D, -1), 4)
    W["ret_v"] = np.stack([rows(w[:, 2048 + h * RDV:2048 + (h + 1) * RDV]) for h in range(RH)])
    W["ret_g"] = blocks(w[:, 4096:], 4)
    W["ret_out"] = blocks(x["ret_w_out"], 2)
    w = x["w_in_2"][0]
    hq, hf, hi, hg, nq = (w[:, 512 * n:512 * (n + 1)] for n in range(5))
    kc, vc, ks, vs, kw, vw = (w[:, 2560 + P * n:2560 + P * (n + 1)] for n in range(6))
    nq = nq.reshape(D, NG, 4, ND).transpose(0, 2, 1, 3).reshape(D, 512)
    W["mix"] = blocks(np.stack([a.reshape(D, 4, P) for a in (hq, hf, hg, nq)], 2).reshape(D, -1), 4)
    W["mix_hi"] = rows(hi)[None]
    W["mix_c"] = blocks(np.concatenate([kc, vc, ks, kw], 1), 4)
    W["mix_v"] = rows(np.concatenate([vs, vw, w[:, 3328:3352]], 1))[None]
    w1 = x["w_cmp1_2"][0].reshape(2, 2, 16, ND, 256).transpose(0, 1, 3, 2, 4).reshape(2, 2, ND, -1)
    W["cmp"] = np.concatenate([w1, w1], 2)
    w = x["w_out_2"][0]
    nsa = w[512:].reshape(NG, 4, ND, D).transpose(1, 0, 2, 3).reshape(512, D)
    W["mix_out"] = blocks(np.concatenate([w[:512], nsa], 0), 4)
    return A, W


def kernel(**inputs):
    import concourse.bacc as bacc
    from concourse.bass_utils import run_bass_kernel_spmd

    A, W = layout({k: np.asarray(v) for k, v in inputs.items()})
    arrays = {f"in_{k}": np.ascontiguousarray(v) for k, v in A.items()}
    arrays.update({f"w_{k}": np.ascontiguousarray(v) for k, v in W.items()})
    plan = {}
    for _ in range(2):
        nc = bacc.Bacc("TRN2", target_bir_lowering=False, num_devices=1)
        ap = {k: nc.dram_tensor(k, v.shape, mybir.dt.from_np(v.dtype), kind="ExternalInput").ap() for k, v in arrays.items()}
        dr = {k: ap[f"in_{k}"] for k in A}
        dr["w"] = {k: ap[f"w_{k}"] for k in W}
        out = nc.dram_tensor("out", (P, KC, T), F32, kind="ExternalOutput").ap()
        program(nc, dr, out, plan)
    r = run_bass_kernel_spmd(nc, [arrays], core_ids=[0])
    y = r.results[0]["out"]
    return np.ascontiguousarray(y.transpose(2, 1, 0)).reshape(1, T, D)
```

```python
from contextlib import ExitStack

import numpy as np
import concourse.bass as bass
from concourse import mybir

ACT = mybir.ActivationFunctionType
ALU = mybir.AluOpType
F32 = mybir.dt.float32
I32 = mybir.dt.int32
AX = mybir.AxisListType.X

P = 128
D = 1024
T = 512
KC = D // P
NT = T // P
ALPHA = 4.0 ** 0.25
LN_EPS = 1e-5
EPS = 1e-6
FF = 2816
FC = FF // P
GH = 8
RH, RDK, RDV = 4, 256, 512
HH = 4
NH, NG, ND = 8, 2, 64
CB, CS = 32, 16
NCMP = (T - CB) // CS + 1
NEG = -1e30
MAGIC = 1.5 * 2.0 ** 23
SLOTS = 3
SLOT = 4096
LEVELS = [1, 2, 4, 8, 16, 32, 64]


class Steps:

    def __init__(self, plan, engine):
        self.n, self.plan, self.engine = 0, plan, engine

    def tick(self, *name):
        self.n += 1
        if name:
            self.plan[(self.engine, *name)] = self.n
        return 1

    def mark(self, *name):
        self.plan[(self.engine, *name)] = self.n


def load_order():
    out = [("cond", 0), ("cond", 1)] + [("ada", 0, l) for l in range(4)]
    out.append(("gdn", 0))
    for h in range(GH):
        if h + 1 < GH:
            out.append(("gdn", h + 1))
        out.append(("ada", 0, 4 + h))
    out += [("gdn_out", l) for l in range(2)]
    for i in range(3):
        for l in range(FC // 2):
            out.append(("up", i, l))
            if i < 2:
                out.append(("ada", i + 1, l))
        if i < 2:
            out.append(("ada", i + 1, 11))
        out += [("down", i, n) for n in range(KC)]
        if i == 0:
            out.append(("ret_qk", 0))
            for h in range(RH):
                out += [("ret_v", h), ("ret_g", h)]
                if h + 1 < RH:
                    out.append(("ret_qk", h + 1))
            out += [("ret_out", l) for l in range(4)]
        if i == 1:
            out += [("mix", h) for h in range(HH)] + [("mix_hi", 0), ("mix_c", 0), ("mix_v", 0)]
            out += [("cmp", 1, 0), ("cmp", 1, 1), ("cmp", 0, 0), ("cmp", 0, 1)]
            out += [("mix_out", l) for l in range(2)]
    return out


def program(nc, dr, out, plan):
    loads = load_order()
    load_at = {key: n for n, key in enumerate(loads)}

    with ExitStack() as ctx:
        def sb(name, shape, dt=F32):
            return ctx.enter_context(nc.sbuf_tensor(name, shape, dt))

        def sem(name):
            return ctx.enter_context(nc.semaphore(name))

        B = [ctx.enter_context(nc.psum_tensor(f"bank{i}", [P, 512], F32)) for i in range(8)]
        B4 = [b[:, :].rearrange("p (i c) -> p i c", c=P) for b in B]

        pe_done, act_done, dve_done, pool_done = (sem(n) for n in ("pe_done", "act_done", "dve_done", "pool_done"))
        ring_full = [sem(f"ring_full{s}") for s in range(SLOTS)]
        consts_in = sem("consts_in")
        ret_tables_in = sem("ret_tables_in")
        nsa_tables_in = sem("nsa_tables_in")
        stored = sem("stored")
        PE, AC, DV, PO = (Steps(plan, e) for e in ("pe", "act", "dve", "pool"))
        DONE = {"pe": pe_done, "act": act_done, "dve": dve_done, "pool": pool_done}

        def at(*name):
            return plan.get(name, 1)

        ring = sb("ring", [P, SLOTS, SLOT])
        XT = sb("XT", [P, KC, T])
        HT = sb("HT", [P, KC, T])
        arena = sb("arena", [P, 21504])
        ident = sb("ident", [P, P])
        maskL = sb("maskL", [P, 7, P])
        maskU = sb("maskU", [P, 7, P])
        causal = sb("causal", [P, 4, P])
        ones = sb("ones", [P, 4, P])
        sel = sb("sel", [GH, GH, P])
        mod = sb("mod", [P, 3, 48])
        mod1 = sb("mod1", [P, 3, 48])
        ada_b = sb("ada_b", [P, 3, 48])
        lnp = sb("lnp", [P, 6, KC, 2])
        ffc = sb("ffc", [P, 3, FC, 2, 4])
        gconv = sb("gconv", [P, 3 * GH, 4])
        gvec = sb("gvec", [P, 16])
        cvec = sb("cvec", [P, 3, KC])
        evec = sb("evec", [P, 2, KC])
        wab = sb("wab", [P, KC, 64])
        small = sb("small", [P, 64])
        rqk = sb("rqk", [P, 16])
        comb_v = sb("comb_v", [P, 4, KC])

        def region(offset, *shape):
            size = int(np.prod(shape))
            v = arena[:, offset:offset + size]
            if len(shape) == 2:
                v = v.rearrange("p (a b) -> p a b", b=shape[1])
            if len(shape) == 3:
                v = v.rearrange("p (a b c) -> p a b c", b=shape[1], c=shape[2])
            return v

        block = ctx.enter_context(nc.Block())
        conv_step = [0]
        ada_step = [0]
        stages = []

        def begin(eng, me, stage):
            n = stages.index(stage) if stage in stages else (stages.append(stage) or len(stages) - 1)
            if n and eng is not None:
                for other, steps in (("pe", PE), ("act", AC), ("dve", DV), ("pool", PO)):
                    v = plan.get((other, "end", stages[n - 1]), 0)
                    if v:
                        eng.wait_ge(DONE[other], v)

        def slot_of(pe, key):
            n = load_at[key]
            pe.wait_ge(ring_full[n % SLOTS], 16 * (n // SLOTS + 1))
            return ring[:, n % SLOTS, :]

        def units(pe, key, kc=KC, width=P):
            v = slot_of(pe, key)
            n = min(SLOT // (kc * width), 4)
            return v[:, 0:n * kc * width].rearrange("p (u k n) -> p u k n", u=n, k=kc)

        def used(key):
            PE.mark("used", load_at[key])

        ada_acc = [region(20480 + n * T, 4, P) for n in range(2)]

        def pe_ada(pe, i, l):
            pe.wait_ge(dve_done, at("dve", "ada", i, l))
            for u in range(4):
                c = 64 + 48 * i + 4 * l + u
                last = nc.tensor.matmul(B[7][:, c:c + 1], ada_acc[l % 2][:, u, :], ones[:, 0, 0:1], start=True, stop=True)
            last.then_inc(pe_done, PE.tick("ada", i, l))

        def dve_ada(dve, i, l, k0=0, k1=KC):
            n = load_at[("ada", i, l)]
            e = int(i == 2)
            if k0 == 0:
                dve.wait_ge(ring_full[n % SLOTS], 16 * (n // SLOTS + 1))
                if l >= 2:
                    dve.wait_ge(pe_done, at("pe", "ada", i, l - 2))
                elif i:
                    dve.wait_ge(pe_done, at("pe", "ada", i - 1, 10 + l))
            w = ring[:, n % SLOTS, :].rearrange("p (u k n) -> p u k n", u=4, k=KC)
            acc = ada_acc[l % 2]
            for k in range(k0, k1):
                if k == 0:
                    ins = nc.vector.tensor_scalar(acc, w[:, :, 0, :], evec[:, e, 0:1], None, ALU.mult)
                else:
                    dve.wait_ge(dve_done, ada_step[0])
                    ins = nc.vector.scalar_tensor_tensor(out=acc, in0=w[:, :, k, :], scalar=evec[:, e, k:k + 1], in1=acc,
                                                         op0=ALU.mult, op1=ALU.add)
                ins.then_inc(dve_done, DV.tick("ada", i, l))
                ada_step[0] = DV.n
            if k1 == KC:
                DV.mark("used", n)

        squares = [region(19456 + n * T, T) for n in range(2)]
        rstd = region(18944, T)
        mean2 = region(18432, T)

        def pe_residual(pe, tag, key_of, kc, src, per_load, has_mean, has_squares=True):
            begin(pe, "pe", tag)

            def sums(n):
                if has_mean:
                    pe.wait_ge(dve_done, at("dve", tag, "res", n))
                    nc.tensor.matmul(B[2][:, :], ones[:, 1, :], XT[:, n, :], start=(n == 0), stop=(n == KC - 1))
                if has_squares:
                    pe.wait_ge(act_done, at("act", tag, "square", n))
                    nc.tensor.matmul(B[3][:, :], ones[:, 1, :], squares[n % 2], start=(n == 0), stop=(n == KC - 1))\
                        .then_inc(pe_done, PE.tick(tag, "sums", n))

            for n in range(KC):
                w = units(pe, key_of(n // per_load), kc)
                bank = B[n % 2]
                if n >= 2:
                    pe.wait_ge(dve_done, at("dve", tag, "res", n - 2))
                for k in range(kc):
                    last = nc.tensor.matmul(bank[:, :], w[:, n % per_load, k, :], src(k), start=(k == 0), stop=(k == kc - 1))
                last.then_inc(pe_done, PE.tick(tag, "proj", n))
                if n % per_load == per_load - 1:
                    used(key_of(n // per_load))
                if n:
                    sums(n - 1)
            sums(KC - 1)
            PE.mark("end", tag)

        def act_residual(act, tag):
            begin(act, "act", tag)
            for n in range(KC):
                act.wait_ge(dve_done, at("dve", tag, "res", n))
                if n >= 2:
                    act.wait_ge(pe_done, at("pe", tag, "sums", n - 2))
                nc.scalar.activation(squares[n % 2], XT[:, n, :], ACT.Square).then_inc(act_done, AC.tick(tag, "square", n))
            AC.mark("end", tag)

        def pe_squares(pe, tag):
            for n in range(KC):
                pe.wait_ge(act_done, at("act", tag, "square", n))
                nc.tensor.matmul(B[3][:, :], ones[:, 1, :], squares[n % 2], start=(n == 0), stop=(n == KC - 1))\
                    .then_inc(pe_done, PE.tick(tag, "sums", n))
            PE.mark("end", tag)

        def wait_input(pe, norm, k):
            pe.wait_ge(act_done, at("act", norm, "modulated", k))

        def pe_up(pe, i):
            tag = f"up{i}"
            begin(None, None, tag)
            for j in range(FC):
                w = units(pe, ("up", i, j // 2))
                if j >= 2:
                    pe.wait_ge(dve_done, at("dve", tag, "hidden", j - 2))
                for half in range(2):
                    for k in range(KC):
                        if j == 0 and half == 0:
                            wait_input(pe, ("norm0", "norm2", "norm5")[i], k)
                        last = nc.tensor.matmul(B[2 * (j % 2) + half][:, :], w[:, 2 * (j % 2) + half, k, :], HT[:, k, :],
                                                start=(k == 0), stop=(k == KC - 1))
                last.then_inc(pe_done, PE.tick(tag, "proj", j))
                if j % 2:
                    used(("up", i, j // 2))
                    if i < 2 and j > 1:
                        pe_ada(pe, i + 1, j // 2 - 1)
            if i < 2:
                pe_ada(pe, i + 1, 10)
                pe_ada(pe, i + 1, 11)
            PE.mark("end", tag)

        hidden = region(0, FC, T)
        ffn_y = region(FC * T, 2, T)
        ffn_u = region(FC * T + 2 * T, 2, T)

        def dve_residual(dve, tag, gate, i):
            begin(dve, "dve", tag)
            g = mod1 if i < 2 else mod
            for n in range(KC):
                dve.wait_ge(pe_done, at("pe", tag, "proj", n))
                nc.vector.scalar_tensor_tensor(out=XT[:, n, :], in0=B[n % 2][:, :], scalar=g[:, i, gate + n:gate + n + 1],
                                               in1=XT[:, n, :], op0=ALU.mult, op1=ALU.add)\
                    .then_inc(dve_done, DV.tick(tag, "res", n))
            DV.mark("end", tag)

        def dve_combine(dve, which, i, sc, sh, scaled):
            g, b, m1 = lnp[:, which, :, 0], lnp[:, which, :, 1], mod1[:, i, sc:sc + KC]
            nc.vector.tensor_tensor(comb_v[:, 0, :], g, m1, ALU.mult).then_inc(dve_done, DV.tick())
            nc.vector.tensor_tensor(comb_v[:, 1, :], b, m1, ALU.mult).then_inc(dve_done, DV.tick())
            dve.wait_ge(dve_done, DV.n)
            nc.vector.tensor_tensor(comb_v[:, 1, :], comb_v[:, 1, :], mod[:, i, sh:sh + KC], ALU.add).then_inc(dve_done, DV.tick())
            nc.vector.tensor_scalar(comb_v[:, 2, :], g, ALPHA if scaled else 1.0, None, ALU.mult).then_inc(dve_done, DV.tick())
            nc.vector.tensor_scalar(comb_v[:, 3, :], b, ALPHA if scaled else 1.0, None, ALU.mult).then_inc(dve_done, DV.tick())

        def dve_layer_norm(dve, tag, stats, which, i, sc, sh, scaled):
            begin(None, None, tag)
            dve_combine(dve, which, i, sc, sh, scaled)
            dve.wait_ge(act_done, at("act", tag, "mean2"))
            nc.vector.tensor_tensor(rstd, B[3][:, :], mean2, ALU.subtract).then_inc(dve_done, DV.tick())
            dve.wait_ge(dve_done, DV.n)
            nc.vector.tensor_scalar(rstd, rstd, 0.0, None, ALU.max).then_inc(dve_done, DV.tick(tag, "var"))
            for n in range(KC):
                nc.vector.tensor_tensor(XT[:, n, :], XT[:, n, :], B[2][:, :], ALU.subtract).then_inc(dve_done, DV.tick())
                if n == 3:
                    dve.wait_ge(act_done, at("act", tag, "std"))
                    nc.vector.reciprocal(rstd, rstd).then_inc(dve_done, DV.tick())
                    dve.wait_ge(dve_done, DV.n)
                    for m in range(4):
                        nc.vector.tensor_tensor(XT[:, m, :], XT[:, m, :], rstd, ALU.mult).then_inc(dve_done, DV.tick(tag, "normed", m))
                if n > 3:
                    dve.wait_ge(dve_done, DV.n)
                    nc.vector.tensor_tensor(XT[:, n, :], XT[:, n, :], rstd, ALU.mult).then_inc(dve_done, DV.tick(tag, "normed", n))
            DV.mark("end", tag)

        def act_layer_norm(act, tag, stats, modulate):
            begin(None, None, tag)
            act.wait_ge(pe_done, at("pe", stats, "sums", KC - 1))
            nc.scalar.activation(mean2, B[2][:, :], ACT.Square).then_inc(act_done, AC.tick(tag, "mean2"))
            act.wait_ge(dve_done, at("dve", tag, "var"))
            nc.scalar.activation(rstd, rstd, ACT.Sqrt, bias=gvec[:, 4:5]).then_inc(act_done, AC.tick(tag, "std"))
            for n in range(KC):
                act.wait_ge(dve_done, at("dve", tag, "normed", n))
                if modulate:
                    nc.scalar.activation(HT[:, n, :], XT[:, n, :], ACT.Identity, bias=comb_v[:, 1, n:n + 1], scale=comb_v[:, 0, n:n + 1])\
                        .then_inc(act_done, AC.tick(tag, "modulated", n))
                else:
                    nc.scalar.activation(XT[:, n, :], XT[:, n, :], ACT.Identity, bias=comb_v[:, 3, n:n + 1], scale=comb_v[:, 2, n:n + 1])\
                        .then_inc(act_done, AC.tick(tag, "affine", n))
            AC.mark("end", tag)

        def pool_layer_norm(pool, tag):
            begin(None, None, tag)
            for n in range(KC):
                pool.wait_ge(act_done, at("act", tag, "modulated", n))
                last = nc.gpsimd.tensor_scalar(XT[:, n, :], XT[:, n, :], comb_v[:, 2, n:n + 1], comb_v[:, 3, n:n + 1], ALU.mult, ALU.add)
            last.then_inc(pool_done, PO.tick(tag, "affine"))
            PO.mark("end", tag)

        def act_rms(act, tag, stats):
            begin(None, None, tag)
            if stats == tag:
                for n in range(KC):
                    act.wait_ge(act_done, at("act", "norm3", "affine", n))
                    if n >= 2:
                        act.wait_ge(pe_done, at("pe", tag, "sums", n - 2))
                    nc.scalar.activation(squares[n % 2], XT[:, n, :], ACT.Square).then_inc(act_done, AC.tick(tag, "square", n))
            act.wait_ge(pe_done, at("pe", stats, "sums", KC - 1))
            nc.scalar.activation(rstd, B[3][:, :], ACT.Sqrt, bias=gvec[:, 5:6]).then_inc(act_done, AC.tick(tag, "std"))
            for n in range(KC):
                act.wait_ge(dve_done, at("dve", tag, "normed", n))
                nc.scalar.activation(HT[:, n, :], HT[:, n, :], ACT.Identity, bias=comb_v[:, 1, n:n + 1])\
                    .then_inc(act_done, AC.tick(tag, "modulated", n))
            AC.mark("end", tag)

        def dve_rms(dve, tag, which, sc, sh):
            begin(None, None, tag)
            dve.wait_ge(act_done, at("act", tag, "std"))
            dve_combine(dve, which, 2, sc, sh, False)
            nc.vector.reciprocal(rstd, rstd).then_inc(dve_done, DV.tick())
            dve.wait_ge(dve_done, DV.n)
            for n in range(KC):
                nc.vector.scalar_tensor_tensor(out=HT[:, n, :], in0=XT[:, n, :], scalar=comb_v[:, 0, n:n + 1], in1=rstd,
                                               op0=ALU.mult, op1=ALU.mult).then_inc(dve_done, DV.tick(tag, "normed", n))
            DV.mark("end", tag)

        def conv(dve, out_, src, taps, width):
            nc.vector.tensor_scalar(out_, src[:, :], taps(width - 1), None, ALU.mult).then_inc(dve_done, DV.tick())
            for j in range(1, width):
                dve.wait_ge(dve_done, DV.n)
                last = nc.vector.scalar_tensor_tensor(out=out_[:, j:], in0=src[:, 0:T - j], scalar=taps(width - 1 - j), in1=out_[:, j:],
                                                      op0=ALU.mult, op1=ALU.add)
                if j < width - 1:
                    last.then_inc(dve_done, DV.tick())
            return last

        def dve_up(dve, i):
            tag = f"up{i}"
            begin(dve, "dve", tag)
            for j in range(FC):
                s = j % 2
                dve.wait_ge(pe_done, at("pe", tag, "proj", j))
                conv(dve, ffn_y[:, s, :], B[2 * s], lambda m: ffc[:, i, j, 0, m:m + 1], 3).then_inc(dve_done, DV.tick(tag, "conv", j))
                if i == 2:
                    conv(dve, ffn_u[:, s, :], B[2 * s + 1], lambda m: ffc[:, i, j, 1, m:m + 1], 3).then_inc(dve_done, DV.tick())
                    dve.wait_ge(dve_done, DV.n)
                    dve.wait_ge(act_done, at("act", tag, "gate", j))
                    nc.vector.scalar_tensor_tensor(out=hidden[:, j, :], in0=ffn_u[:, s, :], scalar=ffc[:, i, j, 1, 3:4],
                                                   in1=ffn_y[:, s, :], op0=ALU.add, op1=ALU.mult)\
                        .then_inc(dve_done, DV.tick(tag, "hidden", j))
                else:
                    dve.wait_ge(act_done, at("act", tag, "gate", j))
                    nc.vector.tensor_tensor(hidden[:, j, :], ffn_y[:, s, :], B[2 * s + 1][:, :], ALU.mult)\
                        .then_inc(dve_done, DV.tick(tag, "hidden", j))
                if i < 2 and j % 2:
                    dve_ada(dve, i + 1, j // 2)
            if i < 2:
                dve_ada(dve, i + 1, 11)
                dve_mod(dve, i + 1, 0, 48, 11)
            DV.mark("end", tag)

        def act_up(act, i):
            tag = f"up{i}"
            begin(act, "act", tag)
            for j in range(FC):
                act.wait_ge(dve_done, at("dve", tag, "conv", j))
                nc.scalar.activation(ffn_y[:, j % 2, :], ffn_y[:, j % 2, :], ACT.Silu, bias=ffc[:, i, j, 0, 3:4])\
                    .then_inc(act_done, AC.tick(tag, "gate", j))
            AC.mark("end", tag)

        def dve_mod(dve, i, c0, c1, l):
            dve.wait_ge(pe_done, at("pe", "ada", i, l))
            nc.vector.tensor_tensor(mod[:, i, c0:c1], B[7][:, 64 + 48 * i + c0:64 + 48 * i + c1], ada_b[:, i, c0:c1], ALU.add)\
                .then_inc(dve_done, DV.tick())
            dve.wait_ge(dve_done, DV.n)
            nc.vector.tensor_scalar(mod1[:, i, c0:c1], mod[:, i, c0:c1], 1.0, None, ALU.add).then_inc(dve_done, DV.tick("mod", i, c1))

        o = 0
        OT_g = region(0, GH, T)
        o = GH * T
        G = {}
        for name in ("cq", "ck", "cv", "qs", "ks", "vs", "zs", "s1", "s2", "r1", "r2", "dp", "dn", "L", "LT", "D", "E", "Tm",
                     "QK", "vb", "kb", "kd", "U", "W", "qe", "eg"):
            G[name] = region(o, T)
            G[name + "4"] = region(o, NT, P)
            o += T
        ROWS = region(o, T); o += T
        COLS = region(o, NT, P); o += T
        gdn_S = region(o, 2, P); o += 2 * P
        gdn_vn = region(o, 2, P); o += 2 * P
        EGL = small[:, 0:4]
        EGLB = small[:, 8:40].rearrange("p (h i) -> p h i", i=4)
        rowt = [G["s1"], G["s2"], G["r1"], G["r2"], G["dp"]]
        reset = G["dn"]
        assert o <= 21504

        def pe_dense4(pe, key, n0, n1):
            h = key[1]
            w = units(pe, key)
            for n in range(n0, n1):
                u, k = n // KC, n % KC
                if k == 0:
                    if u >= 2:
                        pe.wait_ge(dve_done, at("dve", "gdn", "conv", h, u - 2))
                    elif h and u == 0:
                        pe.wait_ge(dve_done, at("dve", "gdn", "conv", h - 1, 2))
                    elif h and u == 1:
                        pe.wait_ge(act_done, at("act", "gdn", "z", h - 1))
                last = nc.tensor.matmul(B[u % 2][:, :], w[:, u, k, :], HT[:, k, :], start=(k == 0), stop=(k == KC - 1))
                if k == KC - 1:
                    last.then_inc(pe_done, PE.tick("gdn", "proj", h, u))
            if n1 == 4 * KC:
                used(key)

        def pe_gdn(pe):
            begin(pe, "pe", "gdn")
            pe.wait_ge(dve_done, at("dve", "gdn", "input"))
            for k in range(KC):
                last = nc.tensor.matmul(B[3][0:64, :], wab[:, k, :], HT[:, k, :], start=(k == 0), stop=(k == KC - 1))
            last.then_inc(pe_done, PE.tick("gdn", "ab"))
            pe_dense4(pe, ("gdn", 0), 0, 16)
            pe.wait_ge(act_done, at("act", "gdn", "rows"))
            pe.wait_ge(dve_done, at("dve", "gdn", "rows"))
            for i in range(NT):
                last = nc.tensor.transpose(B4[3][:, i, :], ROWS[:, i * P:(i + 1) * P], ident[:, :])
            last.then_inc(pe_done, PE.tick("gdn", "cols"))
            for h in range(GH):
                last = nc.tensor.matmul(B[4][:, 4 * h:4 * h + 4], sel[:, h, :], EGL[0:GH, :], start=True, stop=True)
            last.then_inc(pe_done, PE.tick("gdn", "eglb"))
            pe.wait_ge(dve_done, at("dve", "gdn", "eglb"))
            nc.tensor.matmul(B[4][:, :], sel[:, 0, :], ROWS[0:GH, :], start=True, stop=True).then_inc(pe_done, PE.tick("gdn", "gcb", 0))
            pe_dense4(pe, ("gdn", 0), 16, 32)

            for h in range(GH):
                def fill(part):
                    if h + 1 < GH:
                        pe_dense4(pe, ("gdn", h + 1), 2 * part, 2 * part + 2)

                for m, sq in enumerate(("s14", "s24")):
                    pe.wait_ge(act_done, at("act", "gdn", "sq", h, m))
                    for i in range(NT):
                        last = nc.tensor.matmul(B[2][:, 4 * m + i:4 * m + i + 1], G[sq][:, i, :], ones[:, 0, 0:1], start=True, stop=True)
                last.then_inc(pe_done, PE.tick("gdn", "ssq", h))
                fill(0)
                if h:
                    pe.wait_ge(act_done, at("act", "gdn", "oc", h - 1))
                pe.wait_ge(dve_done, at("dve", "gdn", "rqk", h))
                for m, bank in ((1, 2), (0, 3)):
                    for i in range(NT):
                        last = nc.tensor.matmul(B4[bank][:, i, :], rqk[:, 4 * m + i:4 * m + i + 1].to_broadcast([P, P]), ident[:, :],
                                                start=True, stop=True)
                    last.then_inc(pe_done, PE.tick("gdn", "rb", h, m))
                for i in range(NT):
                    last = nc.tensor.transpose(B4[6][:, i, :], G["vs4"][:, i, :], ident[:, :])
                last.then_inc(pe_done, PE.tick("gdn", "vtok", h))
                pe.wait_ge(dve_done, at("dve", "gdn", "khat", h))
                for i in range(NT):
                    last = nc.tensor.matmul(B4[5][:, i, :], G["ks4"][:, i, :], G["ks4"][:, i, :], start=True, stop=True)
                last.then_inc(pe_done, PE.tick("gdn", "kk", h))
                for i in range(NT):
                    last = nc.tensor.transpose(B4[2][:, i, :], G["ks4"][:, i, :], ident[:, :])
                last.then_inc(pe_done, PE.tick("gdn", "ktok", h))
                pe.wait_ge(dve_done, at("dve", "gdn", "qhat", h))
                pe.wait_ge(act_done, at("act", "gdn", "vb", h))
                for i in range(NT):
                    last = nc.tensor.matmul(B4[6][:, i, :], G["ks4"][:, i, :], G["qs4"][:, i, :], start=True, stop=True)
                last.then_inc(pe_done, PE.tick("gdn", "qk", h))
                pe.wait_ge(dve_done, at("dve", "gdn", "L", h))
                for i in range(NT):
                    last = nc.tensor.transpose(B4[5][:, i, :], G["L4"][:, i, :], ident[:, :])
                last.then_inc(pe_done, PE.tick("gdn", "LT", h))
                fill(1)
                fill(2)
                for l in range(1, 7):
                    pe.wait_ge(dve_done, at("dve", "gdn", "D", h, l - 1))
                    if l == 1:
                        pe.wait_ge(act_done, at("act", "gdn", "LT", h))
                    for i in range(NT):
                        last = nc.tensor.matmul(B4[5][:, i, :], G["LT4"][:, i, :], G["D4"][:, i, :], start=True, stop=True)
                    last.then_inc(pe_done, PE.tick("gdn", "LD", h, l))
                    fill(2 * l + 1)
                    pe.wait_ge(dve_done, at("dve", "gdn", "Tm", h, l))
                    pe.wait_ge(dve_done, at("dve", "gdn", "inv", h, l - 1))
                    if l < 6:
                        for i in range(NT):
                            last = nc.tensor.matmul(B4[6][:, i, :], G["E4"][:, i, :], G["Tm4"][:, i, :], start=True, stop=True)
                        last.then_inc(pe_done, PE.tick("gdn", "DT", h, l))
                    for i in range(NT):
                        last = nc.tensor.matmul(B4[4][:, i, :], G["Tm4"][:, i, :], G["E4"][:, i, :], start=True, stop=True)
                    last.then_inc(pe_done, PE.tick("gdn", "TE", h, l))
                    if l < 6:
                        fill(2 * l + 2)
                pe.wait_ge(dve_done, at("dve", "gdn", "inv", h, 6))
                for i in range(NT):
                    last = nc.tensor.matmul(B4[2][:, i, :], G["E4"][:, i, :], G["vb4"][:, i, :], start=True, stop=True)
                last.then_inc(pe_done, PE.tick("gdn", "U", h))
                for i in range(NT):
                    last = nc.tensor.matmul(B4[3][:, i, :], G["kb4"][:, i, :], G["E4"][:, i, :], start=True, stop=True)
                last.then_inc(pe_done, PE.tick("gdn", "W", h))
                fill(14)
                if h + 1 < GH:
                    nc.tensor.matmul(B[4][:, :], sel[:, h + 1, :], ROWS[0:GH, :], start=True, stop=True)\
                        .then_inc(pe_done, PE.tick("gdn", "gcb", h + 1))
                pe.wait_ge(act_done, at("act", "gdn", "UW", h))
                pe.wait_ge(pool_done, at("pool", "gdn", "qe", h))
                for i in range(NT):
                    if i:
                        pe.wait_ge(dve_done, at("dve", "gdn", "S", h, i - 1))
                        nc.tensor.matmul(B[2][:, 0:P], G["W4"][:, i, :], gdn_S[:, (i - 1) % 2, :], start=True, stop=True)\
                            .then_inc(pe_done, PE.tick("gdn", "wS", h, i))
                        nc.tensor.matmul(B4[3][:, i, :], gdn_S[:, (i - 1) % 2, :], G["qe4"][:, i, :], start=True, stop=False)
                    pe.wait_ge(dve_done, at("dve", "gdn", "vn", h, i))
                    if i < NT - 1:
                        nc.tensor.matmul(B[5][:, 0:P], G["kd4"][:, i, :], gdn_vn[:, i % 2, :], start=True, stop=True)\
                            .then_inc(pe_done, PE.tick("gdn", "kv", h, i))
                    last = nc.tensor.matmul(B4[3][:, i, :], gdn_vn[:, i % 2, :], G["QK4"][:, i, :], start=(i == 0), stop=True)
                    if i == 1:
                        fill(15)
                last.then_inc(pe_done, PE.tick("gdn", "o", h))
                pe.wait_ge(act_done, at("act", "gdn", "osq", h))
                for i in range(NT):
                    last = nc.tensor.matmul(B[2][:, i:i + 1], G["s14"][:, i, :], ones[:, 3, 0:1], start=True, stop=True)
                last.then_inc(pe_done, PE.tick("gdn", "oss", h))
                pe_ada(pe, 0, 4 + h)
                pe.wait_ge(dve_done, at("dve", "gdn", "ro", h))
                for i in range(NT):
                    last = nc.tensor.matmul(B4[5][:, i, :], rqk[:, 8 + i:9 + i].to_broadcast([P, P]), ident[:, :], start=True, stop=True)
                last.then_inc(pe_done, PE.tick("gdn", "rob", h))
            PE.mark("end", "gdn")

        def act_gdn(act):
            begin(act, "act", "gdn")
            S1, S2 = G["s1"], G["s2"]
            act.wait_ge(dve_done, at("dve", "gdn", "zeros"))
            act.wait_ge(pe_done, at("pe", "gdn", "ab"))
            nc.scalar.activation(ROWS[32:32 + GH, :], B[3][32:32 + GH, :], ACT.Sigmoid).then_inc(act_done, AC.tick())
            nc.scalar.activation(S1[0:GH, :], B[3][0:GH, :], ACT.Abs, bias=gvec[0:GH, 2:3]).then_inc(act_done, AC.tick())
            nc.scalar.activation(S2[0:GH, :], B[3][0:GH, :], ACT.Relu, bias=gvec[0:GH, 2:3]).then_inc(act_done, AC.tick())
            act.wait_ge(act_done, AC.n)
            nc.scalar.activation(S1[0:GH, :], S1[0:GH, :], ACT.Exp, scale=-1.0).then_inc(act_done, AC.tick())
            nc.scalar.activation(small[0:GH, 40:41], gvec[0:GH, 1:2], ACT.Exp).then_inc(act_done, AC.tick())
            act.wait_ge(act_done, AC.n)
            nc.scalar.activation(S1[0:GH, :], S1[0:GH, :], ACT.Ln, bias=1.0).then_inc(act_done, AC.tick("gdn", "softplus"))
            act.wait_ge(dve_done, at("dve", "gdn", "gc"))
            nc.scalar.activation(ROWS[64:64 + GH, :], ROWS[0:GH, :], ACT.Exp).then_inc(act_done, AC.tick())
            nc.scalar.activation(ROWS[96:96 + GH, :], G["r1"][0:GH, :], ACT.Exp).then_inc(act_done, AC.tick())
            nc.scalar.activation(EGL[0:GH, :], ROWS[0:GH, P - 1::P], ACT.Exp).then_inc(act_done, AC.tick("gdn", "rows"))

            def decays(h):
                act.wait_ge(pe_done, at("pe", "gdn", "gcb", h))
                if h:
                    act.wait_ge(pool_done, at("pool", "gdn", "qe", h - 1))
                    act.wait_ge(dve_done, at("dve", "gdn", "diff", h))
                nc.scalar.activation(G["eg"], B[4][:, :], ACT.Exp).then_inc(act_done, AC.tick("gdn", "eg", h))
                act.wait_ge(dve_done, at("dve", "gdn", "diff", h))
                nc.scalar.activation(G["dp"], G["dp"], ACT.Exp, scale=-1.0).then_inc(act_done, AC.tick())
                nc.scalar.activation(G["dn"], G["dn"], ACT.Exp).then_inc(act_done, AC.tick("gdn", "decay", h))

            decays(0)
            for h in range(GH):
                for u, (src, dst) in enumerate((("cq", "qs"), ("ck", "ks"), ("cv", "vs"))):
                    act.wait_ge(dve_done, at("dve", "gdn", "conv", h, u))
                    if h and u == 0:
                        act.wait_ge(dve_done, at("dve", "gdn", "gated", h - 1))
                        act.wait_ge(pe_done, at("pe", "gdn", "oss", h - 1))
                    nc.scalar.activation(G[dst], G[src], ACT.Silu).then_inc(act_done, AC.tick("gdn", "silu", h, u))
                act.wait_ge(act_done, AC.n)
                nc.scalar.activation(S1, G["qs"], ACT.Square).then_inc(act_done, AC.tick("gdn", "sq", h, 0))
                nc.scalar.activation(S2, G["ks"], ACT.Square).then_inc(act_done, AC.tick("gdn", "sq", h, 1))
                act.wait_ge(pe_done, at("pe", "gdn", "proj", h, 3))
                nc.scalar.activation(G["zs"], B[1][:, :], ACT.Silu).then_inc(act_done, AC.tick("gdn", "z", h))
                act.wait_ge(pe_done, at("pe", "gdn", "ssq", h))
                nc.scalar.activation(rqk[:, 0:8], B[2][:, 0:8], ACT.Sqrt, bias=gvec[:, 5:6]).then_inc(act_done, AC.tick("gdn", "std", h))
                act.wait_ge(pe_done, at("pe", "gdn", "vtok", h))
                for i in range(NT):
                    last = nc.scalar.activation(G["vb4"][:, i, :], B4[6][:, i, :], ACT.Copy, scale=COLS[:, i, 32 + h:33 + h])
                last.then_inc(act_done, AC.tick("gdn", "vb", h))
                act.wait_ge(pe_done, at("pe", "gdn", "LT", h))
                nc.scalar.activation(G["LT"], B[5][:, :], ACT.Copy).then_inc(act_done, AC.tick("gdn", "LT", h))
                act.wait_ge(pe_done, at("pe", "gdn", "W", h))
                nc.scalar.activation(G["U"], B[2][:, :], ACT.Copy).then_inc(act_done, AC.tick())
                nc.scalar.activation(G["W"], B[3][:, :], ACT.Copy).then_inc(act_done, AC.tick("gdn", "UW", h))
                act.wait_ge(pe_done, at("pe", "gdn", "o", h))
                nc.scalar.activation(S1, B[3][:, :], ACT.Square).then_inc(act_done, AC.tick("gdn", "osq", h))
                nc.scalar.activation(OT_g[:, h, :], B[3][:, :], ACT.Copy, scale=gvec[:, 0:1]).then_inc(act_done, AC.tick("gdn", "oc", h))
                act.wait_ge(pe_done, at("pe", "gdn", "oss", h))
                nc.scalar.activation(rqk[:, 8:12], B[2][:, 0:4], ACT.Sqrt, bias=gvec[:, 5:6]).then_inc(act_done, AC.tick("gdn", "ostd", h))
                if h + 1 < GH:
                    decays(h + 1)
            AC.mark("end", "gdn")

        def dve_conv4(dve, h, u, j0=0, j1=4):
            out_, src = G[("cq", "ck", "cv")[u]], B[u % 2]
            if j0 == 0:
                dve.wait_ge(pe_done, at("pe", "gdn", "proj", h, u))
                if h:
                    dve.wait_ge(act_done, at("act", "gdn", "silu", h - 1, u))
            for j in range(j0, j1):
                tap = gconv[:, u * GH + h, 3 - j:4 - j]
                if j == 0:
                    ins = nc.vector.tensor_scalar(out_, src[:, :], tap, None, ALU.mult)
                else:
                    dve.wait_ge(dve_done, conv_step[0])
                    ins = nc.vector.scalar_tensor_tensor(out=out_[:, j:], in0=src[:, 0:T - j], scalar=tap, in1=out_[:, j:],
                                                         op0=ALU.mult, op1=ALU.add)
                ins.then_inc(dve_done, DV.tick("gdn", "conv", h, u))
                conv_step[0] = DV.n

        def dve_diff(dve, h, i0, i1):
            if i0 == 0:
                dve.wait_ge(pe_done, at("pe", "gdn", "gcb", h))
                if h == 0:
                    dve.wait_ge(act_done, at("act", "gdn", "eg", h))
            for i in range(i0, i1):
                gcc = COLS[:, i, h:h + 1]
                nc.vector.tensor_scalar(G["dp4"][:, i, :], B4[4][:, i, :], gcc, 0.0, ALU.subtract, ALU.max)
                nc.vector.tensor_scalar(G["dn4"][:, i, :], B4[4][:, i, :], gcc, 0.0, ALU.subtract, ALU.min)\
                    .then_inc(dve_done, DV.tick("gdn", "diff", h))

        def dve_gdn(dve):
            begin(dve, "dve", "gdn")
            dve.wait_ge(act_done, at("act", "conditions"))
            for l in range(4):
                dve_ada(dve, 0, l)
            dve_mod(dve, 0, 0, 16, 3)
            dve.wait_ge(dve_done, DV.n)
            for n in range(KC):
                last = nc.vector.tensor_scalar(HT[:, n, :], XT[:, n, :], mod1[:, 0, 8 + n:9 + n], mod[:, 0, n:n + 1], ALU.mult, ALU.add)
            last.then_inc(dve_done, DV.tick("gdn", "input"))
            for n in range(KC):
                nc.vector.tensor_scalar(XT[:, n, :], XT[:, n, :], ALPHA, None, ALU.mult).then_inc(dve_done, DV.tick())
            nc.vector.memset(reset[0:GH, :], 1.0).then_inc(dve_done, DV.tick())
            nc.vector.memset(ROWS, 0.0).then_inc(dve_done, DV.tick("gdn", "zeros"))
            dve.wait_ge(dve_done, DV.n)
            nc.vector.memset(reset[0:GH, 0::P], 0.0).then_inc(dve_done, DV.tick())
            dve.wait_ge(act_done, at("act", "gdn", "softplus"))
            nc.vector.tensor_scalar(small[0:GH, 41:42], small[0:GH, 40:41], -1.0, None, ALU.mult).then_inc(dve_done, DV.tick())
            nc.vector.tensor_tensor(G["s1"][0:GH, :], G["s1"][0:GH, :], G["s2"][0:GH, :], ALU.add).then_inc(dve_done, DV.tick())
            dve.wait_ge(dve_done, DV.n)
            nc.vector.tensor_scalar(G["s1"][0:GH, :], G["s1"][0:GH, :], small[0:GH, 41:42], None, ALU.mult).then_inc(dve_done, DV.tick())
            dve.wait_ge(dve_done, DV.n)
            nc.vector.tensor_tensor_scan(ROWS[0:GH, :], reset[0:GH, :], G["s1"][0:GH, :], 0.0, ALU.mult, ALU.add)\
                .then_inc(dve_done, DV.tick())
            dve.wait_ge(dve_done, DV.n)
            rows4 = ROWS[0:GH, :].rearrange("p (i c) -> p i c", c=P)
            nc.vector.tensor_tensor(G["r14"][0:GH, :, :], rows4[:, :, P - 1:P].to_broadcast([GH, NT, P]), rows4, ALU.subtract)\
                .then_inc(dve_done, DV.tick("gdn", "gc"))
            DV.mark("gdn", "rows")
            dve_conv4(dve, 0, 0)
            dve_conv4(dve, 0, 1)
            dve.wait_ge(pe_done, at("pe", "gdn", "cols"))
            nc.vector.tensor_copy(COLS[:, :, :], B4[3]).then_inc(dve_done, DV.tick())
            dve.wait_ge(pe_done, at("pe", "gdn", "eglb"))
            nc.vector.tensor_copy(small[:, 8:40], B[4][:, 0:32]).then_inc(dve_done, DV.tick("gdn", "eglb"))
            dve.wait_ge(dve_done, DV.n)
            nc.vector.tensor_tensor(COLS[:, :, 40:48], COLS[:, :, 32:40], COLS[:, :, 64:72], ALU.mult).then_inc(dve_done, DV.tick())
            dve.wait_ge(dve_done, DV.n)
            dve_diff(dve, 0, 0, NT)
            dve_conv4(dve, 0, 2)

            for h in range(GH):
                beta, bg, el = COLS[:, :, 32 + h:33 + h], COLS[:, :, 40 + h:41 + h], COLS[:, :, 96 + h:97 + h]
                dve.wait_ge(act_done, at("act", "gdn", "std", h))
                nc.vector.reciprocal(rqk[:, 0:8], rqk[:, 0:8]).then_inc(dve_done, DV.tick("gdn", "rqk", h))
                dve.wait_ge(pe_done, at("pe", "gdn", "rb", h, 1))
                nc.vector.tensor_tensor(G["ks"], G["ks"], B[2][:, :], ALU.mult).then_inc(dve_done, DV.tick("gdn", "khat", h))
                dve.wait_ge(pe_done, at("pe", "gdn", "rb", h, 0))
                nc.vector.scalar_tensor_tensor(out=G["qs"], in0=G["qs"], scalar=float(P) ** -0.5, in1=B[3][:, :], op0=ALU.mult, op1=ALU.mult)\
                    .then_inc(dve_done, DV.tick("gdn", "qhat", h))
                dve.wait_ge(pool_done, at("pool", "gdn", "decay", h))
                dve.wait_ge(pe_done, at("pe", "gdn", "kk", h))
                for i in range(NT):
                    last = nc.vector.scalar_tensor_tensor(out=G["L4"][:, i, :], in0=B4[5][:, i, :], scalar=beta[:, i, :],
                                                          in1=G["dp4"][:, i, :], op0=ALU.mult, op1=ALU.mult)
                last.then_inc(dve_done, DV.tick("gdn", "L", h))
                dve.wait_ge(pe_done, at("pe", "gdn", "ktok", h))
                for i in range(NT):
                    nc.vector.tensor_scalar(G["kb4"][:, i, :], B4[2][:, i, :], bg[:, i, :], None, ALU.mult)
                    last = nc.vector.tensor_scalar(G["kd4"][:, i, :], B4[2][:, i, :], el[:, i, :], None, ALU.mult)
                last.then_inc(dve_done, DV.tick())
                dve.wait_ge(pe_done, at("pe", "gdn", "qk", h))
                nc.vector.tensor_tensor(G["QK"], B[6][:, :], G["dn"], ALU.mult).then_inc(dve_done, DV.tick())

                def level(mask, l):
                    return mask[:, l:l + 1, :].to_broadcast([P, NT, P])

                idb = ident[:, :].rearrange("p (a c) -> p a c", a=1).to_broadcast([P, NT, P])
                dve.wait_ge(dve_done, DV.n)
                nc.vector.tensor_tensor(G["D4"], G["L4"], level(maskL, 0), ALU.mult).then_inc(dve_done, DV.tick())
                dve.wait_ge(dve_done, DV.n)
                nc.vector.tensor_tensor(G["D4"], idb, G["D4"], ALU.subtract).then_inc(dve_done, DV.tick("gdn", "D", h, 0))
                dve.wait_ge(act_done, at("act", "gdn", "LT", h))
                nc.vector.tensor_tensor(G["E4"], G["LT4"], level(maskU, 0), ALU.mult).then_inc(dve_done, DV.tick())
                dve.wait_ge(dve_done, DV.n)
                nc.vector.tensor_tensor(G["E4"], idb, G["E4"], ALU.subtract).then_inc(dve_done, DV.tick("gdn", "inv", h, 0))
                for l in range(1, 7):
                    dve.wait_ge(pe_done, at("pe", "gdn", "LD", h, l))
                    nc.vector.tensor_tensor(G["Tm4"], B4[5], level(maskL, l), ALU.mult).then_inc(dve_done, DV.tick("gdn", "Tm", h, l))
                    dve_ada(dve, 0, 4 + h, l - 1, l)
                    if l < 6:
                        dve.wait_ge(pe_done, at("pe", "gdn", "DT", h, l))
                        nc.vector.tensor_tensor(G["D"], G["D"], B[6][:, :], ALU.subtract).then_inc(dve_done, DV.tick("gdn", "D", h, l))
                    dve.wait_ge(pe_done, at("pe", "gdn", "TE", h, l))
                    nc.vector.tensor_tensor(G["E"], G["E"], B[4][:, :], ALU.subtract).then_inc(dve_done, DV.tick("gdn", "inv", h, l))
                    if h + 1 < GH:
                        dve_conv4(dve, h + 1, (l - 1) // 2, 2 * ((l - 1) % 2), 2 * ((l - 1) % 2) + 2)
                dve.wait_ge(act_done, at("act", "gdn", "UW", h))
                for i in range(NT):
                    if i == 0:
                        nc.vector.tensor_copy(gdn_vn[:, 0, :], G["U4"][:, 0, :]).then_inc(dve_done, DV.tick("gdn", "vn", h, 0))
                    else:
                        dve.wait_ge(pe_done, at("pe", "gdn", "wS", h, i))
                        nc.vector.tensor_tensor(gdn_vn[:, i % 2, :], G["U4"][:, i, :], B[2][:, 0:P], ALU.subtract)\
                            .then_inc(dve_done, DV.tick("gdn", "vn", h, i))
                    if h + 1 < GH:
                        dve_diff(dve, h + 1, i, i + 1)
                    if i < NT - 1:
                        dve.wait_ge(pe_done, at("pe", "gdn", "kv", h, i))
                        if i == 0:
                            nc.vector.tensor_copy(gdn_S[:, 0, :], B[5][:, 0:P]).then_inc(dve_done, DV.tick("gdn", "S", h, 0))
                        else:
                            dve.wait_ge(dve_done, at("dve", "gdn", "S", h, i - 1))
                            nc.vector.scalar_tensor_tensor(out=gdn_S[:, i % 2, :], in0=gdn_S[:, (i - 1) % 2, :], scalar=EGLB[:, h, i:i + 1],
                                                           in1=B[5][:, 0:P], op0=ALU.mult, op1=ALU.add)\
                                .then_inc(dve_done, DV.tick("gdn", "S", h, i))
                    if i < 2:
                        dve_ada(dve, 0, 4 + h, 6 + i, 7 + i)
                dve.wait_ge(act_done, at("act", "gdn", "oc", h))
                nc.vector.tensor_tensor(OT_g[:, h, :], OT_g[:, h, :], G["zs"], ALU.mult).then_inc(dve_done, DV.tick("gdn", "gated", h))
                dve.wait_ge(act_done, at("act", "gdn", "ostd", h))
                nc.vector.reciprocal(rqk[:, 8:12], rqk[:, 8:12]).then_inc(dve_done, DV.tick("gdn", "ro", h))
                dve.wait_ge(pe_done, at("pe", "gdn", "rob", h))
                dve.wait_ge(dve_done, DV.n)
                nc.vector.tensor_tensor(OT_g[:, h, :], OT_g[:, h, :], B[5][:, :], ALU.mult).then_inc(dve_done, DV.tick("gdn", "out", h))
            dve_mod(dve, 0, 16, 48, 11)
            DV.mark("end", "gdn")

        def pool_gdn(pool):
            begin(pool, "pool", "gdn")
            for h in range(GH):
                pool.wait_ge(act_done, at("act", "gdn", "decay", h))
                nc.gpsimd.tensor_tensor(G["dp4"], G["dp4"], causal[:, 0:1, :].to_broadcast([P, NT, P]), ALU.mult)
                nc.gpsimd.tensor_tensor(G["dn4"], G["dn4"], causal[:, 1:2, :].to_broadcast([P, NT, P]), ALU.mult)\
                    .then_inc(pool_done, PO.tick("gdn", "decay", h))
                pool.wait_ge(dve_done, at("dve", "gdn", "qhat", h))
                nc.gpsimd.tensor_tensor(G["qe"], G["qs"], G["eg"], ALU.mult).then_inc(pool_done, PO.tick("gdn", "qe", h))
            PO.mark("end", "gdn")

        OT_r = region(0, 16, T)
        o = 16 * T
        R = {}
        for name in ("q1", "q2", "k1", "k2", "ta", "tb", "tc", "td", "sq0", "sq1", "rs"):
            R[name] = region(o, T); o += T
        ret_V = region(o, NT, RDV); o += NT * RDV
        ret_G = region(o, 4, T); o += 4 * T
        ret_P = region(o, NT, T); o += NT * T
        ret_cos = region(o, T); o += T
        ret_sin = region(o, T); o += T
        ret_D = region(o, 1, T); o += T
        assert o <= 21504

        def pe_ret(pe):
            begin(None, None, "ret")

            def qk(h):
                X = 4 * (h % 2)
                w = units(pe, ("ret_qk", h))
                if h:
                    pe.wait_ge(act_done, at("act", "ret", "gate", h - 1, 3))
                for u in range(4):
                    for k in range(KC):
                        if h == 0 and u == 0:
                            wait_input(pe, "norm1", k)
                        last = nc.tensor.matmul(B[X + u][:, :], w[:, u, k, :], HT[:, k, :], start=(k == 0), stop=(k == KC - 1))
                    last.then_inc(pe_done, PE.tick("ret", "qk", h, u))
                used(("ret_qk", h))

            qk(0)
            for h in range(RH):
                X, Y = 4 * (h % 2), 4 - 4 * (h % 2)
                w = slot_of(pe, ("ret_v", h)).rearrange("p (k n) -> p k n", k=KC)
                if h:
                    pe.wait_ge(act_done, at("act", "ret", "std", h - 1))
                for i in range(NT):
                    for k in range(KC):
                        last = nc.tensor.matmul(B[Y + i][:, :], HT[:, k, i * P:(i + 1) * P], w[:, k, :], start=(k == 0), stop=(k == KC - 1))
                    last.then_inc(pe_done, PE.tick("ret", "v", h, i))
                used(("ret_v", h))
                pe.wait_ge(pool_done, at("pool", "ret", "rope", h))
                for j in range(NT):
                    for c, (kk, qq) in enumerate((("k1", "q1"), ("k2", "q2"))):
                        last = nc.tensor.matmul(B[X + j][:, 0:T - j * P], R[kk][:, j * P:(j + 1) * P], R[qq][:, j * P:T],
                                                start=(c == 0), stop=(c == 1))
                    last.then_inc(pe_done, PE.tick("ret", "score", h, j))
                w = units(pe, ("ret_g", h))
                for u in range(4):
                    pe.wait_ge(act_done, at("act", "ret", "v", h, u))
                    for k in range(KC):
                        last = nc.tensor.matmul(B[Y + u][:, :], w[:, u, k, :], HT[:, k, :], start=(k == 0), stop=(k == KC - 1))
                    last.then_inc(pe_done, PE.tick("ret", "gate", h, u))
                used(("ret_g", h))
                pe.wait_ge(dve_done, at("dve", "ret", "p", h, 3))
                for c in range(4):
                    for j in range(NT):
                        last = nc.tensor.matmul(B[X + c][:, j * P:T], ret_V[:, j, c * P:(c + 1) * P], ret_P[:, j, 0:T - j * P],
                                                start=(j == 0), stop=(j == NT - 1))
                    last.then_inc(pe_done, PE.tick("ret", "o", h, c))
                if h + 1 < RH:
                    qk(h + 1)
                for c in range(4):
                    pe.wait_ge(act_done, at("act", "ret", "o", h, 3))
                    last = nc.tensor.matmul(B[X][:, :], ones[:, 2, :], OT_r[:, 4 * h + c, :], start=(c == 0), stop=(c == 3))
                last.then_inc(pe_done, PE.tick("ret", "mean", h))
                for c in range(4):
                    pe.wait_ge(act_done, at("act", "ret", "sq", h, c))
                    last = nc.tensor.matmul(B[X + 1][:, :], ones[:, 2, :], R[f"sq{c % 2}"], start=(c == 0), stop=(c == 3))
                    last.then_inc(pe_done, PE.tick("ret", "var", h, c))
            PE.mark("end", "ret")

        def dve_ret(dve):
            begin(dve, "dve", "ret")
            dve.wait_ge(ret_tables_in, 32)
            for h in range(RH):
                X = 4 * (h % 2)
                for n, dsts in ((0, ("ta", "tb")), (2, ("tc", "td"))):
                    if h:
                        dve.wait_ge(pool_done, at("pool", "ret", "rope", h - 1))
                    if n:
                        dve.wait_ge(pool_done, at("pool", "ret", "ropeq", h))
                    dve.wait_ge(pe_done, at("pe", "ret", "qk", h, n))
                    nc.vector.tensor_tensor(R["ta"], B[X + n][:, :], ret_cos, ALU.mult)
                    nc.vector.tensor_tensor(R["tb"], B[X + n][:, :], ret_sin, ALU.mult)
                    dve.wait_ge(pe_done, at("pe", "ret", "qk", h, n + 1))
                    nc.vector.tensor_tensor(R["tc"], B[X + n + 1][:, :], ret_sin, ALU.mult)
                    nc.vector.tensor_tensor(R["td"], B[X + n + 1][:, :], ret_cos, ALU.mult)\
                        .then_inc(dve_done, DV.tick("ret", "rope", h, n))
                dve.wait_ge(ret_tables_in, 48 + 16 * h)
                for j in range(NT):
                    dve.wait_ge(pe_done, at("pe", "ret", "score", h, j))
                    if h and j == 0:
                        dve.wait_ge(pe_done, at("pe", "ret", "o", h - 1, 3))
                    nc.vector.tensor_tensor(ret_P[:, j, 0:T - j * P], B[X + j][:, 0:T - j * P], ret_D[:, 0, 0:T - j * P], ALU.mult)\
                        .then_inc(dve_done, DV.tick("ret", "p", h, j))
                dve.wait_ge(pe_done, at("pe", "ret", "mean", h))
                for c in range(4):
                    nc.vector.tensor_tensor(OT_r[:, 4 * h + c, :], OT_r[:, 4 * h + c, :], B[X][:, :], ALU.subtract)\
                        .then_inc(dve_done, DV.tick("ret", "centred", h, c))
                dve.wait_ge(act_done, at("act", "ret", "std", h))
                nc.vector.reciprocal(R["rs"], R["rs"]).then_inc(dve_done, DV.tick())
                dve.wait_ge(dve_done, DV.n)
                for c in range(4):
                    nc.vector.tensor_tensor(OT_r[:, 4 * h + c, :], OT_r[:, 4 * h + c, :], R["rs"], ALU.mult).then_inc(dve_done, DV.tick())
                dve.wait_ge(dve_done, DV.n)
                for c in range(4):
                    last = nc.vector.tensor_tensor(OT_r[:, 4 * h + c, :], OT_r[:, 4 * h + c, :], ret_G[:, c, :], ALU.mult)
                last.then_inc(dve_done, DV.tick("ret", "out", h))
            DV.mark("end", "ret")

        def pool_ret(pool):
            begin(pool, "pool", "ret")
            for h in range(RH):
                for n, a, b in ((0, "q1", "q2"), (2, "k1", "k2")):
                    pool.wait_ge(dve_done, at("dve", "ret", "rope", h, n))
                    if h and n == 0:
                        pool.wait_ge(pe_done, at("pe", "ret", "score", h - 1, 3))
                    nc.gpsimd.tensor_tensor(R[a], R["ta"], R["tc"], ALU.subtract)
                    nc.gpsimd.tensor_tensor(R[b], R["tb"], R["td"], ALU.add)\
                        .then_inc(pool_done, PO.tick("ret", "ropeq" if n == 0 else "rope", h))
            PO.mark("end", "ret")

        def act_ret(act):
            begin(act, "act", "ret")
            act.dma_start(ret_cos, dr["ret_cos"]).then_inc(ret_tables_in, 16)
            act.dma_start(ret_sin, dr["ret_sin"]).then_inc(ret_tables_in, 16)
            for h in range(RH):
                X, Y = 4 * (h % 2), 4 - 4 * (h % 2)
                if h:
                    act.wait_ge(dve_done, at("dve", "ret", "p", h - 1, 3))
                act.wait_ge(ret_tables_in, 32 + 16 * h)
                act.dma_start(ret_D[:, 0, :], dr["ret_D"][h]).then_inc(ret_tables_in, 16)
                for i in range(NT):
                    act.wait_ge(pe_done, at("pe", "ret", "v", h, i))
                    nc.scalar.activation(ret_V[:, i, :], B[Y + i][:, :], ACT.Copy).then_inc(act_done, AC.tick("ret", "v", h, i))
                for u in range(4):
                    act.wait_ge(pe_done, at("pe", "ret", "gate", h, u))
                    if h and u == 0:
                        act.wait_ge(dve_done, at("dve", "ret", "out", h - 1))
                    nc.scalar.activation(ret_G[:, u, :], B[Y + u][:, :], ACT.Silu).then_inc(act_done, AC.tick("ret", "gate", h, u))
                for c in range(4):
                    act.wait_ge(pe_done, at("pe", "ret", "o", h, c))
                    nc.scalar.activation(OT_r[:, 4 * h + c, :], B[X + c][:, :], ACT.Copy).then_inc(act_done, AC.tick("ret", "o", h, c))
                for c in range(4):
                    act.wait_ge(dve_done, at("dve", "ret", "centred", h, c))
                    if c >= 2:
                        act.wait_ge(pe_done, at("pe", "ret", "var", h, c - 2))
                    nc.scalar.activation(R[f"sq{c % 2}"], OT_r[:, 4 * h + c, :], ACT.Square).then_inc(act_done, AC.tick("ret", "sq", h, c))
                act.wait_ge(pe_done, at("pe", "ret", "var", h, 3))
                nc.scalar.activation(R["rs"], B[X + 1][:, :], ACT.Sqrt, bias=gvec[:, 5:6]).then_inc(act_done, AC.tick("ret", "std", h))
            AC.mark("end", "ret")

        o = 0
        QH = region(o, HH, T); o += HH * T
        KH = region(o, HH, T); o += HH * T
        BH = region(o, HH, T); o += HH * T
        GH_ = region(o, HH, T); o += HH * T
        NX = region(o, 8, T); o += 8 * T
        HI = region(o, NT, T); o += NT * T
        VSW = region(o, NT, 280); o += NT * 280
        COSF = region(o, T); o += T
        SINF = region(o, T); o += T
        work = o
        assert work + 5024 <= 21504
        angle = [region(work + n * T, T) for n in range(4)]
        hreset = region(work + 4 * T, T)

        def pe_mix(pe):
            begin(None, None, "mix")
            for h in range(HH):
                w = units(pe, ("mix", h))
                X = 4 * (h % 2)
                for u in range(4):
                    if h >= 2:
                        pe.wait_ge(act_done, at("act", "mix", "taken", h - 2, u))
                    for k in range(KC):
                        if h == 0 and u == 0:
                            wait_input(pe, "norm4", k)
                        last = nc.tensor.matmul(B[X + u][:, :], w[:, u, k, :], HT[:, k, :], start=(k == 0), stop=(k == KC - 1))
                    last.then_inc(pe_done, PE.tick("mix", "proj", h, u))
                used(("mix", h))
            w = slot_of(pe, ("mix_hi", 0)).rearrange("p (k n) -> p k n", k=KC)
            for i in range(NT):
                pe.wait_ge(act_done, at("act", "mix", "taken", 2, i))
                for k in range(KC):
                    last = nc.tensor.matmul(B[i][:, :], HT[:, k, i * P:(i + 1) * P], w[:, k, :], start=(k == 0), stop=(k == KC - 1))
                last.then_inc(pe_done, PE.tick("mix", "hi", i))
            used(("mix_hi", 0))
            w = units(pe, ("mix_c", 0))
            for u in range(4):
                pe.wait_ge(act_done, at("act", "mix", "taken", 3, u))
                for k in range(KC):
                    last = nc.tensor.matmul(B[4 + u][:, :], w[:, u, k, :], HT[:, k, :], start=(k == 0), stop=(k == KC - 1))
                last.then_inc(pe_done, PE.tick("mix", "c", u))
            used(("mix_c", 0))
            w = slot_of(pe, ("mix_v", 0))[:, 0:KC * 280].rearrange("p (k n) -> p k n", k=KC)
            for i in range(NT):
                pe.wait_ge(act_done, at("act", "mix", "hi", i))
                for k in range(KC):
                    last = nc.tensor.matmul(B[i][:, 0:280], HT[:, k, i * P:(i + 1) * P], w[:, k, :], start=(k == 0), stop=(k == KC - 1))
                last.then_inc(pe_done, PE.tick("mix", "v", i))
            used(("mix_v", 0))
            PE.mark("end", "mix")

        def act_mix(act):
            begin(act, "act", "mix")
            act.dma_start(angle[0].bitcast(I32), dr["pos"]).then_inc(nsa_tables_in, 16)
            for h in range(HH):
                X = 4 * (h % 2)
                act.wait_ge(pe_done, at("pe", "mix", "proj", h, 3))
                nc.scalar.activation(QH[:, h, :], B[X][:, :], ACT.Silu).then_inc(act_done, AC.tick("mix", "taken", h, 0))
                nc.scalar.activation(GH_[:, h, :], B[X + 2][:, :], ACT.Silu).then_inc(act_done, AC.tick("mix", "taken", h, 2))
                nc.scalar.activation(NX[:, h, :], B[X + 3][:, :], ACT.Copy).then_inc(act_done, AC.tick("mix", "taken", h, 3))
                nc.scalar.activation(BH[:, h, :], B[X + 1][:, :], ACT.Sigmoid).then_inc(act_done, AC.tick())
                nc.scalar.activation(KH[:, h, :], B[X + 1][:, :], ACT.Sigmoid, scale=-1.0).then_inc(act_done, AC.tick("mix", "taken", h, 1))
            for i in range(NT):
                act.wait_ge(pe_done, at("pe", "mix", "hi", i))
                nc.scalar.activation(HI[:, i, :], B[i][:, :], ACT.Copy).then_inc(act_done, AC.tick("mix", "hi", i))
            for u in range(4):
                act.wait_ge(pe_done, at("pe", "mix", "c", u))
                nc.scalar.activation(NX[:, 4 + u, :], B[4 + u][:, :], ACT.Copy).then_inc(act_done, AC.tick("mix", "c", u))
            for i in range(NT):
                act.wait_ge(pe_done, at("pe", "mix", "v", i))
                nc.scalar.activation(VSW[:, i, :], B[i][:, 0:280], ACT.Copy).then_inc(act_done, AC.tick())
            act.wait_ge(act_done, AC.n)
            nc.scalar.activation(VSW[:, :, 256:280], VSW[:, :, 256:280], ACT.Sigmoid).then_inc(act_done, AC.tick())
            act.wait_ge(dve_done, at("dve", "mix", "f"))
            nc.scalar.activation(BH[:, :, :], BH[:, :, :], ACT.Ln).then_inc(act_done, AC.tick("mix", "logf"))
            act.wait_ge(dve_done, at("dve", "mix", "angles"))
            nc.scalar.activation(SINF, angle[1], ACT.Sin).then_inc(act_done, AC.tick())
            nc.scalar.activation(COSF, angle[2], ACT.Sin).then_inc(act_done, AC.tick())
            AC.mark("end", "mix")

        def dve_mix(dve):
            begin(dve, "dve", "mix")

            def step(ins):
                ins.then_inc(dve_done, DV.tick())
                dve.wait_ge(dve_done, DV.n)

            mx, e0, e1 = small[:, 0:4], small[:, 4:8], small[:, 8:12]
            dve.wait_ge(act_done, at("act", "bounds"))
            step(nc.vector.tensor_tensor(mx, e0, e1, ALU.add))
            step(nc.vector.reciprocal(mx, mx))
            nc.vector.tensor_tensor(e0, e0, mx, ALU.mult)
            step(nc.vector.tensor_tensor(e1, e1, mx, ALU.mult))
            dve.wait_ge(nsa_tables_in, 16)
            step(nc.vector.tensor_copy(angle[1], angle[0].bitcast(I32)))
            step(nc.vector.tensor_scalar(angle[1], angle[1], gvec[:, 6:7], None, ALU.mult))
            step(nc.vector.tensor_scalar(angle[2], angle[1], 1.0 / (2.0 * np.pi), MAGIC, ALU.mult, ALU.add))
            step(nc.vector.tensor_scalar(angle[2], angle[2], MAGIC, None, ALU.subtract))
            for c in TWO_PI:
                step(nc.vector.scalar_tensor_tensor(out=angle[1], in0=angle[2], scalar=-c, in1=angle[1], op0=ALU.mult, op1=ALU.add))
            pi = 3.1415925
            step(nc.vector.tensor_scalar(angle[2], angle[1], np.pi / 2, None, ALU.add))
            step(nc.vector.tensor_scalar(angle[3], angle[2], pi, -2.0 * np.pi, ALU.is_gt, ALU.mult))
            step(nc.vector.tensor_tensor(angle[2], angle[2], angle[3], ALU.add))
            step(nc.vector.tensor_scalar(angle[2], angle[2], pi, -pi, ALU.min, ALU.max))
            step(nc.vector.tensor_scalar(angle[1], angle[1], pi, -pi, ALU.min, ALU.max))
            DV.mark("mix", "angles")
            nc.vector.memset(hreset, 1.0).then_inc(dve_done, DV.tick())
            dve.wait_ge(dve_done, DV.n)
            nc.vector.memset(hreset[:, 0::P], 0.0).then_inc(dve_done, DV.tick())
            for h in range(HH):
                dve.wait_ge(act_done, at("act", "mix", "taken", h, 1))
                nc.vector.tensor_scalar(BH[:, h, :], BH[:, h, :], e1[:, h:h + 1], e0[:, h:h + 1], ALU.mult, ALU.add)
                nc.vector.tensor_scalar(KH[:, h, :], KH[:, h, :], e1[:, h:h + 1], None, ALU.mult).then_inc(dve_done, DV.tick("mix", "f"))
            dve.wait_ge(act_done, at("act", "mix", "logf"))
            dve.wait_ge(dve_done, DV.n)
            for h in range(HH):
                nc.vector.tensor_tensor_scan(NXT_B[:, h, :], hreset, BH[:, h, :], 0.0, ALU.mult, ALU.add).then_inc(dve_done, DV.tick())
            DV.mark("end", "mix")

        NXT_B = BH
        hgb = {n: region(work + m * T, T) for m, n in enumerate(("D0", "D1", "P0", "P1", "AT", "QE", "KD", "QL", "KL"))}
        hgS = region(work + 9 * T, 2, P)
        HD = [hgb["D0"], hgb["D1"], hgb["QE"]]
        HP = [hgb["P0"], hgb["P1"], hgb["KD"]]
        TASKS = [("diag", i) for i in range(8)] + [("level", l) for l in (3, 4, 5, 6)] + [("qe", 0), ("kd", 0)]
        NTASK = len(TASKS)

        def halves(v, l):
            w = v.rearrange("p (b a s) -> p b a s", a=2, s=LEVELS[l])
            return w[:, :, 0, :], w[:, :, 1, :]

        def tiles(v):
            return v.rearrange("p (i c) -> p i c", c=P)

        def pe_hg(pe):
            begin(pe, "pe", "hg")
            for h in range(HH):
                for t, (kind, x) in enumerate(TASKS):
                    if kind == "diag":
                        pe.wait_ge(pool_done, at("pool", "hg", "k", h, t))
                        if h and t == 0:
                            pe.wait_ge(dve_done, at("dve", "hg", "AT", h - 1))
                        nc.tensor.matmul(B[0][:, :], comb[:, 8 - x:8 - x + P], HP[t % 3], start=(x == 0), stop=(x == 7))\
                            .then_inc(pe_done, PE.tick("hg", "task", h, t))
                    elif kind == "level":
                        pe.wait_ge(pool_done, at("pool", "hg", "k", h, t))
                        pe.wait_ge(dve_done, at("dve", "hg", "q", h, t))
                        ql, kl = tiles(hgb["QL"]), tiles(hgb["KL"])
                        for i in range(NT):
                            last = nc.tensor.matmul(B4[1 + x % 2][:, i, :], kl[:, i, :], ql[:, i, :], start=True, stop=True)
                        last.then_inc(pe_done, PE.tick("hg", "task", h, t))
                    elif kind == "kd":
                        pe.wait_ge(dve_done, at("dve", "hg", "q", h, t))
                        for i in range(NT):
                            last = nc.tensor.transpose(B4[3][:, i, :], tiles(HP[t % 3])[:, i, :], ident[:, :])
                        last.then_inc(pe_done, PE.tick("hg", "task", h, t))
                pe.wait_ge(act_done, at("act", "hg", "kd", h))
                for i in range(NT):
                    hv = HI[:, i, h * P:(h + 1) * P]
                    if i < NT - 1:
                        if i:
                            pe.wait_ge(dve_done, at("dve", "hg", "S", h, i - 1))
                        nc.tensor.matmul(B[5][:, 0:P], tiles(hgb["KD"])[:, i, :], hv, start=True, stop=True)\
                            .then_inc(pe_done, PE.tick("hg", "kv", h, i))
                    nc.tensor.matmul(B4[4][:, i, :], hv, tiles(hgb["AT"])[:, i, :], start=True, stop=(i == 0))
                    if i:
                        pe.wait_ge(dve_done, at("dve", "hg", "S", h, i - 1))
                        last = nc.tensor.matmul(B4[4][:, i, :], hgS[:, (i - 1) % 2, :], tiles(hgb["QE"])[:, i, :], start=False, stop=True)
                last.then_inc(pe_done, PE.tick("hg", "o", h))
                pe.wait_ge(act_done, at("act", "hg", "osq", h))
                nc.tensor.matmul(B[6][:, :], ones[:, 3, :], hgb["AT"], start=True, stop=True).then_inc(pe_done, PE.tick("hg", "oss", h))
            PE.mark("end", "hg")

        def dve_hg(dve):
            begin(dve, "dve", "hg")
            nc.vector.memset(hgb["QL"], 0.0).then_inc(dve_done, DV.tick())
            nc.vector.memset(hgb["KL"], 0.0).then_inc(dve_done, DV.tick("hg", "zeros"))

            def tail(h):
                dve.wait_ge(act_done, at("act", "hg", "ostd", h))
                nc.vector.reciprocal(hgb["AT"], hgb["AT"]).then_inc(dve_done, DV.tick())
                dve.wait_ge(dve_done, DV.n)
                nc.vector.scalar_tensor_tensor(out=HT[:, h, :], in0=B[4][:, :], scalar=gvec[:, 7:8], in1=hgb["AT"], op0=ALU.mult, op1=ALU.mult)\
                    .then_inc(dve_done, DV.tick())
                dve.wait_ge(dve_done, DV.n)
                nc.vector.tensor_tensor(HT[:, h, :], HT[:, h, :], GH_[:, h, :], ALU.mult).then_inc(dve_done, DV.tick("hg", "out", h))

            for h in range(HH):
                q, k = QH[:, h, :], KH[:, h, :]

                def diff(h, t):
                    kind, x = TASKS[t]
                    b = BH[:, h, :]
                    d = HD[t % 3]
                    if t >= 3:
                        dve.wait_ge(dve_done, at("dve", "hg", "q", h, t - 3))
                    if t >= 3 and TASKS[t - 3][0] == "level":
                        dve.wait_ge(pool_done, at("pool", "hg", "k", h, t - 3))
                    if kind == "diag":
                        b8 = b.rearrange("p (n e) -> p n e", e=8)
                        ins = nc.vector.tensor_tensor(d.rearrange("p (n e) -> p n e", e=8), b8, b8[:, :, x:x + 1].to_broadcast([P, T // 8, 8]),
                                                      ALU.subtract)
                    elif kind == "level":
                        s = LEVELS[x]
                        lo, up = halves(b, x)
                        dlo, dup = halves(d, x)
                        ref = lo[:, :, s - 1:s].to_broadcast([P, T // (2 * s), s])
                        nc.vector.tensor_tensor(dlo, ref, lo, ALU.subtract)
                        ins = nc.vector.tensor_tensor(dup, up, ref, ALU.subtract)
                    elif kind == "qe":
                        ins = nc.vector.tensor_copy(d, b)
                    else:
                        b4 = tiles(b)
                        ins = nc.vector.tensor_tensor(tiles(d), b4[:, :, P - 1:P].to_broadcast([P, NT, P]), b4, ALU.subtract)
                    ins.then_inc(dve_done, DV.tick("hg", "diff", h, t))

                def accumulate(t):
                    x = TASKS[t][1]
                    dve.wait_ge(pe_done, at("pe", "hg", "task", h, t))
                    nc.vector.tensor_tensor(tiles(hgb["KD"]), B4[1 + x % 2], maskU[:, x:x + 1, :].to_broadcast([P, NT, P]), ALU.mult)\
                        .then_inc(dve_done, DV.tick())
                    dve.wait_ge(dve_done, DV.n)
                    nc.vector.tensor_tensor(hgb["AT"], hgb["AT"], hgb["KD"], ALU.add).then_inc(dve_done, DV.tick("hg", "acc", h, t))

                if h == 0:
                    diff(0, 0)
                    diff(0, 1)
                for t, (kind, x) in enumerate(TASKS):
                    d = HD[t % 3]
                    if h and t == 0:
                        dve.wait_ge(pe_done, at("pe", "hg", "o", h - 1))
                    if t + 2 < NTASK:
                        diff(h, t + 2)
                    dve.wait_ge(act_done, at("act", "hg", "exp", h, t))
                    if kind == "diag":
                        if t >= 3:
                            dve.wait_ge(pe_done, at("pe", "hg", "task", h, t - 3))
                        ins = nc.vector.scalar_tensor_tensor(out=HP[t % 3], in0=d, scalar=1.0, in1=q, op0=ALU.min, op1=ALU.mult)
                    elif kind == "level":
                        if x > 3:
                            dve.wait_ge(pe_done, at("pe", "hg", "task", h, t - 1))
                        ins = nc.vector.tensor_tensor(halves(hgb["QL"], x)[1], halves(d, x)[1], halves(q, x)[1], ALU.mult)
                    elif kind == "qe":
                        dve.wait_ge(pool_done, at("pool", "hg", "k", h, t - 1))
                        ins = nc.vector.tensor_tensor(hgb["QE"], d, q, ALU.mult)
                    else:
                        ins = nc.vector.tensor_tensor(HP[t % 3], d, k, ALU.mult)
                    ins.then_inc(dve_done, DV.tick("hg", "q", h, t))
                    if h and t == 2:
                        tail(h - 1)
                    if t == 8:
                        dve.wait_ge(pe_done, at("pe", "hg", "task", h, 7))
                        nc.vector.tensor_tensor(tiles(hgb["AT"]), B4[0], causal[:, 3:4, :].to_broadcast([P, NT, P]), ALU.mult)\
                            .then_inc(dve_done, DV.tick("hg", "AT", h))
                        dve.wait_ge(dve_done, DV.n)
                    if t > 8 and t <= 12:
                        accumulate(t - 1)
                        dve.wait_ge(dve_done, DV.n)
                if h + 1 < HH:
                    dve.wait_ge(dve_done, DV.n)
                    diff(h + 1, 0)
                    diff(h + 1, 1)
                for i in range(NT - 1):
                    dve.wait_ge(pe_done, at("pe", "hg", "kv", h, i))
                    if i == 0:
                        ins = nc.vector.tensor_copy(hgS[:, 0, :], B[5][:, 0:P])
                    else:
                        dve.wait_ge(dve_done, DV.n)
                        ins = nc.vector.scalar_tensor_tensor(out=hgS[:, i % 2, :], in0=hgS[:, (i - 1) % 2, :], scalar=small[:, 16 + i:17 + i],
                                                             in1=B[5][:, 0:P], op0=ALU.mult, op1=ALU.add)
                    ins.then_inc(dve_done, DV.tick("hg", "S", h, i))
            tail(HH - 1)
            DV.mark("end", "hg")

        def pool_hg(pool):
            begin(pool, "pool", "hg")
            pool.wait_ge(dve_done, at("dve", "hg", "zeros"))
            for h in range(HH):
                k = KH[:, h, :]
                for t, (kind, x) in enumerate(TASKS[:12]):
                    pool.wait_ge(dve_done, at("dve", "hg", "q", h, t))
                    if kind == "diag":
                        p8 = HP[t % 3].rearrange("p (n e) -> p n e", e=8)
                        k8 = k.rearrange("p (n e) -> p n e", e=8)
                        ins = nc.gpsimd.tensor_tensor(p8, p8, k8[:, :, x:x + 1].to_broadcast([P, T // 8, 8]), ALU.mult)
                    else:
                        ins = nc.gpsimd.tensor_tensor(halves(hgb["KL"], x)[0], halves(HD[t % 3], x)[0], halves(k, x)[0], ALU.mult)
                    ins.then_inc(pool_done, PO.tick("hg", "k", h, t))
            PO.mark("end", "hg")

        def act_hg(act):
            begin(act, "act", "hg")

            def exp(h, t):
                d = HD[t % 3]
                act.wait_ge(dve_done, at("dve", "hg", "diff", h, t))
                nc.scalar.activation(d, d, ACT.Exp).then_inc(act_done, AC.tick("hg", "exp", h, t))

            exp(0, 0)
            exp(0, 1)
            for h in range(HH):
                for t in range(2, NTASK):
                    exp(h, t)
                nc.scalar.activation(small[:, 16:20], BH[:, h, P - 1::P], ACT.Exp).then_inc(act_done, AC.tick())
                act.wait_ge(pe_done, at("pe", "hg", "task", h, NTASK - 1))
                act.wait_ge(dve_done, at("dve", "hg", "acc", h, 11))
                nc.scalar.activation(hgb["KD"], B[3][:, :], ACT.Copy).then_inc(act_done, AC.tick("hg", "kd", h))
                if h + 1 < HH:
                    exp(h + 1, 0)
                    exp(h + 1, 1)
                act.wait_ge(pe_done, at("pe", "hg", "o", h))
                nc.scalar.activation(hgb["AT"], B[4][:, :], ACT.Square).then_inc(act_done, AC.tick("hg", "osq", h))
                act.wait_ge(pe_done, at("pe", "hg", "oss", h))
                nc.scalar.activation(hgb["AT"], B[6][:, :], ACT.Sqrt, bias=gvec[:, 5:6]).then_inc(act_done, AC.tick("hg", "ostd", h))
            AC.mark("end", "hg")

        sqn = [region(work + m * T, T) for m in range(2)]
        rsn = [region(work + 2 * T, T), region(work + 3 * T, T)]
        tan = region(work + 4 * T, T)
        XP = region(0, 2, CB, 2 * NCMP)
        o = 4 * CB * NCMP
        SIL = region(o, 2, 256); o += 512
        HID = region(o, 4, 2 * NCMP); o += 8 * NCMP
        assert o <= 4 * HH * T
        o = work + 6 * T
        KCMP = region(o, 32); o += 32
        VCMP = region(o, 2, ND); o += 2 * ND
        assert o <= 21504
        Pn = [region(work + m * T, T) for m in range(3)]
        PTn = [region(work + (3 + m) * T, T) for m in range(2)]
        tri = region(work + 5 * T, T)
        SB = (0, 1, 6)
        NORMED = [4, 0, 1, 2, 3, 6, 7]
        GAIN = {0: 0, 1: 0, 2: 0, 3: 0, 4: 1, 6: 2, 7: 3}
        SCALE = ND ** -0.5
        ITEMS = [(r, g, b, i) for r in range(4) for g in range(NG) for b, i in [(0, 0)] + [(b, i) for b in (1, 2) for i in range(NT)]]

        def half(g):
            return slice(ND * g, ND * g + ND)

        def pe_nsa(pe):
            begin(pe, "pe", "nsa")

            def ss(n):
                pe.wait_ge(act_done, at("act", "nsa", "sq", n))
                nc.tensor.matmul(B[n % 2][:, :], headsum[:, :], sqn[n % 2], start=True, stop=True).then_inc(pe_done, PE.tick("nsa", "ss", n))

            def compress(s0, s1):
                for s in range(s0, min(s1, 2 * CB)):
                    kv, l = 1 - s // CB, s % CB
                    if l == 0:
                        pe.wait_ge(dve_done, at("dve", "nsa", "blocks", kv))
                        pe.wait_ge(pool_done, at("pool", "nsa", "zeros"))
                    w = slot_of(pe, ("cmp", kv, l // 16)).rearrange("p (l n) -> p l n", n=256)
                    last = nc.tensor.matmul(B[4 + kv][0:2 * NCMP, 0:256], XP[:, kv, l, :], w[:, l % 16, :], start=(l == 0), stop=(l == CB - 1))
                    if l % 16 == 15:
                        last.then_inc(pe_done, PE.tick("nsa", "cmp1", kv, l // 16))
                        used(("cmp", kv, l // 16))

            ss(0)
            for n, c in enumerate(NORMED):
                if n + 1 < len(NORMED):
                    ss(n + 1)
                compress(10 * n, 10 * n + 5)
                pe.wait_ge(dve_done, at("dve", "nsa", "normed", n))
                nc.tensor.matmul(B[2 + n % 2][:, :], rot[:, :], NX[:, c, :], start=True, stop=True).then_inc(pe_done, PE.tick("nsa", "rot", n))
                compress(10 * n + 5, 10 * n + 10)
            for kv in (1, 0):
                pe.wait_ge(act_done, at("act", "nsa", "silu", kv))
                for hc in range(2):
                    last = nc.tensor.transpose(B[6][:, (2 * kv + hc) * 2 * NCMP:(2 * kv + hc + 1) * 2 * NCMP],
                                               SIL[0:2 * NCMP, kv, hc * P:(hc + 1) * P], ident[0:2 * NCMP, 0:2 * NCMP])
            last.then_inc(pe_done, PE.tick("nsa", "hidT"))
            pe.wait_ge(act_done, at("act", "nsa", "hid"))
            pe.wait_ge(dve_done, at("dve", "nsa", "rotated", len(NORMED) - 1))
            for g in range(NG):
                blk = slice(g * NCMP, (g + 1) * NCMP)
                for hc in range(2):
                    nc.tensor.matmul(B[2][half(g), 0:NCMP], w2c[:, 0, hc, :], HID[:, hc, blk], start=(hc == 0), stop=(hc == 1))
                for hc in range(2):
                    last = nc.tensor.matmul(B[3][0:NCMP, g * ND:(g + 1) * ND], HID[:, 2 + hc, blk], w2c[:, 1, hc, :],
                                            start=(hc == 0), stop=(hc == 1))
            last.then_inc(pe_done, PE.tick("nsa", "cmp2"))
            pe.wait_ge(act_done, at("act", "nsa", "cmp2"))

            def scores(n):
                r, g, b, i = ITEMS[n]
                if n >= 3:
                    pe.wait_ge(act_done, at("act", "nsa", "exp", n - 3))
                if b == 0:
                    for i in range(NT):
                        last = nc.tensor.matmul(B4[SB[n % 3]][:, i, 0:NCMP], NX[half(g), r, i * P:(i + 1) * P], KCMP[half(g), 0:NCMP],
                                                start=True, stop=True)
                else:
                    last = nc.tensor.matmul(B[SB[n % 3]][:, 0:(i + 1) * P], NX[half(g), r, i * P:(i + 1) * P],
                                            NX[half(g), 5 + b, 0:(i + 1) * P], start=True, stop=True)
                last.then_inc(pe_done, PE.tick("nsa", "score", n))

            def values(n):
                r, g, b, i = ITEMS[n]
                pe.wait_ge(act_done, at("act", "nsa", "pt", n))
                O = B[4 + r % 2]
                if b == 0:
                    if g == 0 and r >= 2:
                        pe.wait_ge(dve_done, at("dve", "nsa", "o", r - 2))
                    last = nc.tensor.matmul(O[half(g), :], VCMP[0:NCMP, g, :], PTn[n % 2][0:NCMP, :], start=True, stop=True)
                else:
                    for j in range(i + 1):
                        last = nc.tensor.matmul(O[half(g), i * P:(i + 1) * P], VSW[:, j, (b - 1) * P + g * ND:(b - 1) * P + (g + 1) * ND],
                                                tiles(PTn[n % 2])[:, j, :], start=False, stop=True, skip_group_check=True)
                last.then_inc(pe_done, PE.tick("nsa", "pv", n))

            scores(0)
            scores(1)
            for n, (r, g, b, i) in enumerate(ITEMS):
                if n + 2 < len(ITEMS):
                    scores(n + 2)
                pe.wait_ge(dve_done, at("dve", "nsa", "p", n))
                if n >= 2:
                    pe.wait_ge(act_done, at("act", "nsa", "pt", n - 2))
                p4 = tiles(Pn[n % 3])
                for j in range(NT if b == 0 else i + 1):
                    last = nc.tensor.transpose(B4[2 + n % 2][:, j, :], p4[:, j, :], ident[:, :])
                last.then_inc(pe_done, PE.tick("nsa", "pt", n))
                if n:
                    values(n - 1)
            values(len(ITEMS) - 1)
            PE.mark("end", "nsa")

        def act_nsa(act):
            begin(act, "act", "nsa")
            for n, c in enumerate(NORMED):
                if n >= 2:
                    act.wait_ge(pe_done, at("pe", "nsa", "ss", n - 2))
                nc.scalar.activation(sqn[n % 2], NX[:, c, :], ACT.Square).then_inc(act_done, AC.tick("nsa", "sq", n))
                act.wait_ge(pe_done, at("pe", "nsa", "ss", n))
                if n >= 2:
                    act.wait_ge(dve_done, at("dve", "nsa", "normed", n - 2))
                nc.scalar.activation(rsn[n % 2], B[n % 2][:, :], ACT.Sqrt, bias=gvec[:, 5:6]).then_inc(act_done, AC.tick("nsa", "std", n))
            for kv in (1, 0):
                act.wait_ge(pe_done, at("pe", "nsa", "cmp1", kv, 1))
                nc.scalar.activation(SIL[0:2 * NCMP, kv, :], B[4 + kv][0:2 * NCMP, 0:256], ACT.Silu).then_inc(act_done, AC.tick("nsa", "silu", kv))
            act.wait_ge(pe_done, at("pe", "nsa", "hidT"))
            nc.scalar.activation(HID[:, :, :], B[6][:, 0:8 * NCMP].rearrange("p (a n) -> p a n", a=4), ACT.Copy).then_inc(act_done, AC.tick("nsa", "hid"))
            act.wait_ge(pe_done, at("pe", "nsa", "cmp2"))
            nc.scalar.activation(KCMP[:, 0:NCMP], B[2][:, 0:NCMP], ACT.Copy).then_inc(act_done, AC.tick())
            nc.scalar.activation(VCMP[0:NCMP, :, :], B[3][0:NCMP, 0:2 * ND].rearrange("p (g d) -> p g d", g=2), ACT.Copy)\
                .then_inc(act_done, AC.tick("nsa", "cmp2"))

            def exp(n):
                r, g, b, i = ITEMS[n]
                act.wait_ge(dve_done, at("dve", "nsa", "max", n))
                if n >= 3:
                    act.wait_ge(pe_done, at("pe", "nsa", "pt", n - 3))
                if b == 0:
                    ins = nc.scalar.activation(tiles(Pn[n % 3])[:, :, 0:NCMP], B4[SB[n % 3]][:, :, 0:NCMP], ACT.Exp, scale=SCALE)
                else:
                    ins = nc.scalar.activation(Pn[n % 3][:, 0:(i + 1) * P], B[SB[n % 3]][:, 0:(i + 1) * P], ACT.Exp, scale=SCALE,
                                               bias=small[:, 20 + n % 3:21 + n % 3], accum_out=small[:, 40 + n % 3:41 + n % 3])
                ins.then_inc(act_done, AC.tick("nsa", "exp", n))

            exp(0)
            for n, (r, g, b, i) in enumerate(ITEMS):
                if n + 1 < len(ITEMS):
                    exp(n + 1)
                act.wait_ge(pe_done, at("pe", "nsa", "pt", n))
                if n >= 2:
                    act.wait_ge(pe_done, at("pe", "nsa", "pv", n - 2))
                if b == 0:
                    ins = nc.scalar.activation(PTn[n % 2][0:NCMP, :], B[2 + n % 2][0:NCMP, :], ACT.Copy)
                else:
                    ins = nc.scalar.activation(PTn[n % 2][:, 0:(i + 1) * P], B[2 + n % 2][:, 0:(i + 1) * P], ACT.Copy)
                ins.then_inc(act_done, AC.tick("nsa", "pt", n))
            AC.mark("end", "nsa")

        def dve_nsa(dve):
            begin(dve, "dve", "nsa")

            def step(ins):
                ins.then_inc(dve_done, DV.tick())
                dve.wait_ge(dve_done, DV.n)

            def blocks_of(kv):
                for g in range(NG):
                    for a in range(2):
                        tok = NX[half(g), 4 + kv, a * CS:a * CS + NCMP * CS].rearrange("p (n l) -> p l n", l=CS)
                        dst = XP[half(g), kv, a * CS:(a + 1) * CS, g * NCMP:(g + 1) * NCMP]
                        pos = pecmp[half(g), kv, a * CS:(a + 1) * CS].rearrange("p (l o) -> p l o", o=1).to_broadcast([ND, CS, NCMP])
                        ins = nc.vector.tensor_tensor(dst, tok, pos, ALU.add)
                ins.then_inc(dve_done, DV.tick("nsa", "blocks", kv))

            blocks_of(1)
            for n, c in enumerate(NORMED):
                dve.wait_ge(act_done, at("act", "nsa", "std", n))
                step(nc.vector.reciprocal(rsn[n % 2], rsn[n % 2]))
                nc.vector.scalar_tensor_tensor(out=NX[:, c, :], in0=NX[:, c, :], scalar=gvec[:, 8 + GAIN[c]:9 + GAIN[c]], in1=rsn[n % 2],
                                               op0=ALU.mult, op1=ALU.mult).then_inc(dve_done, DV.tick("nsa", "normed", n))
                dve.wait_ge(pe_done, at("pe", "nsa", "rot", n))
                nc.vector.tensor_tensor(tan, B[2 + n % 2][:, :], SINF, ALU.mult).then_inc(dve_done, DV.tick())
                step(nc.vector.tensor_tensor(NX[:, c, :], NX[:, c, :], COSF, ALU.mult))
                nc.vector.tensor_tensor(NX[:, c, :], NX[:, c, :], tan, ALU.add).then_inc(dve_done, DV.tick("nsa", "rotated", n))
                dve.wait_ge(dve_done, DV.n)
                if c == 4:
                    blocks_of(0)
            for m in range(3):
                nc.vector.memset(Pn[m], 0.0).then_inc(dve_done, DV.tick())
            nc.vector.memset(tri, 0.0).then_inc(dve_done, DV.tick())
            dve.wait_ge(dve_done, DV.n)
            step(nc.vector.tensor_copy(tri[:, 3 * P:4 * P], causal[:, 2, :]))
            cm = cmask[:, :, 0:NCMP]

            def front(n):
                r, g, b, i = ITEMS[n]
                dve.wait_ge(pe_done, at("pe", "nsa", "score", n))
                if n >= 3:
                    dve.wait_ge(act_done, at("act", "nsa", "exp", n - 3))
                if b == 0:
                    S = B4[SB[n % 3]][:, :, 0:NCMP]
                    step(nc.vector.tensor_tensor(S, S, cm, ALU.add))
                    step(nc.vector.reduce_max(small[:, 24:28], S, AX))
                    m4 = small[:, 24:28].rearrange("p (i o) -> p i o", o=1).to_broadcast([P, NT, NCMP])
                    nc.vector.tensor_tensor(S, S, m4, ALU.subtract).then_inc(dve_done, DV.tick("nsa", "max", n))
                else:
                    S = B[SB[n % 3]]
                    mx = small[:, 28 + n % 3:29 + n % 3]
                    step(nc.vector.tensor_tensor_reduce(out=S[:, 0:(i + 1) * P], in0=S[:, 0:(i + 1) * P], in1=tri[:, (3 - i) * P:4 * P],
                                                        scale=1.0, scalar=-3e38, op0=ALU.add, op1=ALU.max, accum_out=mx))
                    nc.vector.tensor_scalar(small[:, 20 + n % 3:21 + n % 3], mx, -SCALE, None, ALU.mult)\
                        .then_inc(dve_done, DV.tick("nsa", "max", n))

            front(0)
            for n, (r, g, b, i) in enumerate(ITEMS):
                if n + 1 < len(ITEMS):
                    front(n + 1)
                dve.wait_ge(act_done, at("act", "nsa", "exp", n))
                head = NG * 2 * g + r
                if b == 0:
                    Pc = tiles(Pn[n % 3])[:, :, 0:NCMP]
                    s4 = small[:, 32:36]
                    step(nc.vector.reduce_sum(s4, Pc, AX))
                    step(nc.vector.reciprocal(s4, s4))
                    step(nc.vector.tensor_tensor(s4, s4, cmask[:, :, 31:32].rearrange("p i o -> p (i o)"), ALU.mult))
                    step(nc.vector.tensor_tensor(s4, s4, VSW[:, :, 256 + 3 * head], ALU.mult))
                    w4 = s4.rearrange("p (i o) -> p i o", o=1).to_broadcast([P, NT, NCMP])
                    nc.vector.tensor_tensor(Pc, Pc, w4, ALU.mult).then_inc(dve_done, DV.tick("nsa", "p", n))
                else:
                    s = small[:, 36 + n % 2:37 + n % 2]
                    step(nc.vector.reciprocal(s, small[:, 40 + n % 3:41 + n % 3]))
                    nc.vector.tensor_scalar(Pn[n % 3][:, 0:(i + 1) * P], Pn[n % 3][:, 0:(i + 1) * P], s,
                                            VSW[:, i, 256 + 3 * head + b:257 + 3 * head + b], ALU.mult, ALU.mult)\
                        .then_inc(dve_done, DV.tick("nsa", "p", n))
                if g == 1 and b == 0 and r:
                    dve_o(dve, r - 1)
            dve_o(dve, 3)
            DV.mark("end", "nsa")

        def pool_nsa(pool):
            begin(pool, "pool", "nsa")
            for g in range(NG):
                other = (1 - g) * NCMP
                ins = nc.gpsimd.memset(XP[half(g), :, :, other:other + NCMP], 0.0)
            ins.then_inc(pool_done, PO.tick("nsa", "zeros"))
            PO.mark("end", "nsa")

        def dve_o(dve, r):
            last_item = max(n for n, item in enumerate(ITEMS) if item[0] == r)
            dve.wait_ge(pe_done, at("pe", "nsa", "pv", last_item))
            nc.vector.tensor_copy(HT[:, 4 + r, :], B[4 + r % 2][:, :]).then_inc(dve_done, DV.tick("nsa", "o", r))

        comb = sb("comb", [P, P + 8])
        headsum = sb("headsum", [P, P])
        rot = sb("rot", [P, P])
        w2c = sb("w2c", [P, 2, 2, ND])
        pecmp = sb("pecmp", [P, 2, CB])
        cmask = sb("cmask", [P, NT, 32])
        lbl = sb("lbl", [P, 2, HH])

        @block.tensor
        def _(pe):
            pe.wait_ge(consts_in, 16 * N_CONSTS)
            for l in range(2):
                w = units(pe, ("cond", l))
                for u in range(4):
                    for k in range(KC):
                        last = nc.tensor.matmul(B[7][:, 4 * l + u:4 * l + u + 1], w[:, u, k, :], cvec[:, 0, k:k + 1],
                                                start=(k == 0), stop=(k == KC - 1))
                last.then_inc(pe_done, PE.tick("cond", l))
                used(("cond", l))
            for l in range(4):
                pe_ada(pe, 0, l)
            PE.mark("end", "cond")

            pe_gdn(pe)
            pe_residual(pe, "gdn_out", lambda l: ("gdn_out", l), KC, lambda k: OT_g[:, k, :], 4, True)
            begin(None, None, "norm0"); PE.mark("end", "norm0")
            pe_up(pe, 0)
            pe_residual(pe, "down0", lambda l: ("down", 0, l), FC, lambda k: hidden[:, k, :], 1, True)
            begin(None, None, "norm1"); PE.mark("end", "norm1")
            pe_ret(pe)
            pe_residual(pe, "ret_out", lambda l: ("ret_out", l), 16, lambda k: OT_r[:, k, :], 2, True)
            begin(None, None, "norm2"); PE.mark("end", "norm2")
            pe_up(pe, 1)
            pe_residual(pe, "down1", lambda l: ("down", 1, l), FC, lambda k: hidden[:, k, :], 1, True)
            begin(None, None, "norm3"); PE.mark("end", "norm3")
            begin(None, None, "norm4")
            pe_squares(pe, "norm4")
            pe_mix(pe)
            pe_hg(pe)
            pe_nsa(pe)
            pe_residual(pe, "mix_out", lambda l: ("mix_out", l), KC, lambda k: HT[:, k, :], 4, False)
            begin(None, None, "norm5"); PE.mark("end", "norm5")
            pe_up(pe, 2)
            pe_residual(pe, "down2", lambda l: ("down", 2, l), FC, lambda k: hidden[:, k, :], 1, False, False)

        @block.sync
        def _(sp):
            for n, key in enumerate(loads):
                if n >= SLOTS and loads[n - SLOTS][0] == "ada":
                    sp.wait_ge(dve_done, at("dve", "used", n - SLOTS))
                elif n >= SLOTS:
                    sp.wait_ge(pe_done, at("pe", "used", n - SLOTS))
                src = dr["w"][key[0]]
                for x in key[1:]:
                    src = src[x]
                sp.dma_start(ring[:, n % SLOTS, 0:src.shape[-1]], src).then_inc(ring_full[n % SLOTS], 16)

        @block.scalar
        def _(act):
            for name, dst in (("xT", XT), ("ident", ident), ("maskL", maskL), ("maskU", maskU), ("causal", causal), ("ones", ones),
                              ("sel", sel), ("ada_b", ada_b), ("lnp", lnp), ("ffc", ffc), ("gconv", gconv), ("gvec", gvec),
                              ("cvec", cvec), ("wab", wab), ("comb", comb), ("headsum", headsum), ("rot", rot), ("w2c", w2c),
                              ("pecmp", pecmp), ("cmask", cmask), ("lbl", lbl)):
                act.dma_start(dst[tuple([slice(None)] * len(dst.shape))], dr[name]).then_inc(consts_in, 16)
            act.wait_ge(consts_in, 16 * N_CONSTS)
            act.wait_ge(dve_done, at("dve", "condition"))
            nc.scalar.activation(evec[:, 0, :], evec[:, 0, :], ACT.Silu).then_inc(act_done, AC.tick())
            nc.scalar.activation(evec[:, 1, :], cvec[:, 2, :], ACT.Silu).then_inc(act_done, AC.tick("conditions"))
            AC.mark("end", "cond")
            act_gdn(act)
            act_residual(act, "gdn_out")
            act_layer_norm(act, "norm0", "gdn_out", True)
            act_up(act, 0)
            act_residual(act, "down0")
            act_layer_norm(act, "norm1", "down0", True)
            act_ret(act)
            act_residual(act, "ret_out")
            act_layer_norm(act, "norm2", "ret_out", True)
            act_up(act, 1)
            act_residual(act, "down1")
            act_layer_norm(act, "norm3", "down1", False)
            act_rms(act, "norm4", "norm4")
            nc.scalar.activation(small[:, 4:8], lbl[:, 0, :], ACT.Exp).then_inc(act_done, AC.tick())
            nc.scalar.activation(small[:, 8:12], lbl[:, 1, :], ACT.Exp).then_inc(act_done, AC.tick("bounds"))
            act_mix(act)
            act_hg(act)
            act_nsa(act)
            act_residual(act, "mix_out")
            act_rms(act, "norm5", "mix_out")
            act_up(act, 2)
            AC.mark("end", "down2")
            act.wait_ge(dve_done, at("dve", "down2", "res", KC - 1))
            act.dma_start(out, XT[:, :, :]).then_inc(stored, 16)
            act.wait_ge(stored, 16)

        @block.vector
        def _(dve):
            dve.wait_ge(consts_in, 16 * N_CONSTS)
            dve.wait_ge(pe_done, at("pe", "cond", 1))
            nc.vector.tensor_tensor(evec[:, 0, :], B[7][:, 0:KC], cvec[:, 1, :], ALU.add).then_inc(dve_done, DV.tick("condition"))
            nc.vector.tensor_tensor(small[:, 48:52], lbl[:, 0, :], lbl[:, 1, :], ALU.max).then_inc(dve_done, DV.tick())
            dve.wait_ge(dve_done, DV.n)
            nc.vector.tensor_tensor(lbl[:, 0, :], lbl[:, 0, :], small[:, 48:52], ALU.subtract).then_inc(dve_done, DV.tick())
            nc.vector.tensor_tensor(lbl[:, 1, :], lbl[:, 1, :], small[:, 48:52], ALU.subtract).then_inc(dve_done, DV.tick())
            DV.mark("end", "cond")
            dve_gdn(dve)
            dve_residual(dve, "gdn_out", 16, 0)
            dve_layer_norm(dve, "norm0", "gdn_out", 0, 0, 32, 24, True)
            dve_up(dve, 0)
            dve_residual(dve, "down0", 40, 0)
            dve_layer_norm(dve, "norm1", "down0", 1, 1, 8, 0, True)
            dve_ret(dve)
            dve_residual(dve, "ret_out", 16, 1)
            dve_layer_norm(dve, "norm2", "ret_out", 2, 1, 32, 24, True)
            dve_up(dve, 1)
            dve_residual(dve, "down1", 40, 1)
            dve_layer_norm(dve, "norm3", "down1", 3, 2, 8, 0, False)
            dve_rms(dve, "norm4", 4, 8, 0)
            dve_mix(dve)
            dve_hg(dve)
            dve_nsa(dve)
            dve_residual(dve, "mix_out", 16, 2)
            dve_rms(dve, "norm5", 5, 32, 24)
            dve_up(dve, 2)
            dve_residual(dve, "down2", 40, 2)

        @block.gpsimd
        def _(pool):
            PO.mark("end", "cond")
            pool_gdn(pool)
            PO.mark("end", "gdn_out")
            pool_layer_norm(pool, "norm0")
            PO.mark("end", "up0")
            PO.mark("end", "down0")
            pool_layer_norm(pool, "norm1")
            pool_ret(pool)
            PO.mark("end", "ret_out")
            pool_layer_norm(pool, "norm2")
            PO.mark("end", "up1")
            PO.mark("end", "down1")
            for s in ("norm3", "norm4", "mix"):
                PO.mark("end", s)
            pool_hg(pool)
            pool_nsa(pool)
            for s in ("mix_out", "norm5", "up2", "down2"):
                PO.mark("end", s)


_a = 6.28125
_b = float(np.float32(np.round((2 * np.pi - _a) * 2 ** 21) / 2 ** 21))
TWO_PI = (_a, _b, float(np.float32(2 * np.pi - _a - _b)))
N_CONSTS = 21


def tables():
    f = np.float32
    i = np.arange(P)
    c, m = i[:, None], i[None, :]
    low = np.stack([(c // (2 * s) == m // (2 * s)) & (c % (2 * s) >= s) & (m % (2 * s) < s) for s in LEVELS], 1).astype(f)
    upp = np.stack([(c // (2 * s) == m // (2 * s)) & (m % (2 * s) >= s) & (c % (2 * s) < s) for s in LEVELS], 1).astype(f)
    t = {"ident": np.eye(P, dtype=f), "maskL": low, "maskU": upp}
    t["causal"] = np.stack([(c > m).astype(f), (c <= m).astype(f), np.where(m > c, f(NEG), f(0)), ((c // 8 == m // 8) & (c <= m)).astype(f)], 1)
    t["ones"] = np.stack([np.full((P, P), v, f) for v in (1.0, 1 / D, 1 / 512, 1 / P)], 1)
    t["sel"] = np.repeat(np.eye(GH, dtype=f)[:, :, None], P, 2)
    t["comb"] = np.repeat((np.arange(P + 8) % 8 == 0).astype(f)[None], P, 0)
    t["headsum"] = ((c // ND == m // ND) / ND).astype(f)
    r = np.zeros((P, P), f)
    for g in (0, ND):
        for e in range(8):
            r[g + 8 + e, g + e] = -1
            r[g + e, g + 8 + e] = 1
    t["rot"] = r
    tok = np.arange(T)
    last = np.arange(NCMP) * CS + CB - 1
    cm = np.zeros((P, NT, 32), f)
    cm[:, :, :NCMP] = np.where(last[None] <= tok[:, None], f(0), f(NEG)).reshape(NT, P, NCMP).transpose(1, 0, 2)
    cm[:, :, 31] = (tok >= last[0]).astype(f).reshape(NT, P).T
    t["cmask"] = cm
    inv = f(10000.0) ** (-np.linspace(0.0, 1.0, RDK // 2, dtype=f))
    ang = (tok.astype(f)[None] * inv[:, None]).astype(f)
    t["ret_cos"], t["ret_sin"] = np.cos(ang).astype(f), np.sin(ang).astype(f)
    lg = np.log(1.0 - 2.0 ** (-5.0 - np.arange(RH)))
    rel = tok[None] - i[:, None]
    t["ret_D"] = (np.where(rel >= 0, np.exp(np.maximum(rel, 0) * lg[:, None, None]), 0) * RDK ** -0.5).astype(f)
    th = np.zeros(P, f)
    for g in (0, ND):
        for e in range(8):
            th[g + e] = th[g + 8 + e] = f(500000.0) ** f(-e * 2.0 / 16)
    t["theta"] = th
    return t


def blocks(w, per):
    k, n = w.shape
    return np.ascontiguousarray(w.reshape(k // P, P, n // P // per, per, P).transpose(2, 1, 3, 0, 4)).reshape(n // P // per, P, -1)


def rows(w):
    k, n = w.shape
    return np.ascontiguousarray(w.reshape(k // P, P, n).transpose(1, 0, 2)).reshape(P, -1)


def cols(v):
    return v.reshape(-1, P).T


def layout(x):
    f = np.float32
    t = tables()
    A = {}
    A["xT"] = x["x"][0].reshape(T, KC, P).transpose(2, 1, 0)
    for k in ("ident", "maskL", "maskU", "causal", "ones", "sel", "comb", "headsum", "rot", "cmask", "ret_cos", "ret_sin", "ret_D"):
        A[k] = t[k]
    A["ada_b"] = np.stack([cols(x["ada_b"][0]), cols(x["ada_b"][1]), cols(x["b_ada_2"][0])], 1)
    z = np.zeros(D, f)
    gains = [x["ln_g"][0, 0], x["ln_g"][0, 1], x["ln_g"][1, 0], x["ln_g"][1, 1], x["norm1_g_2"][0], x["norm2_g_2"][0]]
    biases = [x["ln_b"][0, 0], x["ln_b"][0, 1], x["ln_b"][1, 0], x["ln_b"][1, 1], z, z]
    A["lnp"] = np.stack([np.stack([cols(g), cols(b)], 2) for g, b in zip(gains, biases)], 1)
    ffc = np.zeros((P, 3, FC, 2, 4), f)
    for i in range(2):
        for m in range(3):
            ffc[:, i, :, 0, m] = cols(x["ffn_conv_w"][i, m])
        ffc[:, i, :, 0, 3] = cols(x["ffn_conv_b"][i])
    for half in range(2):
        s = slice(half * FF, (half + 1) * FF)
        for m in range(3):
            ffc[:, 2, :, half, m] = cols(x["conv_w_2"][0, m, s])
        ffc[:, 2, :, half, 3] = cols(x["conv_b_2"][0, s])
    A["ffc"] = ffc
    A["gconv"] = np.stack([cols(x["gdn_conv_w"][m]) for m in range(4)], 2)
    gv = np.zeros((P, 16), f)
    gv[:, 0] = x["gdn_norm_w"]
    gv[:GH, 1], gv[:GH, 2] = x["gdn_a_log"], x["gdn_dt_bias"]
    gv[:, 4], gv[:, 5], gv[:, 6] = LN_EPS, EPS, t["theta"]
    gv[:, 7] = x["hg_norm_g_2"][0]
    gv[:, 8] = np.concatenate([x["q_norm_g_2"][0]] * 2)
    for m in range(3):
        gv[:, 9 + m] = np.concatenate([x["k_norm_g_2"][0, m]] * 2)
    A["gvec"] = gv
    A["cvec"] = np.stack([cols(x["c"][0]), cols(x["cond_b"]), cols(x["c_2"][0])], 1)
    w = x["gdn_w_in"]
    ab = np.zeros((D, 64), f)
    ab[:, 0:GH], ab[:, 32:32 + GH] = w[:, 4096:4104], w[:, 4104:4112]
    A["wab"] = rows(ab).reshape(P, KC, 64)
    A["w2c"] = x["w_cmp2_2"][0].reshape(2, 2, P, ND).transpose(2, 0, 1, 3)
    A["pecmp"] = np.concatenate([x["pe_cmp_2"][0].transpose(2, 0, 1)] * 2, 0)
    A["lbl"] = np.stack([cols(x["lb_logits_2"][0]), cols(x["lb_logits_2"][1])], 1)
    A["pos"] = np.repeat(x["positions_2"].reshape(1, T), P, 0)

    W = {}
    W["cond"] = blocks(x["cond_w"], 4)
    W["ada"] = np.stack([blocks(x["ada_w"][0], 4), blocks(x["ada_w"][1], 4), blocks(x["w_ada_2"][0], 4)])
    W["gdn"] = blocks(w[:, :4096].reshape(D, 4, GH, P).transpose(0, 2, 1, 3).reshape(D, -1), 4)
    W["gdn_out"] = blocks(x["gdn_w_out"], 4)
    ups = [x["ffn_up"][0], x["ffn_up"][1], x["w_up_2"][0]]
    W["up"] = np.stack([blocks(u.reshape(D, 2, FC, P).transpose(0, 2, 1, 3).reshape(D, -1), 4) for u in ups])
    W["down"] = np.stack([blocks(d, 1) for d in (x["ffn_down"][0], x["ffn_down"][1], x["w_down_2"][0])])
    w = x["ret_w_in"]
    W["ret_qk"] = blocks(w[:, :2048].reshape(D, 2, RH, RDK).transpose(0, 2, 1, 3).reshape(D, -1), 4)
    W["ret_v"] = np.stack([rows(w[:, 2048 + h * RDV:2048 + (h + 1) * RDV]) for h in range(RH)])
    W["ret_g"] = blocks(w[:, 4096:], 4)
    W["ret_out"] = blocks(x["ret_w_out"], 2)
    w = x["w_in_2"][0]
    hq, hf, hi, hg, nq = (w[:, 512 * n:512 * (n + 1)] for n in range(5))
    kc, vc, ks, vs, kw, vw = (w[:, 2560 + P * n:2560 + P * (n + 1)] for n in range(6))
    nq = nq.reshape(D, NG, 4, ND).transpose(0, 2, 1, 3).reshape(D, 512)
    W["mix"] = blocks(np.stack([a.reshape(D, 4, P) for a in (hq, hf, hg, nq)], 2).reshape(D, -1), 4)
    W["mix_hi"] = rows(hi)[None]
    W["mix_c"] = blocks(np.concatenate([kc, vc, ks, kw], 1), 4)
    W["mix_v"] = rows(np.concatenate([vs, vw, w[:, 3328:3352]], 1))[None]
    w1 = x["w_cmp1_2"][0].reshape(2, 2, 16, ND, 256).transpose(0, 1, 3, 2, 4).reshape(2, 2, ND, -1)
    W["cmp"] = np.concatenate([w1, w1], 2)
    w = x["w_out_2"][0]
    nsa = w[512:].reshape(NG, 4, ND, D).transpose(1, 0, 2, 3).reshape(512, D)
    W["mix_out"] = blocks(np.concatenate([w[:512], nsa], 0), 4)
    return A, W


def kernel(**inputs):
    import concourse.bacc as bacc
    from concourse.bass_utils import run_bass_kernel_spmd

    A, W = layout({k: np.asarray(v) for k, v in inputs.items()})
    arrays = {f"in_{k}": np.ascontiguousarray(v) for k, v in A.items()}
    arrays.update({f"w_{k}": np.ascontiguousarray(v) for k, v in W.items()})
    plan = {}
    for _ in range(2):
        nc = bacc.Bacc("TRN2", target_bir_lowering=False, num_devices=1)
        ap = {k: nc.dram_tensor(k, v.shape, mybir.dt.from_np(v.dtype), kind="ExternalInput").ap() for k, v in arrays.items()}
        dr = {k: ap[f"in_{k}"] for k in A}
        dr["w"] = {k: ap[f"w_{k}"] for k in W}
        out = nc.dram_tensor("out", (P, KC, T), F32, kind="ExternalOutput").ap()
        program(nc, dr, out, plan)
    r = run_bass_kernel_spmd(nc, [arrays], core_ids=[0])
    y = r.results[0]["out"]
    return np.ascontiguousarray(y.transpose(2, 1, 0)).reshape(1, T, D)
```
